# Optimizing a Trainium2 kernel written in Bass

```python
import jax, jax.numpy as jnp
from jax import lax
import numpy as np
import math

D_MODEL = 1024
BATCH = 1
SEQ = 512
DEPTH = 1

CTX_LEN = 256
GRID_W = 64
D_MIX = D_MODEL
HEAD_DIM = 64
ATT_HEADS = 8
ATT_KV_HEADS = 2
GQA_GROUP = ATT_HEADS // ATT_KV_HEADS
D_ATT = ATT_HEADS * HEAD_DIM
D_ATT_KV = ATT_KV_HEADS * HEAD_DIM
ATT_SCALE = HEAD_DIM ** -0.5
ROPE_THETA = 10000.0
ROPE_PAIRS = HEAD_DIM // 4
Q_BLOCK = 128
RWKV_HEADS = 8
RWKV_HEAD = 64
D_RWKV = RWKV_HEADS * RWKV_HEAD
D_DECAY_LORA = 64
D_AAA_LORA = 64
D_GATE_LORA = 128
D_RWKV_IN = 3 * D_RWKV + D_DECAY_LORA + D_AAA_LORA + D_GATE_LORA
D_IN = D_ATT + 2 * D_ATT_KV + D_RWKV_IN
ATT_CUTS = (D_ATT, D_ATT + D_ATT_KV, D_ATT + 2 * D_ATT_KV)
RWKV_CUTS = (D_RWKV, 2 * D_RWKV, 3 * D_RWKV, 3 * D_RWKV + D_DECAY_LORA,
             3 * D_RWKV + D_DECAY_LORA + D_AAA_LORA)
N_EXPERTS = 16
CAPACITY_FACTOR = 2
D_EXPERT = D_MODEL
N_MOD = 6
LN_EPS = 1e-5
RMS_EPS = 1e-6
GN_EPS = 64e-5
L2_EPS = 1e-12
ALPHA = (2.0 * DEPTH) ** 0.25
BETA = (8.0 * DEPTH) ** -0.25


def layer_norm(x):
    xf = x.astype(jnp.float32)
    mu = jnp.mean(xf, -1, keepdims=True)
    var = jnp.mean(jnp.square(xf - mu), -1, keepdims=True)
    return ((xf - mu) * lax.rsqrt(var + LN_EPS)).astype(x.dtype)

def layer_norm_affine(x, g, b):
    return layer_norm(x) * g + b

def modulate(h, shift, scale):
    return h * (1.0 + scale) + shift

def to_heads(t, n):
    return t.reshape(t.shape[:-1] + (n, t.shape[-1] // n))

def head_rms_norm(t, gain):
    tf = t.astype(jnp.float32)
    return (tf * lax.rsqrt(jnp.mean(tf * tf, -1, keepdims=True) + RMS_EPS) * gain).astype(t.dtype)

def axial_rope_tables(n_tokens):
    rows = n_tokens // GRID_W
    row = jnp.repeat(jnp.arange(rows), GRID_W)
    col = jnp.tile(jnp.arange(GRID_W), rows)
    inv = ROPE_THETA ** (-jnp.arange(ROPE_PAIRS, dtype=jnp.float32) / ROPE_PAIRS)
    ang = jnp.stack([row, col], -1).astype(jnp.float32)[:, :, None] * inv
    return jnp.cos(ang), jnp.sin(ang)

def apply_axial_rope(t, cos, sin):
    B, L, H, _ = t.shape
    tf = t.astype(jnp.float32).reshape(B, L, H, 2, 2, ROPE_PAIRS)
    t1, t2 = tf[..., 0, :], tf[..., 1, :]
    cs, sn = cos[None, :, None], sin[None, :, None]
    out = jnp.stack([t1 * cs - t2 * sn, t2 * cs + t1 * sn], axis=-2)
    return out.reshape(B, L, H, HEAD_DIM).astype(t.dtype)

def gqa_attend(q, k, v):
    B, Tq = q.shape[:2]
    qg = q.reshape(B, Tq, ATT_KV_HEADS, GQA_GROUP, HEAD_DIM)
    s = jnp.einsum('bqkgd,bskd->bkgqs', qg, k).astype(jnp.float32) * ATT_SCALE
    p = jax.nn.softmax(s, axis=-1).astype(v.dtype)
    o = jnp.einsum('bkgqs,bskd->bqkgd', p, v)
    return o.reshape(B, Tq, D_ATT)

def token_shift(p, mu):
    pad = jnp.pad(p, ((0, 0), (1, 1), (0, 0)))
    return p + (0.5 * (pad[:, :-2] + pad[:, 2:]) - p) * mu

def rwkv_inputs(rw, decay_w0, decay_up, iclr_a0, iclr_up, gate_up, k_k, k_a):
    f32 = jnp.float32
    r, k, v, wl, al, gl = jnp.split(rw, RWKV_CUTS, axis=-1)
    g = jax.nn.sigmoid(gl) @ gate_up
    kk = to_heads(k * k_k, RWKV_HEADS).astype(f32)
    kk = kk / jnp.maximum(jnp.sqrt(jnp.sum(kk * kk, -1, keepdims=True)), L2_EPS)
    wt = jnp.tanh(wl)
    dirs = []
    for d in range(2):
        w = -jax.nn.softplus(-(decay_w0[d] + wt @ decay_up[d])) - 0.5
        decay = jnp.exp(-jnp.exp(to_heads(w, RWKV_HEADS).astype(f32)))
        a = jax.nn.sigmoid(iclr_a0[d] + al @ iclr_up[d])
        kd = to_heads(k * (1.0 + (a - 1.0) * k_a), RWKV_HEADS).astype(f32)
        a_h = to_heads(a, RWKV_HEADS).astype(f32)
        dirs.append((decay, kd, -kk, kk * a_h))
    r_h = to_heads(r, RWKV_HEADS).astype(f32)
    k_h = to_heads(k, RWKV_HEADS).astype(f32)
    v_h = to_heads(v, RWKV_HEADS).astype(f32)
    return r_h, k_h, v_h, g, dirs

def wkv7_scan(r, decay, k, v, a, b, s0, reverse, return_y):
    xs = tuple(jnp.moveaxis(t, 1, 0) for t in (r, decay, k, v, a, b))

    def step(s, inp):
        rt, wt, kt, vt, at, bt = inp
        sa = jnp.einsum('bhvk,bhk->bhv', s, at)
        s = s * wt[:, :, None, :] + sa[..., None] * bt[:, :, None, :] + vt[..., None] * kt[:, :, None, :]
        y = jnp.einsum('bhvk,bhk->bhv', s, rt) if return_y else None
        return s, y

    s_fin, ys = lax.scan(step, s0, xs, reverse=reverse)
    return s_fin, (jnp.moveaxis(ys, 0, 1) if return_y else None)

def rwkv_output(y, r, k, v, g, r_k, lnx_g, lnx_b):
    B, T = y.shape[:2]
    mu = jnp.mean(y, -1, keepdims=True)
    var = jnp.mean(jnp.square(y - mu), -1, keepdims=True)
    yn = ((y - mu) * lax.rsqrt(var + GN_EPS)).reshape(B, T, D_RWKV) * lnx_g + lnx_b
    bonus = (jnp.sum(r * k * r_k, -1, keepdims=True) * v).reshape(B, T, D_RWKV)
    return (yn + bonus) * g

def token_mixer(h_lat, h_ctx, w_in, q_gain, k_gain, tshift_mu, decay_w0, decay_up, iclr_a0, iclr_up,
                gate_up, k_k, k_a, r_k, lnx_g, lnx_b, w_out, with_ctx_out):
    B, L, _ = h_lat.shape
    q_l, k_l, v_l, rw_l = jnp.split(h_lat @ w_in, ATT_CUTS, axis=-1)
    q_c, k_c, v_c, rw_c = jnp.split(h_ctx @ w_in, ATT_CUTS, axis=-1)

    cos, sin = axial_rope_tables(L)
    q_l = apply_axial_rope(head_rms_norm(to_heads(q_l, ATT_HEADS), q_gain), cos, sin)
    k_l = apply_axial_rope(head_rms_norm(to_heads(k_l, ATT_KV_HEADS), k_gain), cos, sin)
    k_c = head_rms_norm(to_heads(k_c, ATT_KV_HEADS), k_gain)
    v_l = to_heads(v_l, ATT_KV_HEADS)
    v_c = to_heads(v_c, ATT_KV_HEADS)
    k_all = jnp.concatenate([k_l, k_c], axis=1)
    v_all = jnp.concatenate([v_l, v_c], axis=1)
    n_blk = L // Q_BLOCK
    q_blocks = jnp.moveaxis(q_l.reshape(B, n_blk, Q_BLOCK, ATT_HEADS, HEAD_DIM), 1, 0)
    att_l = lax.map(lambda qb: gqa_attend(qb, k_all, v_all), q_blocks)
    att_l = jnp.moveaxis(att_l, 0, 1).reshape(B, L, D_ATT)

    rwkv_p = (decay_w0, decay_up, iclr_a0, iclr_up, gate_up, k_k, k_a)
    r_c, kb_c, vr_c, g_c, dirs_c = rwkv_inputs(token_shift(rw_c, tshift_mu), *rwkv_p)
    r_l, kb_l, vr_l, g_l, dirs_l = rwkv_inputs(token_shift(rw_l, tshift_mu), *rwkv_p)
    s0 = jnp.zeros((h_ctx.shape[0], RWKV_HEADS, RWKV_HEAD, RWKV_HEAD), jnp.float32)
    y_l, y_c = None, None
    for d, reverse in enumerate((False, True)):
        dc, kc, ac, bc = dirs_c[d]
        s_c, yc = wkv7_scan(r_c, dc, kc, vr_c, ac, bc, s0, reverse, with_ctx_out)
        dl, kl, al, bl = dirs_l[d]
        _, yl = wkv7_scan(r_l, dl, kl, vr_l, al, bl, s_c, reverse, True)
        y_l = yl if y_l is None else y_l + yl
        if with_ctx_out:
            y_c = yc if y_c is None else y_c + yc
    rw_out_l = rwkv_output(y_l, r_l, kb_l, vr_l, g_l, r_k, lnx_g, lnx_b).astype(h_lat.dtype)
    out_l = jnp.concatenate([att_l, rw_out_l], axis=-1) @ w_out
    if not with_ctx_out:
        return out_l, None
    q_c = head_rms_norm(to_heads(q_c, ATT_HEADS), q_gain)
    att_c = gqa_attend(q_c, k_c, v_c)
    rw_out_c = rwkv_output(y_c, r_c, kb_c, vr_c, g_c, r_k, lnx_g, lnx_b).astype(h_ctx.dtype)
    out_c = jnp.concatenate([att_c, rw_out_c], axis=-1) @ w_out
    return out_l, out_c

def expert_choice_ffn(h, router_w, w_gate, w_up, w_down):
    B, T, D = h.shape
    cap = CAPACITY_FACTOR * T // N_EXPERTS
    logits = jnp.einsum('btd,de->bte', h, router_w).astype(jnp.float32)
    aff = jax.nn.softmax(logits, axis=-1)
    gate, idx = lax.top_k(jnp.swapaxes(aff, 1, 2), cap)
    xin = jax.vmap(lambda hb, ib: hb[ib])(h, idx)
    hid = jax.nn.silu(jnp.einsum('becd,edf->becf', xin, w_gate)) * jnp.einsum('becd,edf->becf', xin, w_up)
    y = jnp.einsum('becf,efd->becd', hid, w_down) * gate[..., None].astype(h.dtype)
    return jax.vmap(lambda ib, yb: jnp.zeros((T, D), h.dtype).at[ib.reshape(-1)].add(yb.reshape(-1, D)))(idx, y)

def first_inputs(seed: int = 0) -> dict:
    key = jax.random.key(seed)
    ks = jax.random.split(key, 32)
    f32 = jnp.float32
    nl = DEPTH

    def nrm(k, shape, s):
        return jax.random.normal(k, shape, f32) * s

    return {
        'x': nrm(ks[0], (BATCH, SEQ, D_MODEL), 1.0),
        'c': nrm(ks[1], (BATCH, D_MODEL), 1.0),
        'ctx': nrm(ks[2], (BATCH, CTX_LEN, D_MODEL), 1.0),
        'c_ctx': nrm(ks[3], (D_MODEL,), 1.0),
        'w_ada': nrm(ks[4], (nl, D_MODEL, N_MOD * D_MODEL), 0.02),
        'b_ada': nrm(ks[5], (nl, N_MOD * D_MODEL), 0.02),
        'w_in': nrm(ks[6], (nl, D_MODEL, D_IN), D_MODEL ** -0.5),
        'q_gain': 1.0 + nrm(ks[7], (nl, HEAD_DIM), 0.1),
        'k_gain': 1.0 + nrm(ks[8], (nl, HEAD_DIM), 0.1),
        'tshift_mu': jax.random.uniform(ks[9], (nl, D_RWKV_IN), f32),
        'decay_w0': jax.random.uniform(ks[10], (nl, 2, D_RWKV), f32, -6.0, -1.0),
        'decay_up': nrm(ks[11], (nl, 2, D_DECAY_LORA, D_RWKV), 0.1 * D_DECAY_LORA ** -0.5),
        'iclr_a0': nrm(ks[12], (nl, 2, D_RWKV), 0.5),
        'iclr_up': nrm(ks[13], (nl, 2, D_AAA_LORA, D_RWKV), D_AAA_LORA ** -0.5),
        'gate_up': nrm(ks[14], (nl, D_GATE_LORA, D_RWKV), D_GATE_LORA ** -0.5),
        'k_k': 0.85 + nrm(ks[15], (nl, D_RWKV), 0.1),
        'k_a': 1.0 + nrm(ks[16], (nl, D_RWKV), 0.1),
        'r_k': nrm(ks[17], (nl, RWKV_HEADS, RWKV_HEAD), 0.1),
        'lnx_g': 1.0 + nrm(ks[18], (nl, D_RWKV), 0.1),
        'lnx_b': nrm(ks[19], (nl, D_RWKV), 0.02),
        'w_out': nrm(ks[20], (nl, D_MIX, D_MODEL), BETA * D_MIX ** -0.5),
        'ln1_g': 1.0 + nrm(ks[21], (nl, D_MODEL), 0.1),
        'ln1_b': nrm(ks[22], (nl, D_MODEL), 0.02),
        'router_w': nrm(ks[23], (nl, D_MODEL, N_EXPERTS), D_MODEL ** -0.5),
        'exp_w_gate': nrm(ks[24], (nl, N_EXPERTS, D_MODEL, D_EXPERT), D_MODEL ** -0.5),
        'exp_w_up': nrm(ks[25], (nl, N_EXPERTS, D_MODEL, D_EXPERT), D_MODEL ** -0.5),
        'exp_w_down': nrm(ks[26], (nl, N_EXPERTS, D_EXPERT, D_MODEL), BETA * D_EXPERT ** -0.5),
        'ln2_g': 1.0 + nrm(ks[27], (nl, D_MODEL), 0.1),
        'ln2_b': nrm(ks[28], (nl, D_MODEL), 0.02),
    }

def first_block(x, c, ctx, c_ctx, w_ada, b_ada, w_in, q_gain, k_gain, tshift_mu, decay_w0, decay_up,
              iclr_a0, iclr_up, gate_up, k_k, k_a, r_k, lnx_g, lnx_b, w_out, ln1_g, ln1_b,
              router_w, exp_w_gate, exp_w_up, exp_w_down, ln2_g, ln2_b):
    for li in range(DEPTH):
        last = li == DEPTH - 1
        mod = jax.nn.silu(c) @ w_ada[li] + b_ada[li]
        sh1, sc1, gt1, sh2, sc2, gt2 = jnp.split(mod[:, None, :], N_MOD, axis=-1)
        mc = jnp.split(jax.nn.silu(c_ctx) @ w_ada[li] + b_ada[li], N_MOD, axis=-1)
        h_lat = modulate(layer_norm(x), sh1, sc1)
        h_ctx = modulate(layer_norm(ctx), mc[0], mc[1])
        mix_l, mix_c = token_mixer(h_lat, h_ctx, w_in[li], q_gain[li], k_gain[li], tshift_mu[li],
                                   decay_w0[li], decay_up[li], iclr_a0[li], iclr_up[li], gate_up[li],
                                   k_k[li], k_a[li], r_k[li], lnx_g[li], lnx_b[li], w_out[li],
                                   not last)
        x = layer_norm_affine(ALPHA * x + gt1 * mix_l, ln1_g[li], ln1_b[li])
        h2 = modulate(layer_norm(x), sh2, sc2)
        ffn_l = expert_choice_ffn(h2, router_w[li], exp_w_gate[li], exp_w_up[li], exp_w_down[li])
        x = layer_norm_affine(ALPHA * x + gt2 * ffn_l, ln2_g[li], ln2_b[li])
        if not last:
            ctx = layer_norm_affine(ALPHA * ctx + mc[2] * mix_c, ln1_g[li], ln1_b[li])
            h2c = modulate(layer_norm(ctx), mc[3], mc[4])
            ffn_c = expert_choice_ffn(h2c, router_w[li], exp_w_gate[li], exp_w_up[li], exp_w_down[li])
            ctx = layer_norm_affine(ALPHA * ctx + mc[5] * ffn_c, ln2_g[li], ln2_b[li])
    return x


DEPTH_2 = 2

N_MIX_HEADS = 16
HEAD_DIM_2 = D_MODEL // N_MIX_HEADS
N_HEADS_DIL = 6
DILATED_PAIRS = ((128, 1), (512, 4), (2048, 16))
N_HEADS_DIFF = 4
DIFF_QK_DIM = HEAD_DIM_2 // 2
N_HEADS_SB = 6
D_MIX_2 = (N_HEADS_DIL + N_HEADS_DIFF + N_HEADS_SB) * HEAD_DIM_2
IN_SIZES = (N_HEADS_DIL * HEAD_DIM_2,) * 3 + (N_HEADS_DIFF * 2 * DIFF_QK_DIM,) * 2 + (N_HEADS_DIFF * HEAD_DIM_2,) + (N_HEADS_SB * HEAD_DIM_2,) * 3
D_IN_2 = sum(IN_SIZES)
D_FF = 2816
NORM_EPS = 1e-6
N_NORMS = 6


def rmsnorm(x, g):
    xf = x.astype(jnp.float32)
    y = xf * lax.rsqrt(jnp.mean(xf * xf, axis=-1, keepdims=True) + NORM_EPS)
    return (y * g.astype(jnp.float32)).astype(x.dtype)

def swiglu(h, w_gate, w_up, w_down):
    return (jax.nn.silu(h @ w_gate) * (h @ w_up)) @ w_down

def alibi_slopes(n):
    return 2.0 ** (-8.0 * jnp.arange(1, n + 1, dtype=jnp.float32) / n)

def to_heads_2(t, n_heads):
    b, s, _ = t.shape
    return t.reshape(b, s, n_heads, -1).transpose(0, 2, 1, 3)

def from_heads(t):
    b, h, s, dh = t.shape
    return t.transpose(0, 2, 1, 3).reshape(b, s, h * dh)

def query_blocks(t):
    b, h, s, dh = t.shape
    return t.reshape(b, h, s // Q_BLOCK, Q_BLOCK, dh).transpose(2, 0, 1, 3, 4)

def merge_blocks(t):
    nq, b, h, q, dh = t.shape
    return t.transpose(1, 2, 0, 3, 4).reshape(b, h, nq * q, dh)

def dilated_branch(q, k, v, slopes, window, dilation):
    b, h, s, dh = q.shape
    n_back = window // dilation
    chunk = dilation * n_back
    sp = -(-s // chunk) * chunk
    seg = sp // dilation
    nb = seg // n_back

    def split(t):
        t = jnp.pad(t, ((0, 0), (0, 0), (0, sp - s), (0, 0)))
        t = t.reshape(b, h, seg, dilation, dh).transpose(0, 1, 3, 2, 4)
        return t.reshape(b, h, dilation, nb, n_back, dh)

    def with_prev(t):
        prev = jnp.concatenate([jnp.zeros_like(t[:, :, :, :1]), t[:, :, :, :-1]], axis=3)
        return jnp.concatenate([prev, t], axis=4)

    qb = split(q)
    kk = with_prev(split(k))
    vv = with_prev(split(v))
    sc = jnp.einsum('bhrnqd,bhrnkd->bhrnqk', qb, kk, preferred_element_type=jnp.float32)
    qi = jnp.arange(n_back)[:, None]
    ki = jnp.arange(2 * n_back)[None, :]
    dist = n_back + qi - ki
    band = (dist >= 0) & (dist <= n_back)
    first = (jnp.arange(nb) == 0)[:, None, None] & (ki < n_back)[None]
    valid = band[None] & ~first
    sc = sc - slopes[None, :, None, None, None, None] * (dilation * dist).astype(jnp.float32)
    sc = jnp.where(valid, sc, -jnp.inf)
    m = jnp.max(sc, axis=-1, keepdims=True)
    p = jnp.exp(sc - m)
    den = jnp.sum(p, axis=-1)
    o = jnp.einsum('bhrnqk,bhrnkd->bhrnqd', p, vv, preferred_element_type=jnp.float32) / den[..., None]
    lse = m[..., 0] + jnp.log(den)
    o = o.reshape(b, h, dilation, seg, dh).transpose(0, 1, 3, 2, 4).reshape(b, h, sp, dh)[:, :, :s]
    lse = lse.reshape(b, h, dilation, seg).transpose(0, 1, 3, 2).reshape(b, h, sp)[:, :, :s]
    return o, lse

def dilated_attention(q, k, v):
    slopes = alibi_slopes(q.shape[1])
    outs, lses = zip(*[dilated_branch(q, k, v, slopes, w, d) for (w, d) in DILATED_PAIRS])
    wts = jax.nn.softmax(jnp.stack(lses), axis=0)
    return jnp.sum(wts[..., None] * jnp.stack(outs), axis=0)

def differential_attention(q1, q2, k1, k2, v, lam):
    s = q1.shape[2]
    slopes = alibi_slopes(q1.shape[1])
    kpos = jnp.arange(s)
    starts = jnp.arange(s // Q_BLOCK) * Q_BLOCK

    def block(args):
        start, a, c = args
        rel = (start + jnp.arange(Q_BLOCK))[:, None] - kpos[None, :]
        bias = jnp.where(rel >= 0, -slopes[:, None, None] * rel.astype(jnp.float32), -jnp.inf)
        a1 = jax.nn.softmax(jnp.einsum('bhqd,bhkd->bhqk', a, k1, preferred_element_type=jnp.float32) + bias, axis=-1)
        a2 = jax.nn.softmax(jnp.einsum('bhqd,bhkd->bhqk', c, k2, preferred_element_type=jnp.float32) + bias, axis=-1)
        return jnp.einsum('bhqk,bhkd->bhqd', a1 - lam * a2, v, preferred_element_type=jnp.float32)

    return merge_blocks(lax.map(block, (starts, query_blocks(q1), query_blocks(q2))))

def stick_breaking_attention(q, k, v):
    s = q.shape[2]
    kpos = jnp.arange(s)
    starts = jnp.arange(s // Q_BLOCK) * Q_BLOCK

    def block(args):
        start, a = args
        valid = kpos[None, :] < (start + jnp.arange(Q_BLOCK))[:, None]
        z = jnp.einsum('bhqd,bhkd->bhqk', a, k, preferred_element_type=jnp.float32)
        log_fail = jnp.where(valid, jax.nn.log_sigmoid(-z), 0.0)
        after = lax.cumsum(log_fail, axis=3, reverse=True) - log_fail
        wts = jnp.where(valid, jnp.exp(jax.nn.log_sigmoid(z) + after), 0.0)
        return jnp.einsum('bhqk,bhkd->bhqd', wts, v, preferred_element_type=jnp.float32)

    return merge_blocks(lax.map(block, (starts, query_blocks(q))))

def token_mixer_2(h, w_in, w_out, lam_params, subln_gain, layer):
    proj = h @ w_in
    idx = [int(i) for i in np.cumsum(IN_SIZES)[:-1]]
    qa, ka, va, qb, kb, vb, qc, kc, vc = jnp.split(proj, idx, axis=-1)
    b, s, _ = h.shape
    o_a = dilated_attention(to_heads_2(qa, N_HEADS_DIL) * (HEAD_DIM_2 ** -0.5), to_heads_2(ka, N_HEADS_DIL), to_heads_2(va, N_HEADS_DIL))
    qb = qb.reshape(b, s, N_HEADS_DIFF, 2, DIFF_QK_DIM).transpose(0, 2, 3, 1, 4) * (DIFF_QK_DIM ** -0.5)
    kb = kb.reshape(b, s, N_HEADS_DIFF, 2, DIFF_QK_DIM).transpose(0, 2, 3, 1, 4)
    lam_init = 0.8 - 0.6 * math.exp(-0.3 * layer)
    lam = jnp.exp(jnp.sum(lam_params[0] * lam_params[1])) - jnp.exp(jnp.sum(lam_params[2] * lam_params[3])) + lam_init
    o_b = differential_attention(qb[:, :, 0], qb[:, :, 1], kb[:, :, 0], kb[:, :, 1], to_heads_2(vb, N_HEADS_DIFF), lam.astype(jnp.float32))
    o_b = rmsnorm(o_b, subln_gain) * (1.0 - lam_init)
    o_c = stick_breaking_attention(to_heads_2(qc, N_HEADS_SB) * (HEAD_DIM_2 ** -0.5), to_heads_2(kc, N_HEADS_SB), to_heads_2(vc, N_HEADS_SB))
    mixed = jnp.concatenate([from_heads(o_a), from_heads(o_b), from_heads(o_c)], axis=-1).astype(h.dtype)
    return mixed @ w_out

def second_inputs(seed: int = 0) -> dict:
    key = jax.random.key(seed)
    ks = jax.random.split(key, 10)
    f32 = jnp.float32
    x = jax.random.normal(ks[0], (BATCH, SEQ, D_MODEL), f32)
    norm_gains = 1.0 + 0.02 * jax.random.normal(ks[1], (DEPTH_2, N_NORMS, D_MODEL), f32)
    w_ffn_gate = jax.random.normal(ks[2], (DEPTH_2, 2, D_MODEL, D_FF), f32) * D_MODEL ** -0.5
    w_ffn_up = jax.random.normal(ks[3], (DEPTH_2, 2, D_MODEL, D_FF), f32) * D_MODEL ** -0.5
    w_ffn_down = jax.random.normal(ks[4], (DEPTH_2, 2, D_FF, D_MODEL), f32) * D_FF ** -0.5
    w_in = jax.random.normal(ks[5], (DEPTH_2, D_MODEL, D_IN_2), f32) * D_MODEL ** -0.5
    w_out = jax.random.normal(ks[6], (DEPTH_2, D_MIX_2, D_MODEL), f32) * D_MIX_2 ** -0.5
    diff_lambda = 0.1 * jax.random.normal(ks[7], (DEPTH_2, 4, DIFF_QK_DIM), f32)
    diff_subln_gain = 1.0 + 0.02 * jax.random.normal(ks[8], (DEPTH_2, HEAD_DIM_2), f32)
    return {"x": x, "norm_gains": norm_gains, "w_ffn_gate": w_ffn_gate, "w_ffn_up": w_ffn_up,
            "w_ffn_down": w_ffn_down, "w_in": w_in, "w_out": w_out,
            "diff_lambda": diff_lambda, "diff_subln_gain": diff_subln_gain}

def second_block(x, norm_gains, w_ffn_gate, w_ffn_up, w_ffn_down, w_in, w_out, diff_lambda, diff_subln_gain):
    for layer in range(DEPTH_2):
        g = norm_gains[layer]
        h = rmsnorm(x, g[0])
        x = x + 0.5 * rmsnorm(swiglu(h, w_ffn_gate[layer, 0], w_ffn_up[layer, 0], w_ffn_down[layer, 0]), g[1])
        h = rmsnorm(x, g[2])
        x = x + rmsnorm(token_mixer_2(h, w_in[layer], w_out[layer], diff_lambda[layer], diff_subln_gain[layer], layer), g[3])
        h = rmsnorm(x, g[4])
        x = x + 0.5 * rmsnorm(swiglu(h, w_ffn_gate[layer, 1], w_ffn_up[layer, 1], w_ffn_down[layer, 1]), g[5])
    return x


def setup_inputs(seed=0):
    out = dict(first_inputs(seed))
    for name, value in second_inputs(seed + 1).items():
        if name != "x":
            out[name + "_2"] = value
    return out


def reference(
    x, c, ctx, c_ctx, w_ada, b_ada, w_in, q_gain, k_gain, tshift_mu, decay_w0, decay_up,
    iclr_a0, iclr_up, gate_up, k_k, k_a, r_k, lnx_g, lnx_b, w_out, ln1_g, ln1_b, router_w,
    exp_w_gate, exp_w_up, exp_w_down, ln2_g, ln2_b, norm_gains_2, w_ffn_gate_2, w_ffn_up_2,
    w_ffn_down_2, w_in_2, w_out_2, diff_lambda_2, diff_subln_gain_2,
):
    x = first_block(
        x, c, ctx, c_ctx, w_ada, b_ada, w_in, q_gain, k_gain, tshift_mu, decay_w0, decay_up,
        iclr_a0, iclr_up, gate_up, k_k, k_a, r_k, lnx_g, lnx_b, w_out, ln1_g, ln1_b, router_w,
        exp_w_gate, exp_w_up, exp_w_down, ln2_g, ln2_b,
    )
    return second_block(
        x, norm_gains_2, w_ffn_gate_2, w_ffn_up_2, w_ffn_down_2, w_in_2, w_out_2, diff_lambda_2,
        diff_subln_gain_2,
    )


_drawn_inputs = setup_inputs


def setup_inputs(seed=0):
    import zlib

    import numpy as np

    out = dict(_drawn_inputs(seed))
    spreads = {}
    factors = {'q_gain': 8.0,
     'k_gain': 8.0,
     'decay_up': 8.0,
     'lnx_g': 4.031,
     'lnx_b': 8.0,
     'diff_subln_gain_2': 4.851}
    for name, (base, spread) in spreads.items():
        noise = np.random.default_rng([zlib.crc32(name.encode()), seed]).standard_normal(out[name].shape)
        drawn = base * np.exp(spread * noise) if base else spread * noise
        out[name] = __import__('jax').numpy.asarray(drawn.astype(out[name].dtype))
    for name, factor in factors.items():
        out[name] = (out[name] * factor).astype(out[name].dtype)
    return out
```

```python
from contextlib import ExitStack
import math

import numpy as np
import concourse.bass as bass
from concourse import mybir

F32 = mybir.dt.float32
ALU = mybir.AluOpType
ACT = mybir.ActivationFunctionType
AX = mybir.AxisListType

P = 128
D = 1024
KD = D // P
T, TC = 512, 256
NT, NTC = T // P, TC // P
NTA = NT + NTC
NALL = T + TC
HD = 64
NH, NKV = 8, 2
NE, CAP = 16, 64
NRW = 14
FF = 2816
NF = FF // P
ALPHA = 2.0 ** 0.25
LN_EPS, RMS_EPS, GN_EPS, NORM_EPS, L2_EPS = 1e-5, 1e-6, 64e-5, 1e-6, 1e-12
DECAY_K = math.exp(-0.5)
SLOT = 4096
RING = 4
NEG = -1.0e30


def constants():
    t = np.arange(P)
    ident = np.eye(P, dtype=np.float32)
    cum = np.zeros((2, P, 258), np.float32)
    s = t[:, None]
    q = t[None, :]
    mid = 63
    first = (s <= mid) * 1.0
    cum[0, :, 0:128] = (s <= q) * 1.0 - first
    cum[0, :, 128:256] = (s < q) * 1.0 - first
    cum[0, :, 256] = first[:, 0]
    cum[0, :, 257] = 1.0 - first[:, 0]
    last = (s >= P - 1 - mid) * 1.0
    cum[1, :, 0:128] = (s >= q) * 1.0 - last
    cum[1, :, 128:256] = (s > q) * 1.0 - last
    cum[1, :, 256] = last[:, 0]
    cum[1, :, 257] = 1.0 - last[:, 0]
    strict = np.stack([(s < q), (s > q)]).astype(np.float32)
    incl = np.stack([(s <= q), (s >= q)]).astype(np.float32)
    gram = np.concatenate([strict, incl, strict, incl], -1)
    lev = np.zeros((2, P, 7, P), np.float32)
    for i in range(7):
        n = 1 << i
        same = (s // (2 * n)) == (q // (2 * n))
        lev[0, :, i] = same & (s // n < q // n)
        lev[1, :, i] = same & (s // n > q // n)
    ones2 = np.kron(np.eye(2), np.ones((64, 64))).astype(np.float32)
    hsel = np.kron(np.eye(2), np.ones((64, 1))).astype(np.float32)
    pos = np.arange(T)
    inv = (np.float32(10000.0) ** (-np.arange(16, dtype=np.float32) / np.float32(16))).astype(np.float32)
    ang = np.stack([pos // 64, pos % 64], -1).astype(np.float32)[:, :, None] * inv
    rope = np.stack([np.cos(ang), np.sin(ang)], 1).reshape(NT, P, 64).transpose(1, 0, 2).astype(np.float32)
    before = np.zeros((P, NT, T), np.float32)
    for i in range(NT):
        before[:, i] = (np.arange(T)[None, :] < (i * P + t)[:, None])
    slots = np.tile(np.arange(CAP, dtype=np.float32), (P, 1))
    x = np.arange(896)[None, :] - 384
    rel = t[:, None] - x
    mult = np.zeros(rel.shape)
    for w, dil in ((128, 1), (512, 4), (2048, 16)):
        mult += (rel >= 0) & (rel <= w) & (rel % dil == 0)
    lnm = np.where(mult > 0, np.log(np.maximum(mult, 1)), NEG)
    sl = lambda n: 2.0 ** (-8.0 * np.arange(1, n + 1) / n)
    dil = np.stack([np.where(mult > 0, -a * rel + lnm, NEG) for a in sl(6)]).astype(np.float32)
    dif = np.stack([np.where(rel >= 0, -a * rel, NEG) for a in sl(4)]).astype(np.float32)
    bias = np.concatenate([dil, dif])
    sufneg = -(s >= q).astype(np.float32)
    sb = np.stack([sufneg, -np.ones((P, P), np.float32), (s < q).astype(np.float32)], 1)
    return {"k_ident": ident, "k_cum": cum, "k_gram": gram, "k_lev": lev, "k_ones2": ones2,
            "k_hsel": hsel, "k_rope": rope, "k_before": before, "k_slots": slots,
            "k_bias": np.ascontiguousarray(bias), "k_sb": np.ascontiguousarray(sb)}


class Marks:

    def __init__(self, known, final):
        self.known, self.now, self.final, self.sems = known, {}, final, {}

    def past(self, *key):
        lane, n = self.known.get(key, ("pe", 0))
        assert not self.final or key in self.known, key
        return self.sems[lane], n


class Lane:

    def __init__(self, name, engine, sem, marks):
        self.name, self.engine, self.sem, self.marks = name, engine, sem, marks
        self.wait_ge = engine.wait_ge
        self.n = 0

    def did(self, ins, *key):
        self.n += 1
        if key:
            self.marks.now[key] = (self.name, self.n)

    def name_last(self, *key):
        self.marks.now[key] = (self.name, self.n)

    def own(self):
        return self.sem, self.n


def build(nc, a, out, known, final, upto, debug):
    ctx = ExitStack()
    marks = Marks(known, final)
    with ctx:
        def sem(name):
            return ctx.enter_context(nc.semaphore(name))

        ARENA = 52992
        arena = ctx.enter_context(nc.sbuf_tensor("arena", [P, ARENA], F32))
        banks = ctx.enter_context(nc.psum_tensor("banks", [P, 8, 512], F32))
        used = [0]

        def region(off, *shape):
            n = int(np.prod(shape))
            assert off + n <= ARENA, (off, shape)
            ap = arena[:, off:off + n]
            if len(shape) > 1:
                names = " ".join("abcde"[:len(shape)])
                ap = ap.rearrange(f"p ({names}) -> p {names}", **{k: v for k, v in zip("abcde", shape)})
            return ap

        class Stack:
            def __init__(self, at, end=ARENA):
                self.at, self.end = at, end

            def take(self, *shape):
                r = region(self.at, *shape)
                self.at += int(np.prod(shape))
                assert self.at <= self.end, ("arena", self.at, self.end)
                return r

            def branch(self):
                return Stack(self.at, self.end)

        lanes = {}
        for name, eng in (("pe", nc.tensor), ("act", nc.scalar), ("dve", nc.vector), ("pool", nc.gpsimd),
                          ("sp", nc.sync)):
            s = sem(f"{name}_results")
            marks.sems[name] = s
            lanes[name] = Lane(name, eng, s, marks)
        pe, act, dve, pool = (lanes[n] for n in ("pe", "act", "dve", "pool"))
        ring_full = [sem(f"ring_full{i}") for i in range(RING)]
        small_in = [sem(f"small_in{i}") for i in range(40)]
        stored = sem("stored")
        scratch_io = sem("scratch_io")
        past = marks.past
        V, S, TE, G = nc.vector, nc.scalar, nc.tensor, nc.gpsimd
        views = {"final_x": None}

        def program(l_):
            me = l_
            n_loads, smalls, stages = [0], {}, []
            slot_fills = [0] * RING
            keep = Stack(RING * SLOT)

            def stream_many(parts):
                n = n_loads[0]
                n_loads[0] += 1
                at, views_ = (n % RING) * SLOT, []
                if me.name == "sp" and n >= RING:
                    me.wait_ge(*past("freed", n - RING))
                for shape, src in parts:
                    views_.append(region(at, *shape))
                    at += int(np.prod(shape))
                    if me.name == "sp":
                        me.engine.dma_start(views_[-1], src).then_inc(ring_full[n % RING], 16)
                slot_fills[n % RING] += 16 * len(parts)
                return (n, slot_fills[n % RING]), views_

            def stream(src, shape):
                n, v = stream_many([(shape, src)])
                return n, v[0]

            def hold_stream(after):
                if me.name == "sp":
                    for e in ("pe", "act", "dve", "pool"):
                        me.wait_ge(*past("end", after, e))

            def small(key, pairs, after=None):
                smalls[key] = (small_in[len(smalls)], 16 * len(pairs))
                if me.name == "sp":
                    if after:
                        for e in ("pe", "act", "dve", "pool"):
                            me.wait_ge(*past("end", after, e))
                    for dst, src in pairs:
                        me.engine.dma_start(dst, src).then_inc(smalls[key][0], 16)

            def stage(name, **fns):
                if me.name == "sp":
                    stages.append(name)
                    return
                fn = fns.get(me.name)
                if fn is not None:
                    if stages:
                        for other in ("pe", "act", "dve", "pool"):
                            me.wait_ge(*past("end", stages[-1], other))
                    fn(me)
                me.name_last("end", name, me.name)
                stages.append(name)

            def products(name, groups, act_extra=None, dve_extra=None, pool_fn=None):
                def f_pe(l):
                    for i, g in enumerate(groups):
                        if i >= 8:
                            l.wait_ge(*past(name, "read", i - 8))
                        for n in g.get("loads", ()):
                            l.wait_ge(ring_full[n[0] % RING], n[1])
                        for k in g.get("have", ()):
                            l.wait_ge(*smalls[k])
                        for key in g.get("after", ()):
                            l.wait_ge(*past(*key))
                        bank = banks[:, i % 8, :]
                        ms = g["mms"]
                        for j, m in enumerate(ms):
                            if m[0] == "t":
                                ins = TE.transpose(m[1](bank), m[2], m[3])
                            else:
                                ins = TE.matmul(m[1](bank), m[2], m[3], start=m[4], stop=m[5])
                        l.did(ins.then_inc(l.sem, 1), name, "made", i)
                        if "name" in g:
                            l.name_last(*g["name"])
                        for n in g.get("loads", ()):
                            l.name_last("freed", n[0])
    
                def reader(who):
                    def f(l):
                        for i, g in enumerate(groups):
                            if g.get("first", (None,))[0] == who:
                                l.wait_ge(*past(name, "made", i))
                                g["first"][1](l, banks[:, i % 8, :])
                            if g["by"] == who:
                                l.wait_ge(*past(name, "made", i))
                                g["read"](l, banks[:, i % 8, :])
                                l.name_last(name, "read", i)
                        extra = act_extra if who == "act" else dve_extra
                        if extra:
                            extra(l)
                    return f
                stage(name, pe=f_pe, act=reader("act"), dve=reader("dve"), pool=pool_fn)
    
            def copy_out(dst, view=lambda b: b):
                def read(l, bank):
                    if l is act:
                        l.did(S.activation(dst, view(bank), ACT.Copy).then_inc(l.sem, 1))
                    else:
                        l.did(V.tensor_copy(dst, view(bank)).then_inc(l.sem, 1))
                return read
    
            def acc(view, pairs):
                n = len(pairs)
                return [("m", view, x, y, i == 0, i == n - 1) for i, (x, y) in enumerate(pairs)]
    
            def halves(i):
                return "act" if i % 2 else "dve"

            ident = keep.take(P)
            ones = keep.take(P)
            mixT = keep.take(8, T)
            small("const", [(ident, a["k_ident"])])
            gt1 = keep.take(D)
            gt2 = keep.take(D)
            modcol = keep.take(48, 2)
            stats = keep.take(256)
            base = keep.branch()

            m = base.branch()
            c16, sil, sg16 = m.take(P), m.take(16), m.take(16)
            modrow, brow = m.take(6 * D), m.take(6 * D)
            small("mod", [(c16[0:8, :], a["c"].rearrange("o (k p) -> (o k) p", p=P)),
                          (c16[8:16, :], a["c_ctx"].rearrange("(k p) -> k p", p=P)),
                          (brow[0:1, :], a["b_ada"]), (brow[1:2, :], a["b_ada"])])

            def silu_c_read(l, bank):
                l.did(S.activation(sg16, bank[:, 0:16], ACT.Sigmoid).then_inc(l.sem, 1), "silu_c")

            def silu_c(l):
                l.wait_ge(*past("silu_c"))
                l.did(V.tensor_tensor(sil, banks[:, 0, 0:16], sg16, ALU.mult).then_inc(l.sem, 1))

            def fill_ones(l):
                l.did(G.memset(ones, 1.0).then_inc(l.sem, 1))
            products("c_T", [{"have": ("mod", "const"), "by": "act", "read": silu_c_read,
                              "mms": [("t", lambda b: b[:, 0:16], c16[0:16, :], ident[0:16, 0:16])]}],
                     dve_extra=silu_c, pool_fn=fill_ones)
            silv = sil.rearrange("p (v k) -> p k v", k=KD)
            w_ada = a["w_ada"][0].rearrange("(k p) n -> p k n", p=P)
            groups = []
            for n in range(12):
                ln, w = stream(w_ada[:, :, n * 512:(n + 1) * 512], (KD, 512))
                cs = slice(n * 512, (n + 1) * 512)

                def read(l, bank, cs=cs):
                    l.did(V.tensor_tensor(modrow[0:2, cs], bank[0:2, :], brow[0:2, cs], ALU.add).then_inc(l.sem, 1))
                groups.append({"loads": [ln], "by": "dve", "read": read,
                               "mms": acc(lambda b: b[0:2, :], [(silv[:, k, :], w[:, k, :]) for k in range(KD)])})
            products("mod_rows", groups)

            def modcol_read(l, bank):
                l.did(V.tensor_copy(modcol, bank[:, 0:96].rearrange("p (a b) -> p a b", b=2)).then_inc(l.sem, 1))
                l.wait_ge(*l.own())
                for j in (8, 32):
                    l.did(V.tensor_scalar(modcol[:, j:j + 8, :], modcol[:, j:j + 8, :], 1.0, None, ALU.add).then_inc(l.sem, 1))
            groups = [{"by": "dve", "read": modcol_read,
                       "mms": [("t", (lambda b, j=j: b[:, 2 * j:2 * j + 2]), modrow[0:2, j * P:(j + 1) * P],
                                ident[0:2, 0:2]) for j in range(48)]}]
            for dst, j in ((gt1, 2), (gt2, 5)):
                for hf in range(2):
                    groups.append({"by": "act", "read": copy_out(dst[:, hf * 512:(hf + 1) * 512]),
                                   "mms": acc(lambda b: b, [(ones[0:1, :], modrow[0:1, j * D + hf * 512:j * D + hf * 512 + 512])])})
            products("mod_cols", groups)

            def norm_stage(name, src, dst, tiles, need, affine=None, into=None):
                st = stats[:, 0:tiles * 12].rearrange("p (a b c) -> p a b c", b=2, c=6)
                mv = stats[:, 80:80 + 2 * tiles].rearrange("p (a b) -> p a b", b=2)
                sd = stats[:, 100:100 + tiles]
                rs = stats[:, 110:110 + tiles]

                def f_dve(l):
                    for k in need:
                        l.wait_ge(*smalls[k])
                    for i in range(tiles):
                        for hf in range(2):
                            l.did(V.bn_stats(st[:, i, hf, :], src(i)[:, hf * 512:(hf + 1) * 512]).then_inc(l.sem, 1))
                    l.wait_ge(*l.own())
                    for i in range(tiles):
                        l.did(V.bn_aggr(mv[:, i, :], st[:, i, :, :]).then_inc(l.sem, 1))
                    l.wait_ge(*l.own())
                    l.did(V.tensor_scalar(sd, mv[:, :, 1], LN_EPS, None, ALU.add).then_inc(l.sem, 1), name, "var")
                    l.wait_ge(*past(name, "sd"))
                    l.did(V.reciprocal(rs, rs).then_inc(l.sem, 1))
                    l.wait_ge(*l.own())
                    for i in range(tiles):
                        l.did(V.tensor_scalar(dst(i), src(i), mv[:, i, 0:1], rs[:, i:i + 1], ALU.subtract, ALU.mult).then_inc(l.sem, 1))
                    if affine:
                        g, b = affine
                        l.wait_ge(*l.own())
                        for i in range(tiles):
                            l.did(V.tensor_tensor(dst(i), dst(i), g, ALU.mult).then_inc(l.sem, 1), name, "gained", i)

                def f_act(l):
                    l.wait_ge(*past(name, "var"))
                    l.did(S.activation(rs, sd, ACT.Sqrt).then_inc(l.sem, 1), name, "sd")

                def f_pool(l):
                    if affine:
                        for i in range(tiles):
                            l.wait_ge(*past(name, "gained", i))
                            l.did(G.tensor_tensor(dst(i), dst(i), affine[1], ALU.add).then_inc(l.sem, 1))
                stage(name, dve=f_dve, act=f_act, pool=f_pool)

            def transpose_groups(src, dst_of, n_tiles, tile0, nk, col=None, width=P):
                gs = []
                for k in range(nk):
                    def read(l, bank, k=k):
                        v = bank[:, 0:n_tiles * P]
                        if col is None:
                            if l is act:
                                l.did(S.activation(dst_of(k), v, ACT.Copy).then_inc(l.sem, 1))
                            else:
                                l.did(V.tensor_copy(dst_of(k), v).then_inc(l.sem, 1))
                        else:
                            sc, sh = col(k)
                            if l is act:
                                l.did(S.activation(dst_of(k), v, ACT.Identity, bias=sh, scale=sc).then_inc(l.sem, 1))
                            else:
                                l.did(V.tensor_scalar(dst_of(k), v, sc, sh, ALU.mult, ALU.add).then_inc(l.sem, 1))
                    gs.append({"by": halves(k), "read": read, "mms": [
                        ("t", (lambda b, i=i: b[:, i * P:(i + 1) * P]), src(tile0 + i)[:, k * P:(k + 1) * P], ident)
                        for i in range(n_tiles)]})
                return gs

            m = base.branch()
            hT = m.take(KD, NALL)
            xc = m.take(NTA, D)
            xn = m.take(NTA, D)
            small("x", [(xc[:, 0:NT, :], a["x"][0].rearrange("(t p) n -> p t n", p=P)),
                        (xc[:, NT:NTA, :], a["ctx"][0].rearrange("(t p) n -> p t n", p=P))], after="mod_cols")
            norm_stage("norm1", lambda i: xc[:, i, :], lambda i: xn[:, i, :], NTA, ["x"])
            products("h_T",
                     transpose_groups(lambda i: xn[:, i, :], lambda k: hT[:, k, 0:T], NT, 0, KD,
                                      lambda k: (modcol[:, 8 + k, 0:1], modcol[:, k, 0:1])) +
                     transpose_groups(lambda i: xn[:, i, :], lambda k: hT[:, k, T:NALL], NTC, NT, KD,
                                      lambda k: (modcol[:, 8 + k, 1:2], modcol[:, k, 1:2])))

            m = base.branch()
            hT = m.take(KD, NALL)
            cols = m.take(64)
            sft = m.take(NRW, NALL)
            qkv = m.take(NT, 768)
            kvc = m.take(NTC, 256)
            after_proj = m.branch()
            pb = m.take(2, 772)
            tmp = m.take(2, NALL)
            omu, hmu = m.take(NRW), m.take(NRW)
            colrow = m.take(64)
            rows = m.take(P)
            vec = lambda ap: ap.rearrange("(k p) -> k p", p=P)
            small("cols", [(rows[0:14, :], vec(a["tshift_mu"][0])), (rows[14:18, :], vec(a["k_k"][0])),
                           (rows[18:22, :], vec(a["k_a"][0])),
                           (rows[22:26, :], a["r_k"][0].rearrange("(k h) n -> k (h n)", h=2)),
                           (rows[26:34, :], a["iclr_a0"][0].rearrange("d (k p) -> (d k) p", p=P))], after="h_T")

            def pad_zero(l):
                for i in range(2):
                    for c in (0, 513, 514, 771):
                        l.did(G.memset(pb[:, i, c:c + 1], 0.0).then_inc(l.sem, 1))

            def cols_read(l, bank):
                l.did(V.tensor_copy(cols[:, 0:34], bank[:, 0:34]).then_inc(l.sem, 1))
                l.wait_ge(*l.own())
                l.did(V.tensor_scalar(omu, cols[:, 0:NRW], -1.0, 1.0, ALU.mult, ALU.add).then_inc(l.sem, 1))
                l.did(V.tensor_scalar(hmu, cols[:, 0:NRW], 0.5, None, ALU.mult).then_inc(l.sem, 1))
                l.wait_ge(*l.own())
            products("cols", [{"have": ("cols",), "by": "dve", "read": cols_read,
                               "mms": [("t", lambda b: b[:, 0:34], rows[0:34, :], ident[0:34, 0:34])]}],
                     pool_fn=pad_zero)
            w_in = a["w_in"][0].rearrange("(k p) n -> p k n", p=P)
            ws = [stream(w_in[:, :, s * 512:(s + 1) * 512], (KD, 512)) for s in range(5)]
            groups = []
            for c0, c1, sl in ((0, 512, 0), (512, 768, 1)):
                for t in range(NTA if c0 else NT):
                    if t < NT:
                        dst = qkv[:, t, c0:c1]
                    else:
                        dst = kvc[:, t - NT, :]
                    w = ws[sl][1][:, :, c0 - 512 * sl:c1 - 512 * sl]
                    groups.append({"loads": [ws[sl][0]], "by": "act", "read": copy_out(dst, lambda b, n=c1 - c0: b[:, 0:n]),
                                   "mms": acc(lambda b, n=c1 - c0: b[:, 0:n],
                                              [(hT[:, k, t * P:(t + 1) * P], w[:, k, :]) for k in range(KD)])})
            for j in range(NRW):
                c = 768 + j * P
                sl = c // 512
                w = ws[sl][1][:, :, c - 512 * sl:c - 512 * sl + P]
                for t0, t1, o in ((0, T, 1), (T, NALL, 3)):
                    def read(l, bank, j=j, t0=t0, t1=t1, o=o):
                        if j >= 2 and t0 == 0:
                            l.wait_ge(*past("shifted", j - 2))
                        l.did(S.activation(pb[:, j % 2, t0 + o:t1 + o], bank[:, 0:t1 - t0], ACT.Copy).then_inc(l.sem, 1),
                              "projected", j, t0)
                    groups.append({"loads": [ws[sl][0]], "by": "act", "read": read,
                                   "mms": acc(lambda b, n=t1 - t0: b[:, 0:n],
                                              [(w[:, k, :], hT[:, k, t0:t1]) for k in range(KD)])})

            def shift(l):
                for j in range(NRW):
                    l.wait_ge(*past("projected", j, T))
                    p, tt = pb[:, j % 2, :], tmp[:, j % 2, :]
                    for t0, t1, o in ((0, T, 1), (T, NALL, 3)):
                        l.did(V.tensor_tensor(tt[:, t0:t1], p[:, t0 + o - 1:t1 + o - 1], p[:, t0 + o + 1:t1 + o + 1], ALU.add).then_inc(l.sem, 1))
                    l.wait_ge(*l.own())
                    l.did(V.tensor_scalar(tt, tt, hmu[:, j:j + 1], None, ALU.mult).then_inc(l.sem, 1))
                    l.wait_ge(*l.own())
                    for t0, t1, o in ((0, T, 1), (T, NALL, 3)):
                        l.did(V.scalar_tensor_tensor(out=sft[:, j, t0:t1], in0=p[:, t0 + o:t1 + o], scalar=omu[:, j:j + 1],
                                                     in1=tt[:, t0:t1], op0=ALU.mult, op1=ALU.add).then_inc(l.sem, 1), "shifted", j)
            products("w_in", groups, dve_extra=shift)

            pass

            def attention(name, heads, width, score, val, dst, scale, bufs, bias=None, lam=None, need=()):
                units = [(i, h, t) for i, h in enumerate(heads) for t in range(NT)]
                sb, pt, st = bufs
                nset = 2 if lam is not None else 1
                full = width(0) == width(NT - 1)
                n_key = [width(t) // P for t in range(NT)]

                def sbank(u, s):
                    return (u % 2) * 2 + s
                tb_of, cnt = {}, 0
                for u, (i, h, t) in enumerate(units):
                    for g in range((n_key[t] + 3) // 4):
                        tb_of[u, g] = (4 + cnt % 3, cnt)
                        cnt += 1
                by_cnt = {c: ug for ug, (_, c) in tb_of.items()}

                def sc_view(u, s, w):
                    if w > 512:
                        return banks[:, sbank(u, 0):sbank(u, 0) + 2, :].rearrange("p a b -> p (a b)")[:, 0:w]
                    return banks[:, sbank(u, s), 0:w]

                def f_pe(l):
                    for k in need:
                        l.wait_ge(*smalls[k])

                    def turn(u):
                        i, h, t = units[u]
                        l.wait_ge(*past(name, "P", u))
                        for g in range((n_key[t] + 3) // 4):
                            b, c = tb_of[u, g]
                            if c >= 3:
                                l.wait_ge(*past(name, "T", *by_cnt[c - 3]))
                            for j in range(4 * g, min(4 * g + 4, n_key[t])):
                                ins = TE.transpose(banks[:, b, (j - 4 * g) * P:(j - 4 * g + 1) * P],
                                                   sb[:, u % 2, j * P:(j + 1) * P], ident)
                            l.did(ins.then_inc(l.sem, 1), name, "turned", u, g)
                        if t == NT - 1:
                            if i >= 1:
                                l.wait_ge(*past(name, "out", i - 1))
                            for g in range((n_key[t] + 3) // 4):
                                l.wait_ge(*past(name, "T", u, g))
                            po = HD * (h % 2)
                            for j in range(n_key[t]):
                                q0 = 0 if full else j * P
                                ins = TE.matmul(banks[po:po + HD, 7, q0:T], val(h, j), pt[:, i % 2, j, q0:T],
                                                start=(j == 0), stop=(j == n_key[t] - 1))
                            l.did(ins.then_inc(l.sem, 1), name, "pv", i)
                    for u in range(len(units) + 1):
                        if u < len(units):
                            i, h, t = units[u]
                            if u >= 2:
                                l.wait_ge(*past(name, "E", u - 2))
                            for s, pieces in enumerate(score(h, t)):
                                w = width(t)
                                for q, k, c, n in pieces:
                                    ins = TE.matmul(sc_view(u, s, w)[:, c:c + n], q, k, start=True, stop=True)
                            l.did(ins.then_inc(l.sem, 1), name, "S", u)
                        if u >= 1:
                            turn(u - 1)

                def f_dve(l):
                    def finish(u):
                        i, h, t = units[u]
                        w = width(t)
                        l.wait_ge(*past(name, "E", u))
                        c = st[:, u % 2, :]
                        l.did(V.reciprocal(c[:, 4:4 + nset], c[:, 2:2 + nset]).then_inc(l.sem, 1))
                        l.wait_ge(*l.own())
                        p1 = sb[:, u % 2, 0:w]
                        if nset == 2:
                            p2 = sb[:, u % 2, 512:512 + w]
                            l.did(V.tensor_tensor(c[:, 5:6], c[:, 5:6], lam, ALU.mult).then_inc(l.sem, 1))
                            l.did(V.tensor_scalar(p1, p1, c[:, 4:5], None, ALU.mult).then_inc(l.sem, 1))
                            l.wait_ge(*l.own())
                            l.did(V.scalar_tensor_tensor(out=p1, in0=p2, scalar=c[:, 5:6], in1=p1,
                                                         op0=ALU.mult, op1=ALU.add).then_inc(l.sem, 1), name, "P", u)
                        else:
                            l.did(V.tensor_scalar(p1, p1, c[:, 4:5], None, ALU.mult).then_inc(l.sem, 1), name, "P", u)
                    for u in range(len(units) + 1):
                        if u < len(units):
                            i, h, t = units[u]
                            w = width(t)
                            l.wait_ge(*past(name, "S", u))
                            c = st[:, u % 2, :]
                            if u >= 2:
                                l.wait_ge(*past(name, "turned", u - 2, (n_key[units[u - 2][2]] + 3) // 4 - 1))
                            for s in range(nset):
                                v = sc_view(u, s, w)
                                if bias is not None:
                                    x = sb[:, u % 2, 512 * s:512 * s + w]
                                    l.did(V.scalar_tensor_tensor(out=x, in0=v, scalar=scale, in1=bias(h, t),
                                                                 op0=ALU.mult, op1=ALU.add).then_inc(l.sem, 1))
                                    l.wait_ge(*l.own())
                                    v = x
                                l.did(V.reduce_max(c[:, s:s + 1], v, axis=AX.X).then_inc(l.sem, 1))
                            l.wait_ge(*l.own())
                            l.did(V.tensor_scalar(c[:, 0:nset], c[:, 0:nset], -1.0 if bias is not None else -scale,
                                                  None, ALU.mult).then_inc(l.sem, 1), name, "max", u)
                        if u >= 1:
                            finish(u - 1)

                def f_act(l):
                    def evac(u):
                        i, h, t = units[u]
                        for g in range((n_key[t] + 3) // 4):
                            l.wait_ge(*past(name, "turned", u, g))
                            if i >= 2:
                                l.wait_ge(*past(name, "pv", i - 2))
                            m_ = min(4, n_key[t] - 4 * g)
                            l.did(S.activation(pt[:, i % 2, 4 * g:4 * g + m_, t * P:(t + 1) * P],
                                               banks[:, tb_of[u, g][0], 0:m_ * P].rearrange("p (a b) -> p a b", b=P),
                                               ACT.Copy).then_inc(l.sem, 1), name, "T", u, g)
                        if t == NT - 1:
                            l.wait_ge(*past(name, "pv", i))
                            po = HD * (h % 2)
                            l.did(S.activation(dst(h), banks[po:po + HD, 7, :], ACT.Copy).then_inc(l.sem, 1), name, "out", i)
                    for u in range(len(units) + 1):
                        if u < len(units):
                            i, h, t = units[u]
                            w = width(t)
                            l.wait_ge(*past(name, "max", u))
                            c = st[:, u % 2, :]
                            for s in range(nset):
                                src = sb[:, u % 2, 512 * s:512 * s + w] if bias is not None else sc_view(u, s, w)
                                l.did(S.activation(sb[:, u % 2, 512 * s:512 * s + w], src, ACT.Exp,
                                                   bias=c[:, s:s + 1], scale=1.0 if bias is not None else scale,
                                                   accum_out=c[:, 2 + s:3 + s]).then_inc(l.sem, 1))
                            l.name_last(name, "E", u)
                        if u >= 1:
                            evac(u - 1)
                stage(name, pe=f_pe, act=f_act, dve=f_dve)

            def part_two():
                hole = Stack(base.at, base.at + KD * NALL)
                m2 = after_proj.branch()
                gain = m2.take(640)
                rope = m2.take(NT, 64)
                kdup = m2.take(NTA, 2, 128)
                rms = m2.take(3, 44)
                qT = m2.take(4, T)
                kT = m2.take(2, NALL)
                sbuf_p = m2.take(2, NALL)
                st = m2.take(2, 8)
                ptb = hole.branch().take(2, NTA, T)
                hh = hole.branch()
                sq = hh.take(NT, 640)
                sqc = hh.take(NTC, 128)
                r1, r2, r3, r4 = (hh.take(10, 2, 16) for _ in range(4))
                gs = [(gain[:, h * HD:(h + 1) * HD], a["q_gain"].to_broadcast([P, HD])) for h in range(NH)]
                gs += [(gain[:, h * HD:(h + 1) * HD], a["k_gain"].to_broadcast([P, HD])) for h in range(NH, NH + NKV)]
                small("qk", gs + [(rope, a["k_rope"])], after="w_in")
                heads10 = lambda ap: ap.rearrange("p (h n) -> p h n", n=HD)

                def qk_dve(l):
                    l.wait_ge(*smalls["qk"])
                    for t in range(NT):
                        l.did(V.tensor_tensor(sq[:, t, :], qkv[:, t, 0:640], qkv[:, t, 0:640], ALU.mult).then_inc(l.sem, 1))
                    for t in range(NTC):
                        l.did(V.tensor_tensor(sqc[:, t, :], kvc[:, t, 0:128], kvc[:, t, 0:128], ALU.mult).then_inc(l.sem, 1))
                    l.wait_ge(*l.own())
                    for t in range(NT):
                        l.did(V.reduce_sum(rms[:, 0, 10 * t:10 * t + 10], heads10(sq[:, t, :]), axis=AX.X).then_inc(l.sem, 1))
                    l.did(V.reduce_sum(rms[:, 0, 40:44], heads10(sqc.rearrange("p a b -> p (a b)")), axis=AX.X).then_inc(l.sem, 1))
                    l.wait_ge(*l.own())
                    l.did(V.tensor_scalar(rms[:, 1, :], rms[:, 0, :], 1.0 / HD, RMS_EPS, ALU.mult, ALU.add).then_inc(l.sem, 1), "qk_var")
                    l.wait_ge(*past("qk_sd"))
                    l.did(V.reciprocal(rms[:, 0, :], rms[:, 2, :]).then_inc(l.sem, 1))
                    l.wait_ge(*l.own())
                    for t in range(NT):
                        v = heads10(qkv[:, t, 0:640])
                        l.did(V.tensor_tensor(v, v, rms[:, 0, 10 * t:10 * t + 10].unsqueeze(2).to_broadcast([P, 10, HD]), ALU.mult).then_inc(l.sem, 1))
                    for t in range(NTC):
                        v = heads10(kvc[:, t, 0:128])
                        l.did(V.tensor_tensor(v, v, rms[:, 0, 40 + 2 * t:42 + 2 * t].unsqueeze(2).to_broadcast([P, 2, HD]), ALU.mult).then_inc(l.sem, 1))
                    l.wait_ge(*l.own())
                    for t in range(NT):
                        l.did(V.tensor_tensor(qkv[:, t, 0:640], qkv[:, t, 0:640], gain, ALU.mult).then_inc(l.sem, 1))
                    for t in range(NTC):
                        l.did(V.tensor_tensor(kvc[:, t, 0:128], kvc[:, t, 0:128], gain[:, 512:640], ALU.mult).then_inc(l.sem, 1))
                    l.wait_ge(*l.own())
                    for t in range(NT):
                        v = qkv[:, t, 0:640].rearrange("p (h x y e) -> p h x y e", h=10, x=2, y=2)
                        t1, t2 = v[:, :, :, 0, :], v[:, :, :, 1, :]
                        tab = rope[:, t, :].rearrange("p (y x e) -> p y x e", y=2, x=2)
                        cs = tab[:, 0].unsqueeze(1).to_broadcast([P, 10, 2, 16])
                        sn = tab[:, 1].unsqueeze(1).to_broadcast([P, 10, 2, 16])
                        l.did(V.tensor_tensor(r1, t1, cs, ALU.mult).then_inc(l.sem, 1))
                        l.did(V.tensor_tensor(r2, t2, sn, ALU.mult).then_inc(l.sem, 1))
                        l.did(V.tensor_tensor(r3, t2, cs, ALU.mult).then_inc(l.sem, 1))
                        l.did(V.tensor_tensor(r4, t1, sn, ALU.mult).then_inc(l.sem, 1))
                        l.wait_ge(*l.own())
                        l.did(V.tensor_tensor(t1, r1, r2, ALU.subtract).then_inc(l.sem, 1))
                        l.did(V.tensor_tensor(t2, r3, r4, ALU.add).then_inc(l.sem, 1))
                        l.wait_ge(*l.own())
                    for t in range(NTA):
                        src = qkv[:, t, 512:640] if t < NT else kvc[:, t - NT, 0:128]
                        for e in range(2):
                            l.did(V.tensor_copy(kdup[:, t, :, e * HD:(e + 1) * HD], heads10(src)).then_inc(l.sem, 1))

                def qk_act(l):
                    l.wait_ge(*past("qk_var"))
                    l.did(S.activation(rms[:, 2, :], rms[:, 1, :], ACT.Sqrt).then_inc(l.sem, 1), "qk_sd")
                stage("qk_norm", dve=qk_dve, act=qk_act)
                gs = transpose_groups(lambda t: qkv[:, t, :], lambda k: qT[:, k, :], NT, 0, 4)
                gs += transpose_groups(lambda t: kdup[:, t].rearrange("p a b -> p (a b)"), lambda k: kT[:, k, 0:T], NT, 0, 2)
                gs += transpose_groups(lambda t: kdup[:, t].rearrange("p a b -> p (a b)"), lambda k: kT[:, k, T:NALL], NTC, NT, 2)
                products("qk_T", gs)

                def score(h, t):
                    po = HD * (h % 2)
                    q = qT[po:po + HD, h // 2, t * P:(t + 1) * P]
                    g = h // (NH // NKV)
                    return [[(q, kT[po:po + HD, g, 0:512], 0, 512), (q, kT[po:po + HD, g, 512:768], 512, 256)]]

                def val(h, j):
                    g = h // (NH // NKV)
                    src = qkv[:, j, 640:768] if j < NT else kvc[:, j - NT, 128:256]
                    return src[:, g * HD:(g + 1) * HD]
                attention("attend", list(range(NH)), lambda t: NALL, score, val,
                          lambda h: mixT[HD * (h % 2):HD * (h % 2) + HD, h // 2, :], HD ** -0.5, (sbuf_p, ptb, st))
                views.update(qT=qT, kT=kT, mixA=mixT[:, 0:4, :])

            def part_three():
                low = Stack(0, RING * SLOT)
                hole = Stack(base.at, base.at + KD * NALL)
                high = after_proj.branch()
                high.at -= NT * 768 + NTC * 256
                R, K_, V_ = 0, 4, 8
                vtm = hole.take(NTA, 512)
                gtm = hole.take(NT, 512)
                blk = hole.take(512)
                masks = low.take(2, 512)
                levm = low.take(2, 7, P)
                cum = low.take(2, 258)
                ones2 = low.take(P)
                hsel = low.take(2)
                w0 = low.take(2, 512)
                up = low.take(2, 512)
                gup = low.take(512)
                ytm = high.take(NT, 512)
                bonus = high.take(NT, 8)
                small("rwkv", [(masks, a["k_gram"].rearrange("d p n -> p d n")),
                               (levm, a["k_lev"].rearrange("d p l n -> p d l n")),
                               (cum, a["k_cum"].rearrange("d p n -> p d n")),
                               (ones2, a["k_ones2"]), (hsel, a["k_hsel"]),
                               (w0[:, 0, :], a["decay_w0"][0, 0:1, :].to_broadcast([P, 512])),
                               (w0[:, 1, :], a["decay_w0"][0, 1:2, :].to_broadcast([P, 512])),
                               (up[0:64], a["decay_up"][0].rearrange("d p n -> p d n")),
                               (up[64:128], a["iclr_up"][0].rearrange("d p n -> p d n")),
                               (gup, a["gate_up"][0])], after="attend")

                def gates(l):
                    l.did(S.activation(sft[0:64, 12, :], sft[0:64, 12, :], ACT.Tanh).then_inc(l.sem, 1))
                    l.did(S.activation(sft[:, 13, 0:T], sft[:, 13, 0:T], ACT.Sigmoid).then_inc(l.sem, 1))

                def bonus_dve(l):
                    for j in range(4):
                        l.did(V.scalar_tensor_tensor(out=rkx[:, j, :], in0=sft[:, R + j, 0:T],
                                                     scalar=cols[:, 22 + j:23 + j], in1=sft[:, K_ + j, 0:T],
                                                     op0=ALU.mult, op1=ALU.mult).then_inc(l.sem, 1))
                rkx = high.branch().take(4, T)
                stage("rwkv_gates", act=gates, dve=bonus_dve)
                gs = []
                for t in range(NTA):
                    gs.append({"by": halves(t), "have": ("rwkv",), "read": copy_out(vtm[:, t, :]),
                               "mms": [("t", (lambda b, j=j: b[:, j * P:(j + 1) * P]),
                                        sft[:, V_ + j, t * P:(t + 1) * P], ident) for j in range(4)]})
                for t in range(NT):
                    gs.append({"by": halves(t), "read": copy_out(gtm[:, t, :]),
                               "mms": acc(lambda b: b, [(sft[:, 13, t * P:(t + 1) * P], gup)])})
                for t in range(NT):
                    gs.append({"by": "dve", "read": copy_out(bonus[:, t, :], lambda b: b[:, 0:8]),
                               "mms": [("m", (lambda b, j=j: b[:, 2 * j:2 * j + 2]), rkx[:, j, t * P:(t + 1) * P],
                                        hsel, True, True) for j in range(4)]})
                products("rwkv_tm", gs)

                vdead = Stack(base.at + KD * NALL + 64 + V_ * NALL, base.at + KD * NALL + 64 + 12 * NALL)
                kkn, aa = high.take(NALL), high.take(NALL)
                kd, bb = high.take(NALL), high.take(NALL)
                sw = vdead.take(NTA, P)
                RA = high.take(NTA, 256)
                BK = high.take(NTA, 256)
                ex = vdead.take(2, 384)
                ends = high.take(NTA, 2)
                hop = high.take(NTA)
                Gm = low.take(NTA, 2, 512)
                Am = high.take(NTA, 2, P)
                Al = vdead.take(NTA, 256)
                XT = low.take(NTA, 2, 256)
                P1 = high.take(NTA, 256)
                BKt = high.take(NTA, 256)
                state = low.take(64)
                wsb, usb = low.take(P), low.take(P)

                def kk_pair(j):
                    kcol = cols[:, 14 + j:15 + j]
                    sq = aa

                    def f_dve(l):
                        l.did(V.tensor_scalar(kkn, sft[:, K_ + j, :], kcol, None, ALU.mult).then_inc(l.sem, 1))
                        l.wait_ge(*l.own())
                        l.did(V.tensor_tensor(sq, kkn, kkn, ALU.mult).then_inc(l.sem, 1))
                    stage(f"kk{j}", dve=f_dve)

                    def read(l, bank, t0, t1):
                        l.did(S.activation(bb[:, t0:t1], bank[:, 0:t1 - t0], ACT.Sqrt).then_inc(l.sem, 1))
                    gs = [{"by": "act", "read": (lambda l, b, t0=t0, t1=t1: read(l, b, t0, t1)),
                           "mms": acc(lambda b, n=t1 - t0: b[:, 0:n], [(ones2, sq[:, t0:t1])])}
                          for t0, t1 in ((0, T), (T, NALL))]
                    products(f"kk_norm{j}", gs)

                    def f_dve2(l):
                        l.did(V.tensor_scalar(bb, bb, L2_EPS, None, ALU.max).then_inc(l.sem, 1))
                        l.wait_ge(*l.own())
                        l.did(V.reciprocal(bb, bb).then_inc(l.sem, 1))
                        l.wait_ge(*l.own())
                        l.did(V.tensor_tensor(kkn, kkn, bb, ALU.mult).then_inc(l.sem, 1))
                    stage(f"kk_unit{j}", dve=f_dve2)

                def one_pass(j, d):
                    nm = f"rwkv{j}{d}"
                    js = slice(j * P, (j + 1) * P)
                    a0 = cols[:, 26 + 4 * d + j:27 + 4 * d + j]
                    ka = cols[:, 18 + j:19 + j]
                    gs = []
                    for q in range(2):
                        tiles = range(4) if q == 0 else range(4, 6)

                        def read(l, bank, tiles=tiles):
                            for c in tiles:
                                l.did(V.tensor_tensor(sw[:, c, :], bank[:, (c % 4) * P:(c % 4 + 1) * P], w0[:, d, js], ALU.add).then_inc(l.sem, 1))
                        gs.append({"by": "dve", "read": read, "mms": [
                            ("m", (lambda b, c=c: b[:, (c % 4) * P:(c % 4 + 1) * P]), sft[0:64, 12, c * P:(c + 1) * P],
                             up[0:64, d, js], True, True) for c in tiles]})
                    for t0, t1 in ((0, T), (T, NALL)):
                        def read(l, bank, t0=t0, t1=t1):
                            l.did(S.activation(aa[:, t0:t1], bank[:, 0:t1 - t0], ACT.Sigmoid, bias=a0).then_inc(l.sem, 1), nm, "a", t0)
                        gs.append({"by": "act", "read": read, "mms": acc(lambda b, n=t1 - t0: b[:, 0:n],
                                   [(up[64:128, d, js], sft[64:128, 12, t0:t1])])})

                    def act_x(l):
                        for q in range(2):
                            l.wait_ge(*past(nm + "in", "read", q))
                        l.did(S.activation(sw, sw, ACT.Sigmoid).then_inc(l.sem, 1))

                    def dve_x(l):
                        l.wait_ge(*past(nm, "a", 0))
                        l.wait_ge(*past(nm, "a", T))
                        l.did(V.tensor_scalar(kd, aa, -1.0, ka, ALU.add, ALU.mult).then_inc(l.sem, 1))
                        l.did(V.tensor_tensor(bb, kkn, aa, ALU.mult).then_inc(l.sem, 1))
                        l.wait_ge(*l.own())
                        l.did(V.scalar_tensor_tensor(out=kd, in0=kd, scalar=1.0, in1=sft[:, K_ + j, :], op0=ALU.add, op1=ALU.mult).then_inc(l.sem, 1))
                    products(nm + "in", gs, act_extra=act_x, dve_extra=dve_x)

                    def read_cum(c):
                        def read(l, bank):
                            if c >= 2:
                                l.wait_ge(*past(nm, "scaled", c - 2))
                            e = ex[:, c % 2, :]
                            l.did(S.activation(e[:, 0:256], bank[:, 0:256], ACT.Exp, scale=-DECAY_K).then_inc(l.sem, 1))
                            l.did(S.activation(e[:, 256:384], bank[:, 0:P], ACT.Exp, scale=DECAY_K).then_inc(l.sem, 1))
                            l.did(S.activation(ends[:, c, :], bank[:, 256:258], ACT.Exp, scale=-DECAY_K).then_inc(l.sem, 1), nm, "exps", c)
                        return read
                    gs = [{"by": "act", "read": read_cum(c),
                           "mms": acc(lambda b: b[:, 0:258], [(sw[:, c, :], cum[:, d, :])])} for c in range(NTA)]

                    def dve_y(l):
                        for c in range(NTA):
                            l.wait_ge(*past(nm, "exps", c))
                            e = ex[:, c % 2, :]
                            ts = slice(c * P, (c + 1) * P)
                            l.did(V.scalar_tensor_tensor(out=RA[:, c, 0:P], in0=e[:, P:256], scalar=-1.0, in1=kkn[:, ts],
                                                         op0=ALU.mult, op1=ALU.mult).then_inc(l.sem, 1))
                            l.did(V.tensor_tensor(RA[:, c, P:256], e[:, 0:P], sft[:, R + j, ts], ALU.mult).then_inc(l.sem, 1))
                            l.did(V.tensor_tensor(BK[:, c, 0:P], e[:, 256:384], bb[:, ts], ALU.mult).then_inc(l.sem, 1))
                            l.did(V.tensor_tensor(BK[:, c, P:256], e[:, 256:384], kd[:, ts], ALU.mult).then_inc(l.sem, 1), nm, "scaled", c)
                    products(nm + "cum", gs, dve_extra=dve_y)

                    gs = []
                    for c in range(NTA):
                        for h in range(2):
                            hs = slice(64 * h, 64 * h + 64)

                            def read(l, bank, c=c, h=h):
                                l.did(V.tensor_tensor(Gm[:, c, h, :], bank, masks[:, d, :], ALU.mult).then_inc(l.sem, 1))
                            gs.append({"by": "dve", "read": read, "mms": [
                                ("m", lambda b: b[:, 0:256], BK[hs, c, 0:P], RA[hs, c, :], True, True),
                                ("m", lambda b: b[:, 256:512], BK[hs, c, P:256], RA[hs, c, :], True, True)]})

                        for h in range(2):
                            def read2(l, bank, c=c, h=h):
                                l.did(V.tensor_tensor(Am[:, c, h], bank[:, 0:P], masks[:, 1 - d, 0:P], ALU.mult).then_inc(l.sem, 1))
                                l.did(V.tensor_copy(BKt[:, c, h * P:(h + 1) * P], bank[:, 256:384]).then_inc(l.sem, 1))
                            gs.append({"by": "dve", "read": read2, "mms": [
                                ("m", lambda b: b[:, 0:P], RA[64 * h:64 * h + 64, c, 0:P], BK[64 * h:64 * h + 64, c, 0:P],
                                 True, True),
                                ("t", lambda b: b[:, 256:384], BK[:, c, h * P:(h + 1) * P], ident)]})
                    idb = ident.unsqueeze(1).to_broadcast([P, 2, P])
                    lm = lambda dd, i: levm[:, dd, i, :].unsqueeze(1).to_broadcast([P, 2, P])

                    def start_inverse(l):
                        l.wait_ge(*l.own())
                        for c in range(NTA):
                            l.did(V.tensor_tensor(XT[:, c, :, 0:P], Gm[:, c, :, 0:P], lm(d, 0), ALU.mult).then_inc(l.sem, 1))
                            l.did(V.tensor_tensor(XT[:, c, :, P:256], Am[:, c], lm(1 - d, 0), ALU.mult).then_inc(l.sem, 1))
                        l.wait_ge(*l.own())
                        for c in range(NTA):
                            for e in range(2):
                                l.did(V.tensor_tensor(XT[:, c, :, e * P:(e + 1) * P], XT[:, c, :, e * P:(e + 1) * P], idb, ALU.add).then_inc(l.sem, 1))
                    products(nm + "gram", gs, dve_extra=start_inverse)

                    lv = nm + "lev"

                    def lev_pool(l):
                        for i in range(1, 7):
                            for c in range(NTA):
                                if i > 1:
                                    l.wait_ge(*past(lv, "P1made", i - 1, c))
                                l.did(G.tensor_tensor(Al[:, c, :].rearrange("p (h n) -> p h n", h=2), Am[:, c],
                                                      lm(1 - d, i), ALU.mult).then_inc(l.sem, 1), lv, "Al", i, c)

                    def lev_pe(l):
                        def second(i, c):
                            last = i == 6
                            l.wait_ge(*past(lv, "P1", i, c))
                            q = (i - 1) * NTA + c
                            if q >= 4:
                                l.wait_ge(*past(lv, "XT", *divmod4(q - 4)))
                            b = banks[:, 4 + q % 4, :]
                            for h in range(2):
                                p1 = P1[:, c, h * P:(h + 1) * P]
                                tt = XT[:, c, h, P:256]
                                ins = TE.matmul(b[:, h * 256:h * 256 + P], tt, p1, start=True, stop=True)
                                if not last:
                                    ins = TE.matmul(b[:, h * 256 + P:h * 256 + 256], p1, tt, start=True, stop=True)
                            l.did(ins.then_inc(l.sem, 1), lv, "XTmade", i, c)
                        for i in range(1, 7):
                            for c in range(NTA):
                                l.wait_ge(*past(lv, "Al", i, c))
                                if i > 1:
                                    l.wait_ge(*past(lv, "XT", i - 1, c))
                                q = (i - 1) * NTA + c
                                if q >= 4:
                                    l.wait_ge(*past(lv, "P1", *divmod4(q - 4)))
                                b = banks[:, q % 4, :]
                                for h in range(2):
                                    ins = TE.matmul(b[:, h * P:(h + 1) * P], Al[:, c, h * P:(h + 1) * P], XT[:, c, h, 0:P],
                                                    start=True, stop=True)
                                l.did(ins.then_inc(l.sem, 1), lv, "P1made", i, c)
                                if c >= 2:
                                    second(i, c - 2)
                            second(i, NTA - 2)
                            second(i, NTA - 1)

                    def divmod4(q):
                        return q // NTA + 1, q % NTA

                    def lev_act(l):
                        for i in range(1, 7):
                            for c in range(NTA):
                                l.wait_ge(*past(lv, "P1made", i, c))
                                if i > 1:
                                    l.wait_ge(*past(lv, "XTmade", i - 1, c))
                                l.did(S.activation(P1[:, c, :], banks[:, ((i - 1) * NTA + c) % 4, 0:256], ACT.Copy).then_inc(l.sem, 1), lv, "P1", i, c)

                    def lev_dve(l):
                        for i in range(1, 7):
                            for c in range(NTA):
                                l.wait_ge(*past(lv, "XTmade", i, c))
                                b = banks[:, 4 + ((i - 1) * NTA + c) % 4, :].rearrange("p (h n) -> p h n", h=2)
                                if i < 6:
                                    l.did(V.tensor_tensor(XT[:, c], b, XT[:, c], ALU.add).then_inc(l.sem, 1), lv, "XT", i, c)
                                else:
                                    l.did(V.tensor_tensor(XT[:, c, :, 0:P], b[:, :, 0:P], XT[:, c, :, 0:P], ALU.add).then_inc(l.sem, 1), lv, "XT", i, c)
                    stage(lv, pe=lev_pe, act=lev_act, dve=lev_dve, pool=lev_pool)

                    order = [4, 5, 0, 1, 2, 3] if d == 0 else [5, 4, 3, 2, 1, 0]
                    sq = nm + "seq"

                    def seq_pe(l):
                        for n, c in enumerate(order):
                            if n:
                                l.wait_ge(*past(sq, "state", n - 1))
                            for h in range(2):
                                hs = slice(64 * h, 64 * h + 64)
                                v = vtm[:, c, j * P + 64 * h:j * P + 64 * h + 64]
                                o = banks[:, h, 0:64]
                                if n:
                                    TE.matmul(o, RA[hs, c, 0:P], state[hs, :], start=True, stop=False)
                                ins = TE.matmul(o, Gm[:, c, h, 256:384], v, start=(n == 0), stop=True)
                            l.did(ins.then_inc(l.sem, 1), sq, "Wmade", n)
                            l.wait_ge(*past(sq, "W", n))
                            for h in range(2):
                                ins = TE.matmul(banks[:, 5, 64 * h:64 * h + 64], XT[:, c, h, 0:P], wsb[:, 64 * h:64 * h + 64],
                                                start=True, stop=True)
                            l.did(ins.then_inc(l.sem, 1), sq, "Umade", n)
                            l.wait_ge(*past(sq, "U", n))
                            if n < NTA - 1:
                                for h in range(2):
                                    hs = slice(64 * h, 64 * h + 64)
                                    v = vtm[:, c, j * P + 64 * h:j * P + 64 * h + 64]
                                    TE.matmul(banks[hs, 2, 0:64], BKt[:, c, 64 * h:64 * h + 64], usb[:, 64 * h:64 * h + 64],
                                              start=True, stop=False)
                                    ins = TE.matmul(banks[hs, 2, 0:64], BKt[:, c, P + 64 * h:P + 64 * h + 64], v,
                                                    start=False, stop=True)
                                l.did(ins.then_inc(l.sem, 1), sq, "Smade", n)
                            if c < NT:
                                if n > 3:
                                    l.wait_ge(*past(sq, "Y", n - 2))
                                for h in range(2):
                                    hs = slice(64 * h, 64 * h + 64)
                                    v = vtm[:, c, j * P + 64 * h:j * P + 64 * h + 64]
                                    o = banks[:, 3 + 3 * (n % 2) + h, 0:64]
                                    TE.matmul(o, RA[hs, c, P:256], state[hs, :], start=True, stop=False)
                                    TE.matmul(o, Gm[:, c, h, 128:256], usb[:, 64 * h:64 * h + 64], start=False, stop=False)
                                    ins = TE.matmul(o, Gm[:, c, h, 384:512], v, start=False, stop=True)
                                l.did(ins.then_inc(l.sem, 1), sq, "Ymade", n)

                    def seq_act(l):
                        for n, c in enumerate(order):
                            l.wait_ge(*past(sq, "Wmade", n))
                            l.did(S.activation(wsb.rearrange("p (h n) -> p h n", h=2), banks[:, 0:2, 0:64], ACT.Copy).then_inc(l.sem, 1), sq, "W", n)

                    def seq_dve(l):
                        for n in range(NTA - 1):
                            l.did(V.tensor_tensor(hop[:, n:n + 1], ends[:, order[n], 1:2], ends[:, order[n + 1], 0:1], ALU.mult).then_inc(l.sem, 1))
                        l.wait_ge(*l.own())
                        for n, c in enumerate(order):
                            l.wait_ge(*past(sq, "Umade", n))
                            if n:
                                l.wait_ge(*past(sq, "Ymade" if order[n - 1] < NT else "Smade", n - 1))
                            l.did(V.tensor_copy(usb, banks[:, 5, 0:P]).then_inc(l.sem, 1), sq, "U", n)
                            if n < NTA - 1:
                                l.wait_ge(*past(sq, "Smade", n))
                                if n:
                                    l.wait_ge(*past(sq, "Ymade" if c < NT else "Wmade", n))
                                    l.did(V.tensor_tensor(state, banks[:, 2, 0:64], state, ALU.add).then_inc(l.sem, 1))
                                    l.wait_ge(*l.own())
                                    l.did(V.tensor_scalar(state, state, hop[:, n:n + 1], None, ALU.mult).then_inc(l.sem, 1), sq, "state", n)
                                else:
                                    l.did(V.tensor_scalar(state, banks[:, 2, 0:64], hop[:, n:n + 1], None, ALU.mult).then_inc(l.sem, 1), sq, "state", n)
                            if c < NT:
                                l.wait_ge(*past(sq, "Ymade", n))
                                y = ytm[:, c, js].rearrange("p (h n) -> p h n", h=2)
                                made = banks[:, 3 + 3 * (n % 2):5 + 3 * (n % 2), 0:64]
                                if d == 0:
                                    l.did(V.tensor_copy(y, made).then_inc(l.sem, 1), sq, "Y", n)
                                else:
                                    l.did(V.tensor_tensor(y, made, y, ALU.add).then_inc(l.sem, 1), sq, "Y", n)
                    stage(sq, pe=seq_pe, act=seq_act, dve=seq_dve)

                for j in range(4):
                    kk_pair(j)
                    for d in range(2):
                        one_pass(j, d)
                views.update(ytm=ytm, vtm=vtm, gtm=gtm, bonus=bonus)

                gn = Stack(0, RING * SLOT)
                lg, lb = gn.take(512), gn.take(512)
                yc = gn.take(NT, 512)
                mu8, va8, rs8 = gn.take(32), gn.take(32), gn.take(32)
                small("lnx", [(lg, a["lnx_g"].to_broadcast([P, 512])), (lb, a["lnx_b"].to_broadcast([P, 512]))],
                      after="rwkv31seq")
                h64 = lambda ap: ap.rearrange("p t (h n) -> p (t h) n", n=HD)
                bc = lambda ap: ap.unsqueeze(2).to_broadcast([P, 32, HD])
                flat = lambda ap: ap.rearrange("p a b -> p (a b)")

                def gn_dve(l):
                    y3 = h64(ytm)
                    l.did(V.reduce_sum(mu8, y3, axis=AX.X).then_inc(l.sem, 1))
                    l.wait_ge(*l.own())
                    l.did(V.tensor_scalar(mu8, mu8, 1.0 / HD, None, ALU.mult).then_inc(l.sem, 1))
                    l.wait_ge(*l.own())
                    l.did(V.tensor_tensor(y3, y3, bc(mu8), ALU.subtract).then_inc(l.sem, 1))
                    l.wait_ge(*l.own())
                    l.did(V.tensor_tensor(yc, ytm, ytm, ALU.mult).then_inc(l.sem, 1))
                    l.wait_ge(*l.own())
                    l.did(V.reduce_sum(va8, h64(yc), axis=AX.X).then_inc(l.sem, 1))
                    l.wait_ge(*l.own())
                    l.did(V.tensor_scalar(va8, va8, 1.0 / HD, GN_EPS, ALU.mult, ALU.add).then_inc(l.sem, 1), "gn_var")
                    l.wait_ge(*past("gn_sd"))
                    l.did(V.reciprocal(va8, rs8).then_inc(l.sem, 1))
                    l.wait_ge(*l.own())
                    l.did(V.tensor_tensor(y3, y3, bc(va8), ALU.mult).then_inc(l.sem, 1))
                    l.did(V.tensor_tensor(h64(yc), h64(vtm[:, 0:NT, :]), bc(flat(bonus)), ALU.mult).then_inc(l.sem, 1))
                    l.wait_ge(*smalls["lnx"])
                    l.wait_ge(*l.own())
                    for src, op in ((lg, ALU.mult), (lb, ALU.add)):
                        l.did(V.tensor_tensor(ytm, ytm, src.unsqueeze(1).to_broadcast([P, NT, 512]), op).then_inc(l.sem, 1))
                        l.wait_ge(*l.own())
                    l.did(V.tensor_tensor(ytm, ytm, yc, ALU.add).then_inc(l.sem, 1))
                    l.wait_ge(*l.own())
                    l.did(V.tensor_tensor(ytm, ytm, gtm, ALU.mult).then_inc(l.sem, 1))

                def gn_act(l):
                    l.wait_ge(*past("gn_var"))
                    l.did(S.activation(rs8, va8, ACT.Sqrt).then_inc(l.sem, 1), "gn_sd")
                stage("rwkv_norm", dve=gn_dve, act=gn_act)
                products("rwkv_T", transpose_groups(lambda t: ytm[:, t, :], lambda k: mixT[:, 4 + k, :], NT, 0, 4))
                views.update(rwo=ytm, mixAll=mixT)

            def part_four():
                hold_stream("rwkv_T")
                x1 = region(base.at, NT, D)
                xin_at, gt_at, y_at, hid_at = (base.at + n * D for n in (4, 12, 16, 24))
                xr = region(xin_at, NT, D)
                g1, b1 = region(hid_at, D), region(hid_at + D, D)
                tmpx = region(hid_at + 2 * D, 2, 512)
                small("ln1", [(xr, a["x"][0].rearrange("(t p) n -> p t n", p=P)),
                              (g1, a["ln1_g"].to_broadcast([P, D])), (b1, a["ln1_b"].to_broadcast([P, D]))],
                      after="rwkv_T")

                def residual(name, ws_, gate, x_old, x_new, lhs, nk, tmpx, hv=None):
                    gs = []
                    for hf in range(2):
                        for t in range(NT):
                            i = len(gs)

                            def read(l, bank, hf=hf, t=t, i=i):
                                if hv:
                                    l.wait_ge(*smalls[hv])
                                v = slice(hf * 512, hf * 512 + 512)
                                l.wait_ge(*l.own())
                                l.did(V.tensor_tensor(tmpx[:, i % 2, :], bank, gate[:, v], ALU.mult).then_inc(l.sem, 1))
                                l.wait_ge(*l.own())
                                l.did(V.scalar_tensor_tensor(out=x_new[:, t, v], in0=x_old[:, t, v], scalar=ALPHA,
                                                             in1=tmpx[:, i % 2, :], op0=ALU.mult, op1=ALU.add).then_inc(l.sem, 1))
                            gs.append({"by": "dve", "read": read, "loads": [ws_[hf][0]] if ws_ else [],
                                       "mms": acc(lambda b: b, [lhs(k, t, hf) for k in range(nk)])})
                    products(name, gs)
                wo = a["w_out"][0].rearrange("(k p) n -> p k n", p=P)
                wos = [stream(wo[:, :, hf * 512:(hf + 1) * 512], (KD, 512)) for hf in range(2)]
                residual("w_out", wos, gt1, xr, x1,
                         lambda k, t, hf: (mixT[:, k, t * P:(t + 1) * P], wos[hf][1][:, k, :]), KD, tmpx, hv="ln1")
                norm_stage("norm_x1", lambda i: x1[:, i, :], lambda i: x1[:, i, :], NT, [], affine=(g1, b1))
                views.update(x1=x1)

                xh = region(y_at, NT, D)
                h2T = region(gt_at, KD, T)
                norm_stage("norm_h2", lambda i: x1[:, i, :], lambda i: xh[:, i, :], NT, [])
                products("h2_T", transpose_groups(lambda i: xh[:, i, :], lambda k: h2T[:, k, :], NT, 0, KD,
                                                  lambda k: (modcol[:, 32 + k, 0:1], modcol[:, 24 + k, 0:1])))
                sm = Stack(hid_at, hid_at + 5 * D)
                rw = sm.take(KD, NE)
                aff = stats[:, 120:184].rearrange("p (t e) -> p t e", e=NE)
                rank = stats[:, 184:248].rearrange("p (t e) -> p t e", e=NE)
                eqs = sm.take(NT, NE)
                late = sm.take(NT, NE)
                mx4, sm4 = sm.take(NT), sm.take(NT)
                affT = sm.take(T)
                before = sm.take(P)
                slots = sm.take(CAP)
                junk = sm.take(4, 512)
                small("router", [(rw, a["router_w"][0].rearrange("(k p) e -> p k e", p=P)),
                                 (before, a["k_before"][:, 0, 0:P]), (slots, a["k_slots"])], after="h2_T")

                def logits_read(l, bank):
                    lg = bank[:, 0:64].rearrange("p (t e) -> p t e", e=NE)
                    l.did(V.reduce_max(mx4, lg, axis=AX.X).then_inc(l.sem, 1))
                    l.wait_ge(*l.own())
                    l.did(V.tensor_tensor(aff, lg, mx4.unsqueeze(2).to_broadcast([P, NT, NE]), ALU.subtract).then_inc(l.sem, 1), "router_in")

                def router_act(l):
                    l.wait_ge(*past("router_in"))
                    l.did(S.activation(aff, aff, ACT.Exp).then_inc(l.sem, 1), "router_exp")

                def router_dve(l):
                    l.wait_ge(*past("router_exp"))
                    l.did(V.reduce_sum(sm4, aff, axis=AX.X).then_inc(l.sem, 1))
                    l.wait_ge(*l.own())
                    l.did(V.reciprocal(sm4, sm4).then_inc(l.sem, 1))
                    l.wait_ge(*l.own())
                    l.did(V.tensor_tensor(aff, aff, sm4.unsqueeze(2).to_broadcast([P, NT, NE]), ALU.mult).then_inc(l.sem, 1))
                products("router", [{"have": ("router",), "by": "dve", "read": logits_read, "mms": [
                    m_ for t in range(NT) for m_ in
                    acc(lambda b, t=t: b[:, t * NE:(t + 1) * NE],
                        [(h2T[:, k, t * P:(t + 1) * P], rw[:, k, :]) for k in range(KD)])]}],
                    act_extra=router_act, dve_extra=router_dve)
                products("aff_T", [{"by": "act", "read": copy_out(affT[0:NE, :], lambda b: b[0:NE, :]), "mms": [
                    ("t", (lambda b, t=t: b[0:NE, t * P:(t + 1) * P]), aff[:, t, :], ident) for t in range(NT)]}])

                affb = region(xin_at, NE, T)

                def bounce(l):
                    l.engine.dma_start(a["scratch"], affT[0:NE, :]).then_inc(scratch_io, 16)
                    l.engine.wait_ge(scratch_io, 16)
                    l.engine.dma_start(affb.rearrange("p e t -> p (e t)"), a["scratch"].rearrange("e t -> (e t)")
                                       .unsqueeze(0).to_broadcast([P, NE * T])).then_inc(scratch_io, 16)

                def ranks(l):
                    l.engine.wait_ge(scratch_io, 32)
                    for t in range(NT):
                        for e in range(NE):
                            s_ = aff[:, t, e:e + 1]
                            jk = junk[:, (t * NE + e) % 4, :]
                            if t:
                                l.did(V.tensor_scalar(jk[:, 0:t * P], affb[:, e, 0:t * P], s_, 0.0, ALU.is_ge, ALU.add,
                                                      accum_out=eqs[:, t, e:e + 1]).then_inc(l.sem, 1))
                            l.did(V.tensor_scalar(jk[:, t * P:T], affb[:, e, t * P:T], s_, 0.0, ALU.is_gt, ALU.add,
                                                  accum_out=rank[:, t, e:e + 1]).then_inc(l.sem, 1))
                            l.did(V.scalar_tensor_tensor(out=jk2[:, (t * NE + e) % 4, :], in0=affb[:, e, t * P:(t + 1) * P], scalar=s_,
                                                         in1=before, op0=ALU.is_equal, op1=ALU.mult,
                                                         accum_out=late[:, t, e:e + 1]).then_inc(l.sem, 1))
                            if (t * NE + e) % 4 == 3:
                                l.wait_ge(*l.own())
                    l.wait_ge(*l.own())
                    l.did(V.tensor_tensor(rank, rank, late, ALU.add).then_inc(l.sem, 1))
                    l.wait_ge(*l.own())
                    l.did(V.tensor_tensor(rank[:, 1:NT, :], rank[:, 1:NT, :], eqs[:, 1:NT, :], ALU.add).then_inc(l.sem, 1))
                jk2 = sm.take(4, P)
                stage("ranks", act=bounce, dve=ranks)

                G1 = region(y_at + 4 * D, NT, NE * CAP)
                G2 = region(hid_at, NT, NE * CAP)

                slots2 = region(gt_at, CAP)

                def save_slots(l):
                    l.did(V.tensor_copy(slots2, slots).then_inc(l.sem, 1))
                stage("slots", dve=save_slots)

                def onehot(l):
                    es = lambda ap: ap.rearrange("p (e c) -> p e c", c=CAP)
                    for t in range(NT):
                        l.did(V.tensor_tensor(es(G1[:, t, :]), slots2.unsqueeze(1).to_broadcast([P, NE, CAP]),
                                              rank[:, t, :].unsqueeze(2).to_broadcast([P, NE, CAP]), ALU.is_equal).then_inc(l.sem, 1))
                    l.wait_ge(*l.own())
                    for t in range(NT):
                        l.did(V.tensor_tensor(es(G2[:, t, :]), es(G1[:, t, :]),
                                              aff[:, t, :].unsqueeze(2).to_broadcast([P, NE, CAP]), ALU.mult).then_inc(l.sem, 1))
                stage("onehot", dve=onehot)
                xinT = region(xin_at, KD, NE * CAP)
                GgT = region(gt_at, NE // 2, T)
                gs = []
                for k in range(KD):
                    for hf in range(2):
                        v = slice(hf * 512, hf * 512 + 512)

                        def read(l, bank, k=k, v=v):
                            sc, sh = modcol[:, 32 + k, 0:1], modcol[:, 24 + k, 0:1]
                            if l is act:
                                l.did(S.activation(xinT[:, k, v], bank, ACT.Identity, bias=sh, scale=sc).then_inc(l.sem, 1))
                            else:
                                l.did(V.tensor_scalar(xinT[:, k, v], bank, sc, sh, ALU.mult, ALU.add).then_inc(l.sem, 1))
                        gs.append({"by": halves(k), "read": read, "mms": acc(lambda b: b, [
                            (xh[:, t, k * P:(k + 1) * P], G1[:, t, v]) for t in range(NT)])})
                for q in range(NE // 2):
                    gs.append({"by": halves(q), "read": copy_out(GgT[:, q, :]), "mms": [
                        ("t", (lambda b, t=t: b[:, t * P:(t + 1) * P]), G2[:, t, q * P:(q + 1) * P], ident) for t in range(NT)]})
                products("gather", gs)
                views.update(rank=rank, aff=aff, xinT=xinT)

                ysb = region(y_at, NE // 2, D)
                hb = Stack(hid_at, hid_at + 5 * D)
                hid = hb.take(2, D)
                sgt = hb.take(2, 512)
                hidT = hb.take(2, KD, P)
                gs, ex_ = [], "experts"
                wsrc = {n: a["exp_w_" + n] for n in ("gate", "up", "down")}

                def pair_weights(kind, q, hf):
                    return [stream(wsrc[kind][0, 2 * q + e].rearrange("(k p) n -> p k n", p=P)[:, :, hf * 512:(hf + 1) * 512],
                                   (KD, 512)) for e in range(2)]

                def two(w, lhs):
                    return [("m", (lambda b, e=e: b[64 * e:64 * e + 64, :]), lhs(k, e), w[e][1][:, k, :], k == 0, k == KD - 1)
                            for k in range(KD) for e in range(2)]

                def gate_up(q):
                    for hf in range(2):
                        v = slice(hf * 512, hf * 512 + 512)
                        for kind in ("gate", "up"):
                            w = pair_weights(kind, q, hf)
                            lhs = lambda k, e, q=q: xinT[:, k, (2 * q + e) * CAP:(2 * q + e + 1) * CAP]
                            g = {"by": "dve", "loads": [w[0][0], w[1][0]], "mms": two(w, lhs)}
                            if kind == "gate":
                                def first(l, bank, q=q, hf=hf):
                                    if 2 * q + hf >= 2:
                                        l.wait_ge(*past(ex_, "gated", 2 * q + hf - 2))
                                    l.did(S.activation(sgt[:, hf, :], bank, ACT.Sigmoid).then_inc(l.sem, 1), ex_, "sig", q, hf)

                                def read(l, bank, q=q, hf=hf, v=v):
                                    l.wait_ge(*past(ex_, "sig", q, hf))
                                    if q >= 2:
                                        l.wait_ge(*past(ex_, "turned", q - 2))
                                    l.did(V.tensor_tensor(hid[:, q % 2, v], bank, sgt[:, hf, :], ALU.mult).then_inc(l.sem, 1), ex_, "gated", 2 * q + hf)
                                g["first"] = ("act", first)
                            else:
                                def read(l, bank, q=q, hf=hf, v=v):
                                    l.wait_ge(*l.own())
                                    l.did(V.tensor_tensor(hid[:, q % 2, v], bank, hid[:, q % 2, v], ALU.mult).then_inc(l.sem, 1), ex_, "hid", q, hf)
                            g["read"] = read
                            gs.append(g)

                def down(q):
                    for hf in range(2):
                        g = {"by": "act", "after": [(ex_, "hid", q, hf)], "mms": [
                            ("t", (lambda b, i=i: b[:, i * P:(i + 1) * P]), hid[:, q % 2, (4 * hf + i) * P:(4 * hf + i + 1) * P], ident)
                            for i in range(4)]}

                        def read(l, bank, q=q, hf=hf):
                            if q >= 2:
                                l.wait_ge(*past(ex_, "downed", q - 2))
                            l.did(S.activation(hidT[:, q % 2, 4 * hf:4 * hf + 4, :], bank.rearrange("p (a b) -> p a b", b=P),
                                               ACT.Copy).then_inc(l.sem, 1), ex_, "hidT", q, hf)
                        g["read"] = read
                        if hf == 1:
                            g["name"] = (ex_, "turned", q)
                        gs.append(g)
                    for hf in range(2):
                        v = slice(hf * 512, hf * 512 + 512)
                        w = pair_weights("down", q, hf)
                        g = {"by": halves(hf), "loads": [w[0][0], w[1][0]], "after": [(ex_, "hidT", q, 0), (ex_, "hidT", q, 1)],
                             "mms": two(w, lambda k, e, q=q: hidT[:, q % 2, k, 64 * e:64 * e + 64]),
                             "read": copy_out(ysb[:, q, v])}
                        if hf == 1:
                            g["name"] = (ex_, "downed", q)
                        gs.append(g)
                for q in range(NE // 2 + 1):
                    if q < NE // 2:
                        gate_up(q)
                    if q:
                        down(q - 1)
                products(ex_, gs)

                small("ln2", [(region(xin_at, D), a["ln2_g"].to_broadcast([P, D])),
                              (region(xin_at + D, D), a["ln2_b"].to_broadcast([P, D]))], after="experts")
                tmpx2 = region(xin_at + 2 * D, 2, 512)
                residual("scatter", None, gt2, x1, x1,
                         lambda q, t, hf: (GgT[:, q, t * P:(t + 1) * P], ysb[:, q, hf * 512:(hf + 1) * 512]), NE // 2, tmpx2, hv="ln2")
                norm_stage("norm_x2", lambda i: x1[:, i, :], lambda i: x1[:, i, :], NT, [],
                           affine=(region(xin_at, D), region(xin_at + D, D)))
                views.update(x2=x1)

            def part_five():
                x = region(base.at, NT, D)
                hT = region(base.at + 4 * D, KD, T)
                rest = Stack(base.at + 8 * D)
                gcols = rest.take(98)
                grow = rest.take(D)
                ones2 = rest.take(P)
                sbk = rest.take(3, P)
                lamp = rest.take(2, 4, 32)
                lam = rest.take(8)
                st = rest.take(2, 8)
                ss = rest.take(16)
                grows = region(base.at + 4 * D, P)
                gains = a["norm_gains_2"]
                small("second", [(grows[0:96, :], gains.rearrange("l n (k p) -> (l n k) p", p=P)),
                                 (grows[96:98, 0:64], a["diff_subln_gain_2"]), (grows[96:98, 64:128], a["diff_subln_gain_2"]),
                                 (ones2, a["k_ones2"]), (sbk, a["k_sb"]),
                                 (lamp, a["diff_lambda_2"].rearrange("l a n -> (l a n)").unsqueeze(0).to_broadcast([P, 256]))],
                      after="norm_x2")
                lam_init = [0.8 - 0.6 * math.exp(-0.3 * l) for l in range(2)]

                def lam_dve(l):
                    l.wait_ge(*smalls["second"])
                    l.did(V.tensor_tensor(lamp[:, :, 0::2, :], lamp[:, :, 0::2, :], lamp[:, :, 1::2, :], ALU.mult).then_inc(l.sem, 1))
                    l.wait_ge(*l.own())
                    l.did(V.reduce_sum(lam[:, 0:4].rearrange("p (l a) -> p l a", l=2), lamp[:, :, 0::2, :], axis=AX.X).then_inc(l.sem, 1), "lam_sums")
                    l.wait_ge(*past("lam_exp"))
                    lv = lam[:, 0:4].rearrange("p (l a) -> p l a", l=2)
                    l.did(V.tensor_tensor(lam[:, 4:6], lv[:, :, 1], lv[:, :, 0], ALU.subtract).then_inc(l.sem, 1))
                    l.wait_ge(*l.own())
                    for i in range(2):
                        l.did(V.tensor_scalar(lam[:, 4 + i:5 + i], lam[:, 4 + i:5 + i], -lam_init[i], None, ALU.add).then_inc(l.sem, 1))

                def lam_act(l):
                    l.wait_ge(*past("lam_sums"))
                    l.did(S.activation(lam[:, 0:4], lam[:, 0:4], ACT.Exp).then_inc(l.sem, 1), "lam_exp")
                stage("lambda", dve=lam_dve, act=lam_act)
                products("gain_cols", [{"by": "dve", "read": copy_out(gcols, lambda b: b[:, 0:98]),
                                        "mms": [("t", lambda b: b[:, 0:98], grows[0:98, :], ident[0:98, 0:98])]}])

                def between(name, coef, row, col, key=None):
                    ybank = lambda t: banks[:, 2 * t:2 * t + 2, :].rearrange("p a b -> p (a b)")
                    scr = region(rest_end, 2, D)

                    def f_act(l):
                        if row is not None:
                            for t in range(NT):
                                l.did(S.activation(scr[:, t % 2, :], ybank(t), ACT.Square, accum_out=ss[:, t:t + 1]).then_inc(l.sem, 1), name, "yy", t)
                                l.wait_ge(*l.own())
                            for t in range(NT):
                                l.wait_ge(*past(name, "yvar", t))
                                l.did(S.activation(ss[:, 4 + t:5 + t], ss[:, 4 + t:5 + t], ACT.Sqrt).then_inc(l.sem, 1), name, "ysd", t)
                        if col is None:
                            return
                        for t in range(NT):
                            if row is not None:
                                l.wait_ge(*past(name, "x", t))
                            l.wait_ge(*l.own())
                            l.did(S.activation(scr[:, t % 2, :], x[:, t, :], ACT.Square, accum_out=ss[:, 8 + t:9 + t]).then_inc(l.sem, 1), name, "xx", t)
                        for t in range(NT):
                            l.wait_ge(*past(name, "xvar", t))
                            l.did(S.activation(ss[:, 12 + t:13 + t], ss[:, 12 + t:13 + t], ACT.Sqrt).then_inc(l.sem, 1), name, "xsd", t)
                        for t in range(NT):
                            for hf in (1,):
                                l.wait_ge(*past(name, "turned", t, hf))
                                for i in range(4):
                                    k = 4 * hf + i
                                    if True:
                                        l.did(S.activation(hT[:, k, t * P:(t + 1) * P], banks[:, 2 * t + hf, i * P:(i + 1) * P],
                                                           ACT.Copy, scale=col(k)).then_inc(l.sem, 1))

                    def f_dve(l):
                        if row is not None:
                            l.wait_ge(*smalls[key])
                            for t in range(NT):
                                l.wait_ge(*past(name, "yy", t))
                                l.did(V.tensor_scalar(ss[:, 4 + t:5 + t], ss[:, t:t + 1], 1.0 / D, NORM_EPS, ALU.mult, ALU.add).then_inc(l.sem, 1), name, "yvar", t)
                            for t in range(NT):
                                l.wait_ge(*past(name, "ysd", t))
                                l.did(V.reciprocal(ss[:, 4 + t:5 + t], ss[:, 4 + t:5 + t]).then_inc(l.sem, 1))
                            l.wait_ge(*l.own())
                            if coef != 1.0:
                                l.did(V.tensor_scalar(ss[:, 4:8], ss[:, 4:8], coef, None, ALU.mult).then_inc(l.sem, 1))
                                l.wait_ge(*l.own())
                            for t in range(NT):
                                l.did(V.scalar_tensor_tensor(out=ytmp[:, t % 2, :], in0=ybank(t), scalar=ss[:, 4 + t:5 + t], in1=grow,
                                                             op0=ALU.mult, op1=ALU.mult).then_inc(l.sem, 1))
                                l.wait_ge(*l.own())
                                l.did(V.tensor_tensor(x[:, t, :], x[:, t, :], ytmp[:, t % 2, :], ALU.add).then_inc(l.sem, 1), name, "x", t)
                        if col is None:
                            return
                        for t in range(NT):
                            l.wait_ge(*past(name, "xx", t))
                            l.did(V.tensor_scalar(ss[:, 12 + t:13 + t], ss[:, 8 + t:9 + t], 1.0 / D, NORM_EPS, ALU.mult, ALU.add).then_inc(l.sem, 1), name, "xvar", t)
                        for t in range(NT):
                            l.wait_ge(*past(name, "xsd", t))
                            l.did(V.reciprocal(ss[:, 12 + t:13 + t], ss[:, 12 + t:13 + t]).then_inc(l.sem, 1))
                            l.wait_ge(*l.own())
                            if t >= 2:
                                l.wait_ge(*past(name, "turned", t - 2, 1))
                            l.did(V.tensor_scalar(ytmp[:, t % 2, :], x[:, t, :], ss[:, 12 + t:13 + t], None, ALU.mult).then_inc(l.sem, 1), name, "xs", t)
                            if t:
                                evac(l, t - 1)
                        evac(l, NT - 1)

                    def evac(l, t):
                        for hf in (0,):
                            l.wait_ge(*past(name, "turned", t, hf))
                            for i in range(4):
                                k = 4 * hf + i
                                if True:
                                    l.did(V.tensor_scalar(hT[:, k, t * P:(t + 1) * P], banks[:, 2 * t + hf, i * P:(i + 1) * P],
                                                          col(k), None, ALU.mult).then_inc(l.sem, 1))

                    def f_pe(l):
                        if col is None:
                            return
                        for t in range(NT):
                            l.wait_ge(*past(name, "xs", t))
                            for hf in range(2):
                                for i in range(4):
                                    k = 4 * hf + i
                                    ins = TE.transpose(banks[:, 2 * t + hf, i * P:(i + 1) * P], ytmp[:, t % 2, k * P:(k + 1) * P], ident)
                                l.did(ins.then_inc(l.sem, 1), name, "turned", t, hf)
                    stage(name, act=f_act, dve=f_dve, pe=f_pe)
                ytmp = rest.take(2, D)
                rest_end = rest.at
                rest.take(2, D)
                body = rest.at
                gcol = lambda l, n: (lambda k: gcols[:, (l * 6 + n) * KD + k:(l * 6 + n) * KD + k + 1])

                def ffn(l_, f_):
                    nm = f"ffn{l_}{f_}"
                    hidT = region(body, NF, T)
                    sgt = region(rest_end, 2, T)
                    wg, wu, wd = (a["w_ffn_" + n + "_2"][l_, f_] for n in ("gate", "up", "down"))
                    src = lambda w, c: w.rearrange("(k p) n -> p k n", p=P)[:, :, c * 256:(c + 1) * 256]
                    gs = []
                    for s_ in range(NF // 2):
                        n, w = stream_many([((KD, 256), src(wg, s_)), ((KD, 256), src(wu, s_))])
                        for c in range(2):
                            f = 2 * s_ + c
                            cs = slice(c * P, (c + 1) * P)

                            def first(l, bank, f=f):
                                if f >= 2:
                                    l.wait_ge(*past(nm, "gated", f - 2))
                                l.did(S.activation(sgt[:, f % 2, :], bank, ACT.Sigmoid).then_inc(l.sem, 1), nm, "sig", f)

                            def read(l, bank, f=f):
                                l.wait_ge(*past(nm, "sig", f))
                                l.did(V.tensor_tensor(hidT[:, f, :], bank, sgt[:, f % 2, :], ALU.mult).then_inc(l.sem, 1), nm, "gated", f)

                            def read_up(l, bank, f=f):
                                l.wait_ge(*l.own())
                                l.did(V.tensor_tensor(hidT[:, f, :], bank, hidT[:, f, :], ALU.mult).then_inc(l.sem, 1), nm, "hid", f)
                            gs.append({"by": "dve", "first": ("act", first), "read": read, "loads": [n],
                                       "mms": acc(lambda b: b, [(w[0][:, k, cs], hT[:, k, :]) for k in range(KD)])})
                            gs.append({"by": "dve", "read": read_up, "loads": [n],
                                       "mms": acc(lambda b: b, [(w[1][:, k, cs], hT[:, k, :]) for k in range(KD)])})
                    products(nm, gs)
                    downs = []
                    for s_ in range((NF + 3) // 4):
                        m_ = min(4, NF - 4 * s_)
                        downs.append(stream(wd.rearrange("(f p) n -> p f n", p=P)[:, 4 * s_:4 * s_ + m_, :], (m_, D)) + (m_,))
                    small(nm + "g", [(grow, gains[l_, 1 if f_ == 0 else 5, :].unsqueeze(0).to_broadcast([P, D]))], after=nm)

                    def f_pe(l):
                        for s_, (n, w, m_) in enumerate(downs):
                            l.wait_ge(ring_full[n[0] % RING], n[1])
                            for f in range(4 * s_, 4 * s_ + m_):
                                for t in range(NT):
                                    for hf in range(2):
                                        ins = TE.matmul(banks[:, 2 * t + hf, :], hidT[:, f, t * P:(t + 1) * P],
                                                        w[:, f - 4 * s_, hf * 512:(hf + 1) * 512], start=(f == 0), stop=(f == NF - 1))
                            l.did(ins.then_inc(l.sem, 1), nm, "downed", s_)
                            l.name_last("freed", n[0])
                    stage(nm + "down", pe=f_pe)

                def mixer(l_):
                    nm = f"mix{l_}"
                    m5 = Stack(body)
                    qk = m5.take(16, T)
                    vt = m5.take(NT, D)
                    extra = m5.at
                    w_src = a["w_in_2"][l_].rearrange("(k p) n -> p k n", p=P)
                    ws = [stream(w_src[:, :, s_ * 512:(s_ + 1) * 512], (KD, 512)) for s_ in range(6)]
                    fm = {c * P: i for i, c in enumerate([0, 1, 2, 3, 4, 5, 9, 10, 11, 12, 15, 16, 17, 18, 19, 20])}
                    tm = {768: (256, 0), 1024: (128, 256), 1664: (256, 384), 2688: (384, 640)}
                    gs = []
                    for c0 in sorted(list(fm) + list(tm)):
                        n, w = ws[c0 // 512]
                        o = c0 % 512
                        if c0 in fm:
                            i = fm[c0]

                            def read(l, bank, i=i):
                                if 10 <= i < 13:
                                    if l is act:
                                        l.did(S.activation(qk[:, i, :], bank, ACT.Copy, scale=HD ** -0.5).then_inc(l.sem, 1))
                                    else:
                                        l.did(V.tensor_scalar(qk[:, i, :], bank, HD ** -0.5, None, ALU.mult).then_inc(l.sem, 1))
                                else:
                                    copy_out(qk[:, i, :])(l, bank)
                            gs.append({"by": halves(len(gs)), "loads": [n], "read": read,
                                       "mms": acc(lambda b: b, [(w[:, k, o:o + P], hT[:, k, :]) for k in range(KD)])})
                        else:
                            width, v0 = tm[c0]
                            for t in range(NT):
                                gs.append({"by": halves(len(gs)), "loads": [n],
                                           "read": copy_out(vt[:, t, v0:v0 + width], lambda b, width=width: b[:, 0:width]),
                                           "mms": acc(lambda b, width=width: b[:, 0:width],
                                                      [(hT[:, k, t * P:(t + 1) * P], w[:, k, o:o + width]) for k in range(KD)])})
                    products(nm, gs)
                    pt = region(base.at + 4 * D, 2, NT, T)
                    sb = region(rest_end - 2 * D, 2, D)
                    b_dil = region(extra, 6, T)
                    b_dif = region(rest_end, 4, T)
                    small(nm + "bias", [(b_dil, a["k_bias"][0:6, :, 0:T].rearrange("h p n -> p h n")),
                                        (b_dif, a["k_bias"][6:10, :, 0:T].rearrange("h p n -> p h n")),
                                        (grow, gains[l_, 3, :].unsqueeze(0).to_broadcast([P, D]))], after=nm)
                    smalls[f"mix{l_}g"] = smalls[nm + "bias"]
                    width = lambda t: P * (t + 1)
                    half = lambda h: HD * (h % 2)

                    def s_dil(h, t):
                        po = half(h)
                        return [[(qk[po:po + HD, h // 2, t * P:(t + 1) * P], qk[po:po + HD, 3 + h // 2, 0:width(t)], 0, width(t))]]
                    attention(nm + "dil", list(range(6)), width, s_dil, lambda h, j: vt[:, j, h * HD:(h + 1) * HD],
                              lambda h: mixT[half(h):half(h) + HD, h // 2, :], HD ** -0.5, (sb, pt, st),
                              bias=lambda h, t: b_dil[:, h, 384 - P * t:T], need=(nm + "bias",))

                    def s_dif(h, t):
                        out_ = []
                        for e in range(2):
                            po = half(h) + 32 * e
                            out_.append([(qk[po:po + 32, 6 + h // 2, t * P:(t + 1) * P], qk[po:po + 32, 8 + h // 2, 0:width(t)], 0, width(t))])
                        return out_
                    attention(nm + "dif", list(range(4)), width, s_dif, lambda h, j: vt[:, j, 384 + h * HD:384 + (h + 1) * HD],
                              lambda h: mixT[half(h):half(h) + HD, 3 + h // 2, :], 32 ** -0.5, (sb, pt, st),
                              bias=lambda h, t: b_dif[:, h, 384 - P * t:T], lam=lam[:, 4 + l_:5 + l_], need=(nm + "bias",))

                    sq2 = region(extra, 2, T)
                    rs2 = region(extra + 2 * T, 2, T)

                    def sub_sq(l):
                        l.did(V.tensor_tensor(sq2, mixT[:, 3:5, :], mixT[:, 3:5, :], ALU.mult).then_inc(l.sem, 1))
                    stage(nm + "subsq", dve=sub_sq)

                    def sub_read(l, bank, i):
                        l.did(V.tensor_scalar(sq2[:, i, :], bank, 1.0 / HD, NORM_EPS, ALU.mult, ALU.add).then_inc(l.sem, 1), nm, "subvar", i)

                    def sub_act(l):
                        for i in range(2):
                            l.wait_ge(*past(nm, "subvar", i))
                            l.did(S.activation(rs2[:, i, :], sq2[:, i, :], ACT.Sqrt).then_inc(l.sem, 1), nm, "subsd", i)

                    def sub_dve(l):
                        for i in range(2):
                            l.wait_ge(*past(nm, "subsd", i))
                            l.did(V.reciprocal(rs2[:, i, :], rs2[:, i, :]).then_inc(l.sem, 1))
                            l.wait_ge(*l.own())
                            l.did(V.scalar_tensor_tensor(out=mixT[:, 3 + i, :], in0=mixT[:, 3 + i, :], scalar=gcols[:, 96 + l_:97 + l_],
                                                         in1=rs2[:, i, :], op0=ALU.mult, op1=ALU.mult).then_inc(l.sem, 1))
                        l.wait_ge(*l.own())
                        l.did(V.tensor_scalar(mixT[:, 3:5, :], mixT[:, 3:5, :], 1.0 - lam_init[l_], None, ALU.mult).then_inc(l.sem, 1))
                    products(nm + "sub", [{"by": "dve", "read": (lambda l, b, i=i: sub_read(l, b, i)),
                                           "mms": acc(lambda b: b, [(ones2, sq2[:, i, :])])} for i in range(2)],
                             act_extra=sub_act, dve_extra=sub_dve)

                    sp = region(extra, 2, 1280)
                    wt = region(base.at + 4 * D, 2, 1280)
                    nb = nm + "stick"
                    where = {0: (0, 0, 0), 1: (1, 0, 512), 3: (1, 384, 896), 2: (2, 0, 1024)}
                    full3 = lambda b0: [(banks[:, b0, :], 0), (banks[:, b0 + 1, :], 512), (banks[:, b0 + 2, 0:256], 1024)]

                    def st_pe(l):
                        def zs(i, b0, start_only):
                            po = half(i)
                            for s_ in (0, 1, 3, 2):
                                b, c, _ = where[s_]
                                n = T - s_ * P
                                ins = TE.matmul(banks[:, b0 + b, c:c + n], qk[po:po + HD, 13 + i // 2, s_ * P:(s_ + 1) * P],
                                                qk[po:po + HD, 10 + i // 2, s_ * P:T], start=True, stop=start_only)
                                if not start_only:
                                    for j in range(s_, NT):
                                        m_ = T - j * P
                                        oj = where[j][2]
                                        ins = TE.matmul(banks[:, b0 + b, c + (j - s_) * P:c + n], sbk[:, 0 if j == s_ else 1, :],
                                                        sp[:, i % 2, oj:oj + m_], start=False, stop=(j == NT - 1))
                            return ins
                        for i in range(6 + 2):
                            if i < 6:
                                if i:
                                    l.wait_ge(*past(nb, "sp", i - 1))
                                l.did(zs(i, 0, True).then_inc(l.sem, 1), nb, "z", i)
                            if i >= 2:
                                h = i - 2
                                po = half(h)
                                l.wait_ge(*past(nb, "w", h))
                                if h >= 2:
                                    l.wait_ge(*past(nb, "o", h - 2))
                                for j in range(NT):
                                    oj = where[j][2]
                                    ins = TE.matmul(banks[po:po + HD, 6 + h % 2, j * P:T], vt[:, j, 640 + h * HD:640 + (h + 1) * HD],
                                                    wt[:, h % 2, oj:oj + T - j * P], start=(j == 0), stop=(j == NT - 1))
                                l.did(ins.then_inc(l.sem, 1), nb, "pv", h)
                            if 1 <= i <= 6:
                                h = i - 1
                                l.wait_ge(*past(nb, "sp", h))
                                if h:
                                    l.wait_ge(*past(nb, "w", h - 1))
                                l.did(zs(h, 3, False).then_inc(l.sem, 1), nb, "zc", h)

                    def st_act(l):
                        for i in range(7):
                            if i < 6:
                                l.wait_ge(*past(nb, "z", i))
                                if i >= 2:
                                    l.wait_ge(*past(nb, "zc", i - 2))
                                for b, o in full3(0):
                                    n = b.shape[1]
                                    l.did(S.activation(sp[:, i % 2, o:o + n], b, ACT.Abs).then_inc(l.sem, 1))
                                l.wait_ge(*l.own())
                                l.did(S.activation(sp[:, i % 2, :], sp[:, i % 2, :], ACT.Exp, scale=-1.0).then_inc(l.sem, 1))
                                l.wait_ge(*l.own())
                                l.did(S.activation(sp[:, i % 2, :], sp[:, i % 2, :], ACT.Ln, bias=1.0).then_inc(l.sem, 1), nb, "ln", i)
                            if i >= 1:
                                h = i - 1
                                l.wait_ge(*past(nb, "clamped", h))
                                l.did(S.activation(wt[:, h % 2, :], wt[:, h % 2, :], ACT.Exp).then_inc(l.sem, 1), nb, "exp", h)
                                if h:
                                    l.wait_ge(*past(nb, "pv", h - 1))
                                    out_copy(l, h - 1)
                        l.wait_ge(*past(nb, "pv", 5))
                        out_copy(l, 5)

                    def out_copy(l, h):
                        po = half(h)
                        l.did(S.activation(mixT[po:po + HD, 5 + h // 2, :], banks[po:po + HD, 6 + h % 2, :], ACT.Copy).then_inc(l.sem, 1), nb, "o", h)

                    def st_dve(l):
                        def mask(buf):
                            for s_ in range(NT):
                                o = where[s_][2]
                                l.did(V.tensor_tensor(buf[:, o:o + P], buf[:, o:o + P], sbk[:, 2, :], ALU.mult).then_inc(l.sem, 1))
                        for i in range(7):
                            if i >= 1:
                                h = i - 1
                                l.wait_ge(*past(nb, "zc", h))
                                if h >= 2:
                                    l.wait_ge(*past(nb, "pv", h - 2))
                                for b, o in full3(3):
                                    n = b.shape[1]
                                    l.did(V.tensor_scalar(wt[:, h % 2, o:o + n], b, 0.0, None, ALU.min).then_inc(l.sem, 1))
                                l.name_last(nb, "clamped", h)
                            if i < 6:
                                l.wait_ge(*past(nb, "ln", i))
                                for b, o in full3(0):
                                    n = b.shape[1]
                                    l.did(V.scalar_tensor_tensor(out=sp[:, i % 2, o:o + n], in0=b, scalar=0.0, in1=sp[:, i % 2, o:o + n],
                                                                 op0=ALU.max, op1=ALU.add).then_inc(l.sem, 1))
                                l.wait_ge(*l.own())
                                mask(sp[:, i % 2, :])
                                l.name_last(nb, "sp", i)
                            if i >= 1:
                                h = i - 1
                                l.wait_ge(*past(nb, "exp", h))
                                mask(wt[:, h % 2, :])
                                l.name_last(nb, "w", h)
                    stage(nb, pe=st_pe, act=st_act, dve=st_dve)

                    wo_src = a["w_out_2"][l_].rearrange("(k p) n -> p k n", p=P)
                    wos = [stream(wo_src[:, :, hf * 512:(hf + 1) * 512], (KD, 512)) for hf in range(2)]

                    def out_pe(l):
                        for hf, (n, w) in enumerate(wos):
                            l.wait_ge(ring_full[n[0] % RING], n[1])
                            for t in range(NT):
                                for k in range(KD):
                                    ins = TE.matmul(banks[:, 2 * t + hf, :], mixT[:, k, t * P:(t + 1) * P], w[:, k, :],
                                                    start=(k == 0), stop=(k == KD - 1))
                            l.did(ins.then_inc(l.sem, 1), nm, "out", hf)
                            l.name_last("freed", n[0])
                    stage(nm + "out", pe=out_pe)
                    if l_ == 0:
                        views["mix0"] = mixT

                between("open", None, None, gcol(0, 0))
                for l_ in range(2):
                    ffn(l_, 0)
                    between(f"mid{l_}a", 0.5, True, gcol(l_, 2), key=f"ffn{l_}0g")
                    mixer(l_)
                    between(f"mid{l_}b", 1.0, True, gcol(l_, 4), key=f"mix{l_}g")
                    ffn(l_, 1)
                    between(f"mid{l_}c", 0.5, True, gcol(1, 0) if l_ == 0 else None, key=f"ffn{l_}1g")
                views["final_x"] = x
                views["xfinal"] = x


            if upto >= 2:
                part_two()
            if upto >= 3:
                part_three()
            if upto >= 4:
                part_four()
            if upto >= 5:
                part_five()
            if me.name == "sp":
                for e in ("pe", "act", "dve", "pool"):
                    me.wait_ge(*past("end", stages[-1], e))
                sends = []
                if upto >= 5:
                    sends.append((out[0].rearrange("(t p) n -> p t n", p=P), views["final_x"]))
                for name in debug or ():
                    v = views[name]
                    shape = [v.shape[i] for i in range(len(v.shape))]
                    sends.append((nc.dram_tensor("dbg_" + name, shape, F32, kind="ExternalOutput").ap(), v))
                for dst, src in sends:
                    me.engine.dma_start(dst, src).then_inc(stored, 16)
                me.wait_ge(stored, 16 * len(sends))

        block = ctx.enter_context(nc.Block())

        @block.sync
        def _(eng):
            program(lanes["sp"])

        @block.tensor
        def _(eng):
            program(pe)

        @block.scalar
        def _(eng):
            program(act)

        @block.vector
        def _(eng):
            program(dve)

        @block.gpsimd
        def _(eng):
            program(pool)
    return marks.now


_INS = ['x', 'c', 'ctx', 'c_ctx', 'w_ada', 'b_ada', 'w_in', 'q_gain', 'k_gain', 'tshift_mu', 'decay_w0',
        'decay_up', 'iclr_a0', 'iclr_up', 'gate_up', 'k_k', 'k_a', 'r_k', 'lnx_g', 'lnx_b', 'w_out', 'ln1_g',
        'ln1_b', 'router_w', 'exp_w_gate', 'exp_w_up', 'exp_w_down', 'ln2_g', 'ln2_b', 'norm_gains_2',
        'w_ffn_gate_2', 'w_ffn_up_2', 'w_ffn_down_2', 'w_in_2', 'w_out_2', 'diff_lambda_2',
        'diff_subln_gain_2']


def kernel(_upto=5, _debug=None, **inputs):
    import numpy as _np
    import concourse.bacc as _bacc
    from concourse.bass_utils import run_bass_kernel_spmd as _run

    known = {}
    for final in (False, True):
        nc = _bacc.Bacc("TRN2", target_bir_lowering=False, num_devices=1)
        arrays, args = {}, {}
        for name in _INS:
            arr = _np.ascontiguousarray(inputs[name])
            arrays[f"in_{name}"] = arr
            args[name] = nc.dram_tensor(f"in_{name}", arr.shape, F32, kind="ExternalInput").ap()
        for name, arr in constants().items():
            arrays[name] = arr
            args[name] = nc.dram_tensor(name, arr.shape, F32, kind="ExternalInput").ap()
        out = nc.dram_tensor("out", (1, T, D), F32, kind="ExternalOutput").ap()
        args["scratch"] = nc.dram_tensor("scratch", (NE, T), F32, kind="Internal").ap()
        known = build(nc, args, out, known, final, _upto, _debug)
    r = _run(nc, [arrays], core_ids=[0])
    return r.results[0]["out"]
```

```python
from contextlib import ExitStack
import math

import numpy as np
import concourse.bass as bass
from concourse import mybir

F32 = mybir.dt.float32
F32R = mybir.dt.float32r
ALU = mybir.AluOpType
ACT = mybir.ActivationFunctionType
AX = mybir.AxisListType

P = 128
D = 1024
KD = D // P
T, TC = 512, 256
NT, NTC = T // P, TC // P
NTA = NT + NTC
NALL = T + TC
HD = 64
NH, NKV = 8, 2
NE, CAP = 16, 64
NRW = 14
FF = 2816
NF = FF // P
ALPHA = 2.0 ** 0.25
LN_EPS, RMS_EPS, GN_EPS, NORM_EPS, L2_EPS = 1e-5, 1e-6, 64e-5, 1e-6, 1e-12
DECAY_K = math.exp(-0.5)
SLOT = 4096
RING = 4
NEG = -1.0e30


def constants():
    t = np.arange(P)
    ident = np.eye(P, dtype=np.float32)
    cum = np.zeros((2, P, 258), np.float32)
    s = t[:, None]
    q = t[None, :]
    mid = 63
    first = (s <= mid) * 1.0
    cum[0, :, 0:128] = (s <= q) * 1.0 - first
    cum[0, :, 128:256] = (s < q) * 1.0 - first
    cum[0, :, 256] = first[:, 0]
    cum[0, :, 257] = 1.0 - first[:, 0]
    last = (s >= P - 1 - mid) * 1.0
    cum[1, :, 0:128] = (s >= q) * 1.0 - last
    cum[1, :, 128:256] = (s > q) * 1.0 - last
    cum[1, :, 256] = last[:, 0]
    cum[1, :, 257] = 1.0 - last[:, 0]
    strict = np.stack([(s < q), (s > q)]).astype(np.float32)
    incl = np.stack([(s <= q), (s >= q)]).astype(np.float32)
    gram = np.concatenate([strict, incl, strict, incl], -1)
    lev = np.zeros((2, P, 7, P), np.float32)
    for i in range(7):
        n = 1 << i
        same = (s // (2 * n)) == (q // (2 * n))
        lev[0, :, i] = same & (s // n < q // n)
        lev[1, :, i] = same & (s // n > q // n)
    ones2 = np.kron(np.eye(2), np.ones((64, 64))).astype(np.float32)
    hsel = np.kron(np.eye(2), np.ones((64, 1))).astype(np.float32)
    pos = np.arange(T)
    inv = (np.float32(10000.0) ** (-np.arange(16, dtype=np.float32) / np.float32(16))).astype(np.float32)
    ang = np.stack([pos // 64, pos % 64], -1).astype(np.float32)[:, :, None] * inv
    rope = np.stack([np.cos(ang), np.sin(ang)], 1).reshape(NT, P, 64).transpose(1, 0, 2).astype(np.float32)
    before = np.zeros((P, NT, T), np.float32)
    for i in range(NT):
        before[:, i] = (np.arange(T)[None, :] < (i * P + t)[:, None])
    slots = np.tile(np.arange(CAP, dtype=np.float32), (P, 1))
    x = np.arange(896)[None, :] - 384
    rel = t[:, None] - x
    mult = np.zeros(rel.shape)
    for w, dil in ((128, 1), (512, 4), (2048, 16)):
        mult += (rel >= 0) & (rel <= w) & (rel % dil == 0)
    lnm = np.where(mult > 0, np.log(np.maximum(mult, 1)), NEG)
    sl = lambda n: 2.0 ** (-8.0 * np.arange(1, n + 1) / n)
    dil = np.stack([np.where(mult > 0, -a * rel + lnm, NEG) for a in sl(6)]).astype(np.float32)
    dif = np.stack([np.where(rel >= 0, -a * rel, NEG) for a in sl(4)]).astype(np.float32)
    bias = np.concatenate([dil, dif])
    sufneg = -(s >= q).astype(np.float32)
    sb = np.stack([sufneg, -np.ones((P, P), np.float32), (s < q).astype(np.float32)], 1)
    return {"k_ident": ident, "k_cum": cum, "k_gram": gram, "k_lev": lev, "k_ones2": ones2,
            "k_hsel": hsel, "k_rope": rope, "k_before": before, "k_slots": slots,
            "k_bias": np.ascontiguousarray(bias), "k_sb": np.ascontiguousarray(sb)}


class Marks:

    def __init__(self, known, final):
        self.known, self.now, self.final, self.sems = known, {}, final, {}

    def past(self, *key):
        lane, n = self.known.get(key, ("pe", 0))
        assert not self.final or key in self.known, key
        return self.sems[lane], n


class Lane:

    def __init__(self, name, engine, sem, marks):
        self.name, self.engine, self.sem, self.marks = name, engine, sem, marks
        self.wait_ge = engine.wait_ge
        self.n = 0

    def did(self, ins, *key):
        self.n += 1
        if key:
            self.marks.now[key] = (self.name, self.n)

    def name_last(self, *key):
        self.marks.now[key] = (self.name, self.n)

    def own(self):
        return self.sem, self.n


def build(nc, a, out, known, final, upto, debug):
    ctx = ExitStack()
    marks = Marks(known, final)
    with ctx:
        def sem(name):
            return ctx.enter_context(nc.semaphore(name))

        ARENA = 52992
        RING_WORDS = RING * SLOT
        arena_at = (nc.sbuf_base + 31) // 32 * 32
        ring = ctx.enter_context(nc.sbuf_tensor("ring", [P, RING_WORDS], F32))
        arena = ctx.enter_context(nc.sbuf_tensor("arena", [P, ARENA - RING_WORDS], F32))

        twins = {}

        def parts_of(name, off, words):
            if name not in twins:
                twins[name] = nc.alloc_sbuf_tensor_at(name, [P, words], F32R, offset=arena_at + 4 * off)
            t = twins[name]

            def view(at, *shape):
                assert off <= at and at + int(np.prod(shape)) <= off + words
                return shaped(t[:, at - off:at - off + int(np.prod(shape))], shape)
            return view
        banks = ctx.enter_context(nc.psum_tensor("banks", [P, 8, 512], F32))
        used = [0]

        def shaped(ap, shape):
            if len(shape) > 1:
                names = " ".join("abcde"[:len(shape)])
                ap = ap.rearrange(f"p ({names}) -> p {names}", **{k: v for k, v in zip("abcde", shape)})
            return ap

        def region(off, *shape):
            n = int(np.prod(shape))
            if off < RING_WORDS:
                assert off + n <= RING_WORDS, (off, shape)
                return shaped(ring[:, off:off + n], shape)
            assert off + n <= ARENA, (off, shape)
            return shaped(arena[:, off - RING_WORDS:off - RING_WORDS + n], shape)
        ring_r = parts_of("ring_r", 0, RING_WORDS)

        class Stack:
            def __init__(self, at, end=ARENA):
                self.at, self.end = at, end

            def take(self, *shape):
                r = region(self.at, *shape)
                self.at += int(np.prod(shape))
                assert self.at <= self.end, ("arena", self.at, self.end)
                return r

            def branch(self):
                return Stack(self.at, self.end)

        lanes = {}
        for name, eng in (("pe", nc.tensor), ("act", nc.scalar), ("dve", nc.vector), ("pool", nc.gpsimd),
                          ("sp", nc.sync)):
            s = sem(f"{name}_results")
            marks.sems[name] = s
            lanes[name] = Lane(name, eng, s, marks)
        pe, act, dve, pool = (lanes[n] for n in ("pe", "act", "dve", "pool"))
        ring_full = [sem(f"ring_full{i}") for i in range(RING)]
        small_in = [sem(f"small_in{i}") for i in range(40)]
        stored = sem("stored")
        scratch_io = sem("scratch_io")
        past = marks.past
        V, S, TE, G = nc.vector, nc.scalar, nc.tensor, nc.gpsimd
        views = {"final_x": None}

        def program(l_):
            me = l_
            n_loads, smalls, stages = [0], {}, []
            slot_fills = [0] * RING
            keep = Stack(RING * SLOT)

            def stream_many(parts):
                n = n_loads[0]
                n_loads[0] += 1
                at, views_ = (n % RING) * SLOT, []
                if me.name == "sp" and n >= RING:
                    me.wait_ge(*past("freed", n - RING))
                for shape, src in parts:
                    views_.append(region(at, *shape))
                    at += int(np.prod(shape))
                    if me.name == "sp":
                        me.engine.dma_start(views_[-1], src).then_inc(ring_full[n % RING], 16)
                slot_fills[n % RING] += 16 * len(parts)
                return (n, slot_fills[n % RING]), views_

            def stream(src, shape):
                n, v = stream_many([(shape, src)])
                return n, v[0]

            def hold_stream(after):
                if me.name == "sp":
                    for e in ("pe", "act", "dve", "pool"):
                        me.wait_ge(*past("end", after, e))

            def small(key, pairs, after=None):
                smalls[key] = (small_in[len(smalls)], 16 * len(pairs))
                if me.name == "sp":
                    if after:
                        for e in ("pe", "act", "dve", "pool"):
                            me.wait_ge(*past("end", after, e))
                    for dst, src in pairs:
                        me.engine.dma_start(dst, src).then_inc(smalls[key][0], 16)

            def stage(name, **fns):
                if me.name == "sp":
                    stages.append(name)
                    return
                fn = fns.get(me.name)
                if fn is not None:
                    if stages:
                        for other in ("pe", "act", "dve", "pool"):
                            me.wait_ge(*past("end", stages[-1], other))
                    fn(me)
                me.name_last("end", name, me.name)
                stages.append(name)

            def split(l, name, v, unit, depth):
                x_, lo, hi, n = unit
                if l is act:
                    if n is not None:
                        l.wait_ge(ring_full[n[0] % RING], n[1])
                    if v >= depth:
                        l.wait_ge(*past(name, "used", v - depth))
                    l.did(S.activation(hi, x_, ACT.Copy).then_inc(l.sem, 1), name, "hi", v)
                else:
                    l.wait_ge(*past(name, "hi", v))
                    l.did(V.tensor_tensor(lo, x_, hi, ALU.subtract).then_inc(l.sem, 1), name, "lo", v)

            def three(view, parts, start=True, stop=True):
                ms = []
                for (xh_, xl_), (yh_, yl_) in parts:
                    ms += [(xh_, yh_), (xh_, yl_), (xl_, yh_)]
                return [("m", view, x_, y_, start and i == 0, stop and i == len(ms) - 1) for i, (x_, y_) in enumerate(ms)]

            def products(name, groups, act_extra=None, dve_extra=None, pool_fn=None, units=(), depth=2, before=None):
                def split_ahead(l, g, done):
                    while done[0] < min(len(units), g.get("unit", -depth) + depth):
                        split(l, name, done[0], units[done[0]], depth)
                        done[0] += 1

                def f_pe(l):
                    for i, g in enumerate(groups):
                        if i >= 8:
                            l.wait_ge(*past(name, "read", i - 8))
                        for n in g.get("loads", ()):
                            l.wait_ge(ring_full[n[0] % RING], n[1])
                        for k in g.get("have", ()):
                            l.wait_ge(*smalls[k])
                        for key in g.get("after", ()):
                            l.wait_ge(*past(*key))
                        if "unit" in g:
                            l.wait_ge(*past(name, "lo", g["unit"]))
                        bank = banks[:, i % 8, :]
                        ms = g["mms"]
                        for j, m in enumerate(ms):
                            if m[0] == "t":
                                ins = TE.transpose(m[1](bank), m[2], m[3])
                            else:
                                ins = TE.matmul(m[1](bank), m[2], m[3], start=m[4], stop=m[5])
                        l.did(ins.then_inc(l.sem, 1), name, "made", i)
                        if "name" in g:
                            l.name_last(*g["name"])
                        if "unit" in g:
                            l.name_last(name, "used", g["unit"])
                        for n in g.get("loads", ()):
                            l.name_last("freed", n[0])
    
                def reader(who):
                    def f(l):
                        done = [0]
                        if before:
                            before(l)
                        for i, g in enumerate(groups):
                            split_ahead(l, g, done)
                            if g.get("first", (None,))[0] == who:
                                l.wait_ge(*past(name, "made", i))
                                g["first"][1](l, banks[:, i % 8, :])
                            if g["by"] == who:
                                l.wait_ge(*past(name, "made", i))
                                g["read"](l, banks[:, i % 8, :])
                                l.name_last(name, "read", i)
                        extra = act_extra if who == "act" else dve_extra
                        if extra:
                            extra(l)
                    return f
                stage(name, pe=f_pe, act=reader("act"), dve=reader("dve"), pool=pool_fn)
    
            def copy_out(dst, view=lambda b: b):
                def read(l, bank):
                    if l is act:
                        l.did(S.activation(dst, view(bank), ACT.Copy).then_inc(l.sem, 1))
                    else:
                        l.did(V.tensor_copy(dst, view(bank)).then_inc(l.sem, 1))
                return read
    
            def acc(view, pairs):
                n = len(pairs)
                return [("m", view, x, y, i == 0, i == n - 1) for i, (x, y) in enumerate(pairs)]
    
            def halves(i):
                return "act" if i % 2 else "dve"

            ident = keep.take(P)
            ones = keep.take(P)
            mixT_at = keep.at
            mixT = keep.take(8, T)
            small("const", [(ident, a["k_ident"])])
            gt1 = keep.take(D)
            gt2 = keep.take(D)
            modcol = keep.take(48, 2)
            stats = keep.take(256)
            base = keep.branch()

            m = base.branch()
            c16, sil, sg16 = m.take(P), m.take(16), m.take(16)
            modrow, brow = m.take(6 * D), m.take(6 * D)
            small("mod", [(c16[0:8, :], a["c"].rearrange("o (k p) -> (o k) p", p=P)),
                          (c16[8:16, :], a["c_ctx"].rearrange("(k p) -> k p", p=P)),
                          (brow[0:1, :], a["b_ada"]), (brow[1:2, :], a["b_ada"])])

            def silu_c_read(l, bank):
                l.did(S.activation(sg16, bank[:, 0:16], ACT.Sigmoid).then_inc(l.sem, 1), "silu_c")

            def silu_c(l):
                l.wait_ge(*past("silu_c"))
                l.did(V.tensor_tensor(sil, banks[:, 0, 0:16], sg16, ALU.mult).then_inc(l.sem, 1))

            def fill_ones(l):
                l.did(G.memset(ones, 1.0).then_inc(l.sem, 1))
            products("c_T", [{"have": ("mod", "const"), "by": "act", "read": silu_c_read,
                              "mms": [("t", lambda b: b[:, 0:16], c16[0:16, :], ident[0:16, 0:16])]}],
                     dve_extra=silu_c, pool_fn=fill_ones)
            silv = sil.rearrange("p (v k) -> p k v", k=KD)
            w_ada = a["w_ada"][0].rearrange("(k p) n -> p k n", p=P)
            groups = []
            for n in range(12):
                ln, w = stream(w_ada[:, :, n * 512:(n + 1) * 512], (KD, 512))
                cs = slice(n * 512, (n + 1) * 512)

                def read(l, bank, cs=cs):
                    l.did(V.tensor_tensor(modrow[0:2, cs], bank[0:2, :], brow[0:2, cs], ALU.add).then_inc(l.sem, 1))
                groups.append({"loads": [ln], "by": "dve", "read": read,
                               "mms": acc(lambda b: b[0:2, :], [(silv[:, k, :], w[:, k, :]) for k in range(KD)])})
            products("mod_rows", groups)

            def modcol_read(l, bank):
                l.did(V.tensor_copy(modcol, bank[:, 0:96].rearrange("p (a b) -> p a b", b=2)).then_inc(l.sem, 1))
                l.wait_ge(*l.own())
                for j in (8, 32):
                    l.did(V.tensor_scalar(modcol[:, j:j + 8, :], modcol[:, j:j + 8, :], 1.0, None, ALU.add).then_inc(l.sem, 1))
            groups = [{"by": "dve", "read": modcol_read,
                       "mms": [("t", (lambda b, j=j: b[:, 2 * j:2 * j + 2]), modrow[0:2, j * P:(j + 1) * P],
                                ident[0:2, 0:2]) for j in range(48)]}]
            for dst, j in ((gt1, 2), (gt2, 5)):
                for hf in range(2):
                    groups.append({"by": "act", "read": copy_out(dst[:, hf * 512:(hf + 1) * 512]),
                                   "mms": acc(lambda b: b, [(ones[0:1, :], modrow[0:1, j * D + hf * 512:j * D + hf * 512 + 512])])})
            products("mod_cols", groups)

            def norm_stage(name, src, dst, tiles, need, affine=None, into=None):
                st = stats[:, 0:tiles * 12].rearrange("p (a b c) -> p a b c", b=2, c=6)
                mv = stats[:, 80:80 + 2 * tiles].rearrange("p (a b) -> p a b", b=2)
                sd = stats[:, 100:100 + tiles]
                rs = stats[:, 110:110 + tiles]

                def f_dve(l):
                    for k in need:
                        l.wait_ge(*smalls[k])
                    for i in range(tiles):
                        for hf in range(2):
                            l.did(V.bn_stats(st[:, i, hf, :], src(i)[:, hf * 512:(hf + 1) * 512]).then_inc(l.sem, 1))
                    l.wait_ge(*l.own())
                    for i in range(tiles):
                        l.did(V.bn_aggr(mv[:, i, :], st[:, i, :, :]).then_inc(l.sem, 1))
                    l.wait_ge(*l.own())
                    l.did(V.tensor_scalar(sd, mv[:, :, 1], LN_EPS, None, ALU.add).then_inc(l.sem, 1), name, "var")
                    l.wait_ge(*past(name, "sd"))
                    l.did(V.reciprocal(rs, rs).then_inc(l.sem, 1))
                    l.wait_ge(*l.own())
                    for i in range(tiles):
                        l.did(V.tensor_scalar(dst(i), src(i), mv[:, i, 0:1], rs[:, i:i + 1], ALU.subtract, ALU.mult).then_inc(l.sem, 1))
                    if affine:
                        g, b = affine
                        l.wait_ge(*l.own())
                        for i in range(tiles):
                            l.did(V.tensor_tensor(dst(i), dst(i), g, ALU.mult).then_inc(l.sem, 1), name, "gained", i)

                def f_act(l):
                    l.wait_ge(*past(name, "var"))
                    l.did(S.activation(rs, sd, ACT.Sqrt).then_inc(l.sem, 1), name, "sd")

                def f_pool(l):
                    if affine:
                        for i in range(tiles):
                            l.wait_ge(*past(name, "gained", i))
                            l.did(G.tensor_tensor(dst(i), dst(i), affine[1], ALU.add).then_inc(l.sem, 1))
                stage(name, dve=f_dve, act=f_act, pool=f_pool)

            def transpose_groups(src, dst_of, n_tiles, tile0, nk, col=None, width=P):
                gs = []
                for k in range(nk):
                    def read(l, bank, k=k):
                        v = bank[:, 0:n_tiles * P]
                        if col is None:
                            if l is act:
                                l.did(S.activation(dst_of(k), v, ACT.Copy).then_inc(l.sem, 1))
                            else:
                                l.did(V.tensor_copy(dst_of(k), v).then_inc(l.sem, 1))
                        else:
                            sc, sh = col(k)
                            if l is act:
                                l.did(S.activation(dst_of(k), v, ACT.Identity, bias=sh, scale=sc).then_inc(l.sem, 1))
                            else:
                                l.did(V.tensor_scalar(dst_of(k), v, sc, sh, ALU.mult, ALU.add).then_inc(l.sem, 1))
                    gs.append({"by": halves(k), "read": read, "mms": [
                        ("t", (lambda b, i=i: b[:, i * P:(i + 1) * P]), src(tile0 + i)[:, k * P:(k + 1) * P], ident)
                        for i in range(n_tiles)]})
                return gs

            m = base.branch()
            hT = m.take(KD, NALL)
            xc = m.take(NTA, D)
            xn = m.take(NTA, D)
            small("x", [(xc[:, 0:NT, :], a["x"][0].rearrange("(t p) n -> p t n", p=P)),
                        (xc[:, NT:NTA, :], a["ctx"][0].rearrange("(t p) n -> p t n", p=P))], after="mod_cols")
            norm_stage("norm1", lambda i: xc[:, i, :], lambda i: xn[:, i, :], NTA, ["x"])
            products("h_T",
                     transpose_groups(lambda i: xn[:, i, :], lambda k: hT[:, k, 0:T], NT, 0, KD,
                                      lambda k: (modcol[:, 8 + k, 0:1], modcol[:, k, 0:1])) +
                     transpose_groups(lambda i: xn[:, i, :], lambda k: hT[:, k, T:NALL], NTC, NT, KD,
                                      lambda k: (modcol[:, 8 + k, 1:2], modcol[:, k, 1:2])))

            m = base.branch()
            hT = m.take(KD, NALL)
            cols = m.take(64)
            sft = m.take(NRW, NALL)
            qkv = m.take(NT, 768)
            kvc = m.take(NTC, 256)
            after_proj = m.branch()
            pb = m.take(2, 772)
            tmp = m.take(2, NALL)
            omu, hmu = m.take(NRW), m.take(NRW)
            colrow = m.take(64)
            rows = m.take(P)
            vec = lambda ap: ap.rearrange("(k p) -> k p", p=P)
            small("cols", [(rows[0:14, :], vec(a["tshift_mu"][0])), (rows[14:18, :], vec(a["k_k"][0])),
                           (rows[18:22, :], vec(a["k_a"][0])),
                           (rows[22:26, :], a["r_k"][0].rearrange("(k h) n -> k (h n)", h=2)),
                           (rows[26:34, :], a["iclr_a0"][0].rearrange("d (k p) -> (d k) p", p=P))], after="h_T")

            def pad_zero(l):
                for i in range(2):
                    for c in (0, 513, 514, 771):
                        l.did(G.memset(pb[:, i, c:c + 1], 0.0).then_inc(l.sem, 1))

            def cols_read(l, bank):
                l.did(V.tensor_copy(cols[:, 0:34], bank[:, 0:34]).then_inc(l.sem, 1))
                l.wait_ge(*l.own())
                l.did(V.tensor_scalar(omu, cols[:, 0:NRW], -1.0, 1.0, ALU.mult, ALU.add).then_inc(l.sem, 1))
                l.did(V.tensor_scalar(hmu, cols[:, 0:NRW], 0.5, None, ALU.mult).then_inc(l.sem, 1))
                l.wait_ge(*l.own())
            products("cols", [{"have": ("cols",), "by": "dve", "read": cols_read,
                               "mms": [("t", lambda b: b[:, 0:34], rows[0:34, :], ident[0:34, 0:34])]}],
                     pool_fn=pad_zero)
            w_in = a["w_in"][0].rearrange("(k p) n -> p k n", p=P)
            ws = [stream(w_in[:, :, s * 512:(s + 1) * 512], (KD, 512)) for s in range(5)]
            groups = []
            for c0, c1, sl in ((0, 512, 0), (512, 768, 1)):
                for t in range(NTA if c0 else NT):
                    if t < NT:
                        dst = qkv[:, t, c0:c1]
                    else:
                        dst = kvc[:, t - NT, :]
                    w = ws[sl][1][:, :, c0 - 512 * sl:c1 - 512 * sl]
                    groups.append({"loads": [ws[sl][0]], "by": "act", "read": copy_out(dst, lambda b, n=c1 - c0: b[:, 0:n]),
                                   "mms": acc(lambda b, n=c1 - c0: b[:, 0:n],
                                              [(hT[:, k, t * P:(t + 1) * P], w[:, k, :]) for k in range(KD)])})
            for j in range(NRW):
                c = 768 + j * P
                sl = c // 512
                w = ws[sl][1][:, :, c - 512 * sl:c - 512 * sl + P]
                for t0, t1, o in ((0, T, 1), (T, NALL, 3)):
                    def read(l, bank, j=j, t0=t0, t1=t1, o=o):
                        if j >= 2 and t0 == 0:
                            l.wait_ge(*past("shifted", j - 2))
                        l.did(S.activation(pb[:, j % 2, t0 + o:t1 + o], bank[:, 0:t1 - t0], ACT.Copy).then_inc(l.sem, 1),
                              "projected", j, t0)
                    groups.append({"loads": [ws[sl][0]], "by": "act", "read": read,
                                   "mms": acc(lambda b, n=t1 - t0: b[:, 0:n],
                                              [(w[:, k, :], hT[:, k, t0:t1]) for k in range(KD)])})

            def shift(l):
                for j in range(NRW):
                    l.wait_ge(*past("projected", j, T))
                    p, tt = pb[:, j % 2, :], tmp[:, j % 2, :]
                    for t0, t1, o in ((0, T, 1), (T, NALL, 3)):
                        l.did(V.tensor_tensor(tt[:, t0:t1], p[:, t0 + o - 1:t1 + o - 1], p[:, t0 + o + 1:t1 + o + 1], ALU.add).then_inc(l.sem, 1))
                    l.wait_ge(*l.own())
                    l.did(V.tensor_scalar(tt, tt, hmu[:, j:j + 1], None, ALU.mult).then_inc(l.sem, 1))
                    l.wait_ge(*l.own())
                    for t0, t1, o in ((0, T, 1), (T, NALL, 3)):
                        l.did(V.scalar_tensor_tensor(out=sft[:, j, t0:t1], in0=p[:, t0 + o:t1 + o], scalar=omu[:, j:j + 1],
                                                     in1=tt[:, t0:t1], op0=ALU.mult, op1=ALU.add).then_inc(l.sem, 1), "shifted", j)
            products("w_in", groups, dve_extra=shift)

            pass

            def attention(name, heads, width, score, val, dst, scale, bufs, bias=None, lam=None, need=()):
                units = [(i, h, t) for i, h in enumerate(heads) for t in range(NT)]
                sbs, pt, st = bufs
                sb = lambda u: sbs[u % 3]
                lag = 2
                nset = 2 if lam is not None else 1
                full = width(0) == width(NT - 1)
                n_key = [width(t) // P for t in range(NT)]

                def sbank(u, s):
                    if nset == 1 and not full:
                        return u % 3
                    return (u % 2) * 2 + s
                tb_of, cnt = {}, 0
                for u, (i, h, t) in enumerate(units):
                    for g in range((n_key[t] + 3) // 4):
                        tb_of[u, g] = (4 + cnt % 3, cnt)
                        cnt += 1
                by_cnt = {c: ug for ug, (_, c) in tb_of.items()}

                def sc_view(u, s, w):
                    if w > 512:
                        return banks[:, sbank(u, 0):sbank(u, 0) + 2, :].rearrange("p a b -> p (a b)")[:, 0:w]
                    return banks[:, sbank(u, s), 0:w]

                def f_pe(l):
                    for k in need:
                        l.wait_ge(*smalls[k])

                    def turn(u):
                        i, h, t = units[u]
                        l.wait_ge(*past(name, "P", u))
                        for g in range((n_key[t] + 3) // 4):
                            b, c = tb_of[u, g]
                            if c >= 3:
                                l.wait_ge(*past(name, "T", *by_cnt[c - 3]))
                            for j in range(4 * g, min(4 * g + 4, n_key[t])):
                                ins = TE.transpose(banks[:, b, (j - 4 * g) * P:(j - 4 * g + 1) * P],
                                                   sb(u)[:, j * P:(j + 1) * P], ident)
                            l.did(ins.then_inc(l.sem, 1), name, "turned", u, g)
                        if t == NT - 1:
                            if i >= 1:
                                l.wait_ge(*past(name, "out", i - 1))
                            for g in range((n_key[t] + 3) // 4):
                                l.wait_ge(*past(name, "T", u, g))
                            po = HD * (h % 2)
                            for j in range(n_key[t]):
                                q0 = 0 if full else j * P
                                ins = TE.matmul(banks[po:po + HD, 7, q0:T], val(h, j), pt[:, i % 2, j, q0:T],
                                                start=(j == 0), stop=(j == n_key[t] - 1))
                            l.did(ins.then_inc(l.sem, 1), name, "pv", i)
                    ahead = 3 if nset == 1 and not full else 2
                    for u in range(len(units) + lag):
                        if u < len(units):
                            i, h, t = units[u]
                            if u >= ahead:
                                l.wait_ge(*past(name, "E", u - ahead))
                            for s, pieces in enumerate(score(h, t)):
                                w = width(t)
                                for q, k, c, n in pieces:
                                    ins = TE.matmul(sc_view(u, s, w)[:, c:c + n], q, k, start=True, stop=True)
                            l.did(ins.then_inc(l.sem, 1), name, "S", u)
                        if u >= lag:
                            turn(u - lag)

                def f_dve(l):
                    def finish(u):
                        i, h, t = units[u]
                        w = width(t)
                        l.wait_ge(*past(name, "E", u))
                        c = st[:, u % 3, :]
                        l.did(V.reciprocal(c[:, 4:4 + nset], c[:, 2:2 + nset]).then_inc(l.sem, 1))
                        l.wait_ge(*l.own())
                        p1 = sb(u)[:, 0:w]
                        if nset == 2:
                            p2 = sb(u)[:, 512:512 + w]
                            l.did(V.tensor_tensor(c[:, 5:6], c[:, 5:6], lam, ALU.mult).then_inc(l.sem, 1))
                            l.did(V.tensor_scalar(p1, p1, c[:, 4:5], None, ALU.mult).then_inc(l.sem, 1))
                            l.wait_ge(*l.own())
                            l.did(V.scalar_tensor_tensor(out=p1, in0=p2, scalar=c[:, 5:6], in1=p1,
                                                         op0=ALU.mult, op1=ALU.add).then_inc(l.sem, 1), name, "P", u)
                        else:
                            l.did(V.tensor_scalar(p1, p1, c[:, 4:5], None, ALU.mult).then_inc(l.sem, 1), name, "P", u)
                    for u in range(len(units) + 1):
                        if u < len(units):
                            i, h, t = units[u]
                            w = width(t)
                            l.wait_ge(*past(name, "S", u))
                            c = st[:, u % 3, :]
                            if u >= 3:
                                l.wait_ge(*past(name, "turned", u - 3, (n_key[units[u - 3][2]] + 3) // 4 - 1))
                            for s in range(nset):
                                v = sc_view(u, s, w)
                                if bias is not None:
                                    x = sb(u)[:, 512 * s:512 * s + w]
                                    l.did(V.scalar_tensor_tensor(out=x, in0=v, scalar=scale, in1=bias(h, t),
                                                                 op0=ALU.mult, op1=ALU.add).then_inc(l.sem, 1))
                                    l.wait_ge(*l.own())
                                    v = x
                                l.did(V.reduce_max(c[:, s:s + 1], v, axis=AX.X).then_inc(l.sem, 1))
                            l.wait_ge(*l.own())
                            l.did(V.tensor_scalar(c[:, 0:nset], c[:, 0:nset], -1.0 if bias is not None else -scale,
                                                  None, ALU.mult).then_inc(l.sem, 1), name, "max", u)
                        if u >= 1:
                            finish(u - 1)

                def f_act(l):
                    def evac(u):
                        i, h, t = units[u]
                        for g in range((n_key[t] + 3) // 4):
                            l.wait_ge(*past(name, "turned", u, g))
                            if i >= 2:
                                l.wait_ge(*past(name, "pv", i - 2))
                            m_ = min(4, n_key[t] - 4 * g)
                            l.did(S.activation(pt[:, i % 2, 4 * g:4 * g + m_, t * P:(t + 1) * P],
                                               banks[:, tb_of[u, g][0], 0:m_ * P].rearrange("p (a b) -> p a b", b=P),
                                               ACT.Copy).then_inc(l.sem, 1), name, "T", u, g)
                        if t == NT - 1:
                            l.wait_ge(*past(name, "pv", i))
                            po = HD * (h % 2)
                            l.did(S.activation(dst(h), banks[po:po + HD, 7, :], ACT.Copy).then_inc(l.sem, 1), name, "out", i)
                    for u in range(len(units) + lag):
                        if u < len(units):
                            i, h, t = units[u]
                            w = width(t)
                            l.wait_ge(*past(name, "max", u))
                            c = st[:, u % 3, :]
                            for s in range(nset):
                                src = sb(u)[:, 512 * s:512 * s + w] if bias is not None else sc_view(u, s, w)
                                l.did(S.activation(sb(u)[:, 512 * s:512 * s + w], src, ACT.Exp,
                                                   bias=c[:, s:s + 1], scale=1.0 if bias is not None else scale,
                                                   accum_out=c[:, 2 + s:3 + s]).then_inc(l.sem, 1))
                            l.name_last(name, "E", u)
                        if u >= lag:
                            evac(u - lag)
                stage(name, pe=f_pe, act=f_act, dve=f_dve)

            def part_two():
                hole = Stack(base.at, base.at + KD * NALL)
                m2 = after_proj.branch()
                sb_at = m2.at
                gain = m2.take(640)
                rope = m2.take(NT, 64)
                kdup = m2.take(NTA, 2, 128)
                rms = m2.take(3, 44)
                qz = m2.take(NH, T)
                kT = m2.take(2, NALL)
                sbs = [region(sb_at + i * NALL, NALL) for i in range(3)]
                st = m2.take(3, 8)
                ptb = hole.branch().take(2, NTA, T)
                hh = hole.branch()
                sq = hh.take(NT, 640)
                sqc = hh.take(NTC, 128)
                r1, r2, r3, r4 = (hh.take(10, 2, 16) for _ in range(4))
                gs = [(gain[:, h * HD:(h + 1) * HD], a["q_gain"].to_broadcast([P, HD])) for h in range(NH)]
                gs += [(gain[:, h * HD:(h + 1) * HD], a["k_gain"].to_broadcast([P, HD])) for h in range(NH, NH + NKV)]
                small("qk", gs + [(rope, a["k_rope"])], after="w_in")
                heads10 = lambda ap: ap.rearrange("p (h n) -> p h n", n=HD)

                def qk_dve(l):
                    l.wait_ge(*smalls["qk"])
                    for t in range(NT):
                        l.did(V.tensor_tensor(sq[:, t, :], qkv[:, t, 0:640], qkv[:, t, 0:640], ALU.mult).then_inc(l.sem, 1))
                    for t in range(NTC):
                        l.did(V.tensor_tensor(sqc[:, t, :], kvc[:, t, 0:128], kvc[:, t, 0:128], ALU.mult).then_inc(l.sem, 1))
                    l.wait_ge(*l.own())
                    for t in range(NT):
                        l.did(V.reduce_sum(rms[:, 0, 10 * t:10 * t + 10], heads10(sq[:, t, :]), axis=AX.X).then_inc(l.sem, 1))
                    l.did(V.reduce_sum(rms[:, 0, 40:44], heads10(sqc.rearrange("p a b -> p (a b)")), axis=AX.X).then_inc(l.sem, 1))
                    l.wait_ge(*l.own())
                    l.did(V.tensor_scalar(rms[:, 1, :], rms[:, 0, :], 1.0 / HD, RMS_EPS, ALU.mult, ALU.add).then_inc(l.sem, 1), "qk_var")
                    l.wait_ge(*past("qk_sd"))
                    l.did(V.reciprocal(rms[:, 0, :], rms[:, 2, :]).then_inc(l.sem, 1))
                    l.wait_ge(*l.own())
                    for t in range(NT):
                        v = heads10(qkv[:, t, 0:640])
                        l.did(V.tensor_tensor(v, v, rms[:, 0, 10 * t:10 * t + 10].unsqueeze(2).to_broadcast([P, 10, HD]), ALU.mult).then_inc(l.sem, 1))
                    for t in range(NTC):
                        v = heads10(kvc[:, t, 0:128])
                        l.did(V.tensor_tensor(v, v, rms[:, 0, 40 + 2 * t:42 + 2 * t].unsqueeze(2).to_broadcast([P, 2, HD]), ALU.mult).then_inc(l.sem, 1))
                    l.wait_ge(*l.own())
                    for t in range(NT):
                        l.did(V.tensor_tensor(qkv[:, t, 0:640], qkv[:, t, 0:640], gain, ALU.mult).then_inc(l.sem, 1))
                    for t in range(NTC):
                        l.did(V.tensor_tensor(kvc[:, t, 0:128], kvc[:, t, 0:128], gain[:, 512:640], ALU.mult).then_inc(l.sem, 1))
                    l.wait_ge(*l.own())
                    for t in range(NT):
                        v = qkv[:, t, 0:640].rearrange("p (h x y e) -> p h x y e", h=10, x=2, y=2)
                        t1, t2 = v[:, :, :, 0, :], v[:, :, :, 1, :]
                        tab = rope[:, t, :].rearrange("p (y x e) -> p y x e", y=2, x=2)
                        cs = tab[:, 0].unsqueeze(1).to_broadcast([P, 10, 2, 16])
                        sn = tab[:, 1].unsqueeze(1).to_broadcast([P, 10, 2, 16])
                        l.did(V.tensor_tensor(r1, t1, cs, ALU.mult).then_inc(l.sem, 1))
                        l.did(V.tensor_tensor(r2, t2, sn, ALU.mult).then_inc(l.sem, 1))
                        l.did(V.tensor_tensor(r3, t2, cs, ALU.mult).then_inc(l.sem, 1))
                        l.did(V.tensor_tensor(r4, t1, sn, ALU.mult).then_inc(l.sem, 1))
                        l.wait_ge(*l.own())
                        l.did(V.tensor_tensor(t1, r1, r2, ALU.subtract).then_inc(l.sem, 1))
                        l.did(V.tensor_tensor(t2, r3, r4, ALU.add).then_inc(l.sem, 1))
                        l.wait_ge(*l.own())
                    for t in range(NTA):
                        src = qkv[:, t, 512:640] if t < NT else kvc[:, t - NT, 0:128]
                        for e in range(2):
                            l.did(V.tensor_copy(kdup[:, t, :, e * HD:(e + 1) * HD], heads10(src)).then_inc(l.sem, 1))

                def qk_act(l):
                    l.wait_ge(*past("qk_var"))
                    l.did(S.activation(rms[:, 2, :], rms[:, 1, :], ACT.Sqrt).then_inc(l.sem, 1), "qk_sd")
                stage("qk_norm", dve=qk_dve, act=qk_act)
                gs = []
                for k in range(4):
                    def read(l, bank, k=k):
                        for h in range(2):
                            hs = slice(64 * h, 64 * h + 64)
                            copy_out(qz[hs, 2 * k + h, :], lambda b, hs=hs: b[hs, :])(l, bank)
                    gs.append({"by": halves(k), "read": read, "mms": [
                        ("t", (lambda b, t=t: b[:, t * P:(t + 1) * P]), qkv[:, t, k * P:(k + 1) * P], ident)
                        for t in range(NT)]})

                def zero_q(l):
                    for h in range(NH):
                        z = 64 - 64 * (h % 2)
                        l.did(G.memset(qz[z:z + 64, h, :], 0.0).then_inc(l.sem, 1))
                gs += transpose_groups(lambda t: kdup[:, t].rearrange("p a b -> p (a b)"), lambda k: kT[:, k, 0:T], NT, 0, 2)
                gs += transpose_groups(lambda t: kdup[:, t].rearrange("p a b -> p (a b)"), lambda k: kT[:, k, T:NALL], NTC, NT, 2)
                products("qk_T", gs, pool_fn=zero_q)

                def score(h, t):
                    q = qz[:, h, t * P:(t + 1) * P]
                    g = h // (NH // NKV)
                    return [[(q, kT[:, g, 0:512], 0, 512), (q, kT[:, g, 512:768], 512, 256)]]

                def val(h, j):
                    g = h // (NH // NKV)
                    src = qkv[:, j, 640:768] if j < NT else kvc[:, j - NT, 128:256]
                    return src[:, g * HD:(g + 1) * HD]
                attention("attend", list(range(NH)), lambda t: NALL, score, val,
                          lambda h: mixT[HD * (h % 2):HD * (h % 2) + HD, h // 2, :], HD ** -0.5, (sbs, ptb, st))
                views.update(kT=kT, mixA=mixT[:, 0:4, :])

            wos = []

            def part_three():
                low = Stack(0, RING * SLOT)
                hole = Stack(base.at, base.at + KD * NALL)
                sft_at = base.at + KD * NALL + 64
                high = after_proj.branch()
                high.at -= NT * 768 + NTC * 256
                R, K_, V_ = 0, 4, 8
                CELLS = 8
                masks = low.take(2, 512)
                levm = low.take(2, 7, P)
                cum = low.take(2, 258)
                ones2 = low.take(P)
                hsel = low.take(2)
                w0 = low.take(2, 512)
                upd, upi = low.take(2, 512), low.take(2, 512)
                big = low.branch()
                vtm = hole.take(NTA, 512)
                ytm = high.take(NT, 512)
                bonus = high.take(NT, 8)
                kkn = high.take(4, NALL)
                RA = high.take(CELLS, 256)
                XT = high.take(CELLS, 2, 256)
                ends = high.take(2, 8)
                end_old = high.take(2, 4)
                hop = high.take(2, 4)
                vdead = Stack(sft_at + V_ * NALL, sft_at + 12 * NALL)
                BKt = vdead.take(CELLS, 2, P)
                state = vdead.take(2, 4, P)
                Am = region(RING * SLOT + 2 * P + 4 * T, CELLS, 2, P)
                wu = region(RING * SLOT + 2 * P + 4 * T, 2, 2, 512)
                cells_from = hole.at
                cell_at = [hole.take(512) for _ in range(6)] + [high.take(512) for _ in range(2)]
                BKz = lambda q, h: cell_at[q][:, h * 256:(h + 1) * 256]
                P1 = lambda q: cell_at[q][:, 0:256]
                Al = lambda q: cell_at[q][:, 256:512]
                Gm = big.take(CELLS, 2, 512)
                pre = Stack(big.at - CELLS * 2 * 512)
                sw, aa = pre.take(2, 512), pre.take(2, 4, P)
                kd, bb = pre.take(2, 4, P), pre.take(2, 4, P)
                E1, Em, E0 = pre.take(2, 4, P), pre.take(2, 4, P), pre.take(2, 4, P)
                order = [[4, 5, 0, 1, 2, 3], [5, 4, 3, 2, 1, 0]]
                small("rwkv", [(masks, a["k_gram"].rearrange("d p n -> p d n")),
                               (levm, a["k_lev"].rearrange("d p l n -> p d l n")),
                               (cum, a["k_cum"].rearrange("d p n -> p d n")),
                               (ones2, a["k_ones2"]), (hsel, a["k_hsel"]),
                               (w0[:, 0, :], a["decay_w0"][0, 0:1, :].to_broadcast([P, 512])),
                               (w0[:, 1, :], a["decay_w0"][0, 1:2, :].to_broadcast([P, 512])),
                               (upd[0:64], a["decay_up"][0].rearrange("d p n -> p d n")),
                               (upi[64:128], a["iclr_up"][0].rearrange("d p n -> p d n"))], after="attend")
                rkx = region(cells_from, 4, T)
                sq = region(big.at - CELLS * 2 * 512, 4, NALL)

                def gates(l):
                    l.did(S.activation(sft[0:64, 12, :], sft[0:64, 12, :], ACT.Tanh).then_inc(l.sem, 1))
                    l.did(S.activation(sft[:, 13, 0:T], sft[:, 13, 0:T], ACT.Sigmoid).then_inc(l.sem, 1))

                def gates_dve(l):
                    for j in range(4):
                        l.did(V.scalar_tensor_tensor(out=rkx[:, j, :], in0=sft[:, R + j, 0:T], scalar=cols[:, 22 + j:23 + j],
                                                     in1=sft[:, K_ + j, 0:T], op0=ALU.mult, op1=ALU.mult).then_inc(l.sem, 1))
                        l.did(V.tensor_scalar(kkn[:, j, :], sft[:, K_ + j, :], cols[:, 14 + j:15 + j], None, ALU.mult)
                              .then_inc(l.sem, 1))
                    l.wait_ge(*l.own())
                    l.did(V.tensor_tensor(sq, kkn, kkn, ALU.mult).then_inc(l.sem, 1))

                def gates_pool(l):
                    l.did(G.memset(upd[64:128], 0.0).then_inc(l.sem, 1))
                    l.did(G.memset(upi[0:64], 0.0).then_inc(l.sem, 1))
                stage("rwkv_gates", act=gates, dve=gates_dve, pool=gates_pool)
                gs = []
                for j in range(4):
                    for t0, t1 in ((0, T), (T, NALL)):
                        def read(l, bank, j=j, t0=t0, t1=t1):
                            l.did(S.activation(sq[:, j, t0:t1], bank[:, 0:t1 - t0], ACT.Sqrt).then_inc(l.sem, 1))
                        gs.append({"by": "act", "read": read, "have": ("rwkv",),
                                   "mms": acc(lambda b, n=t1 - t0: b[:, 0:n], [(ones2, sq[:, j, t0:t1])])})
                for t in range(NTA):
                    gs.append({"by": "dve", "read": copy_out(vtm[:, t, :]),
                               "mms": [("t", (lambda b, j=j: b[:, j * P:(j + 1) * P]),
                                        sft[:, V_ + j, t * P:(t + 1) * P], ident) for j in range(4)]})
                for t in range(NT):
                    gs.append({"by": "dve", "read": copy_out(bonus[:, t, :], lambda b: b[:, 0:8]),
                               "mms": [("m", (lambda b, j=j: b[:, 2 * j:2 * j + 2]), rkx[:, j, t * P:(t + 1) * P],
                                        hsel, True, True) for j in range(4)]})

                def unit_kk(l):
                    l.wait_ge(*past("rwkv_tm", "read", 7))
                    l.did(V.tensor_scalar(sq, sq, L2_EPS, None, ALU.max).then_inc(l.sem, 1))
                    l.wait_ge(*l.own())
                    l.did(V.reciprocal(sq, sq).then_inc(l.sem, 1))
                    l.wait_ge(*l.own())
                    l.did(V.tensor_tensor(kkn, kkn, sq, ALU.mult).then_inc(l.sem, 1))
                products("rwkv_tm", gs, dve_extra=unit_kk)

                lm = lambda dd, i: levm[:, dd, i, :].unsqueeze(1).to_broadcast([P, 2, P])
                idb = ident.unsqueeze(1).to_broadcast([P, 2, P])
                col4 = lambda c: cols[:, c:c + 4].unsqueeze(2).to_broadcast([P, 4, P])
                four = lambda ap: ap.rearrange("p (j n) -> p j n", j=4)

                def step(n):
                    nm = f"rwkv{n}"
                    tok = [slice(order[d][n] * P, order[d][n] * P + P) for d in range(2)]

                    gs = []
                    for d in range(2):
                        def read(l, bank, d=d):
                            l.did(V.tensor_tensor(sw[:, d, :], bank, w0[:, d, :], ALU.add).then_inc(l.sem, 1), nm, "w", d)

                        def read_a(l, bank, d=d):
                            l.did(V.tensor_tensor(aa[:, d], four(bank), col4(26 + 4 * d), ALU.add).then_inc(l.sem, 1), nm, "a_in", d)
                        gs.append({"by": "dve", "read": read, "mms": acc(lambda b: b, [(sft[:, 12, tok[d]], upd[:, d, :])])})
                        gs.append({"by": "dve", "read": read_a, "mms": [
                            ("m", (lambda b, j=j: b[:, j * P:(j + 1) * P]), upi[:, d, j * P:(j + 1) * P], sft[:, 12, tok[d]],
                             True, True) for j in range(4)]})

                    def act_x(l):
                        for d in range(2):
                            l.wait_ge(*past(nm, "w", d))
                            l.did(S.activation(sw[:, d, :], sw[:, d, :], ACT.Sigmoid).then_inc(l.sem, 1), nm, "sw", d)
                            l.wait_ge(*past(nm, "a_in", d))
                            l.did(S.activation(aa[:, d], aa[:, d], ACT.Sigmoid).then_inc(l.sem, 1), nm, "a", d)

                    def zero_pool(l):
                        for q in range(CELLS):
                            for h in range(2):
                                l.did(G.memset(BKz(q, h)[64 - 64 * h:128 - 64 * h, :], 0.0).then_inc(l.sem, 1))

                    def dve_x(l):
                        for d in range(2):
                            l.wait_ge(*past(nm, "a", d))
                            l.did(V.scalar_tensor_tensor(out=kd[:, d], in0=aa[:, d], scalar=-1.0, in1=col4(18), op0=ALU.add,
                                                         op1=ALU.mult).then_inc(l.sem, 1))
                            l.did(V.tensor_tensor(bb[:, d], kkn[:, :, tok[d]], aa[:, d], ALU.mult).then_inc(l.sem, 1))
                            l.wait_ge(*l.own())
                            l.did(V.scalar_tensor_tensor(out=kd[:, d], in0=kd[:, d], scalar=1.0, in1=sft[:, K_:K_ + 4, tok[d]],
                                                         op0=ALU.add, op1=ALU.mult).then_inc(l.sem, 1))
                    products(nm + "in", gs, act_extra=act_x, dve_extra=dve_x, pool_fn=zero_pool)

                    gs = []
                    for d in range(2):
                        def read1(l, bank, d=d):
                            l.did(S.activation(E1[:, d], four(bank), ACT.Exp, scale=-DECAY_K).then_inc(l.sem, 1))
                            l.did(S.activation(Em[:, d], four(bank), ACT.Exp, scale=DECAY_K).then_inc(l.sem, 1))

                        def read0(l, bank, d=d):
                            l.did(S.activation(E0[:, d], four(bank), ACT.Exp, scale=-DECAY_K).then_inc(l.sem, 1), nm, "exps", d)

                        def read_e(l, bank, d=d):
                            l.did(S.activation(ends[:, d, :], bank[:, 0:8], ACT.Exp, scale=-DECAY_K).then_inc(l.sem, 1))
                        for c0, w, read in ((0, P, read1), (P, P, read0), (256, 2, read_e)):
                            gs.append({"by": "act", "read": read, "mms": [
                                ("m", (lambda b, j=j, w=w: b[:, j * w:(j + 1) * w]), sw[:, d, j * P:(j + 1) * P],
                                 cum[:, d, c0:c0 + w], True, True) for j in range(4)]})

                    def dve_y(l):
                        for d in range(2):
                            l.wait_ge(*past(nm, "exps", d))
                            qs = slice(4 * d, 4 * d + 4)
                            l.did(V.scalar_tensor_tensor(out=RA[:, qs, 0:P], in0=E0[:, d], scalar=-1.0, in1=kkn[:, :, tok[d]],
                                                         op0=ALU.mult, op1=ALU.mult).then_inc(l.sem, 1))
                            l.did(V.tensor_tensor(RA[:, qs, P:256], E1[:, d], sft[:, R:R + 4, tok[d]], ALU.mult).then_inc(l.sem, 1))
                            for j in range(4):
                                for h in range(2):
                                    hs = slice(64 * h, 64 * h + 64)
                                    z = BKz(4 * d + j, h)
                                    l.did(V.tensor_tensor(z[hs, 0:P], Em[hs, d, j], bb[hs, d, j], ALU.mult).then_inc(l.sem, 1))
                                    l.did(V.tensor_tensor(z[hs, P:256], Em[hs, d, j], kd[hs, d, j], ALU.mult).then_inc(l.sem, 1))
                    products(nm + "cum", gs, dve_extra=dve_y)

                    gs = []
                    for q in range(CELLS):
                        d = q // 4
                        for h in range(2):
                            hs = slice(64 * h, 64 * h + 64)
                            z = BKz(q, h)

                            def read(l, bank, q=q, h=h, d=d):
                                l.did(V.tensor_tensor(Gm[:, q, h, :], bank, masks[:, d, :], ALU.mult).then_inc(l.sem, 1), nm, "Gm", q, h)

                            def turned(l, bank, q=q, h=h):
                                l.did(S.activation(BKt[:, q, :, 64 * h:64 * h + 64], bank[:, 256:384].rearrange("p (e n) -> p e n", e=2),
                                                   ACT.Copy).then_inc(l.sem, 1), nm, "BKt", q, h)

                            def read_A(l, bank, q=q, h=h, d=d):
                                l.wait_ge(*past(nm, "BKt", q, h))
                                l.did(V.tensor_tensor(Am[:, q, h], bank[:, 0:P], masks[:, 1 - d, 0:P], ALU.mult).then_inc(l.sem, 1), nm, "Am", q, h)
                            gs.append({"by": "dve", "read": read, "mms": [
                                ("m", lambda b: b[:, 0:256], z[:, 0:P], RA[:, q, :], True, True),
                                ("m", lambda b: b[:, 256:512], z[:, P:256], RA[:, q, :], True, True)]})
                            gs.append({"by": "dve", "first": ("act", turned), "read": read_A, "mms": [
                                ("m", lambda b: b[:, 0:P], RA[:, q, 0:P], z[:, 0:P], True, True)] + [
                                ("t", (lambda b, e=e: b[:, 256 + 64 * e:320 + 64 * e]), z[hs, e * P:(e + 1) * P], ident[hs, hs])
                                for e in range(2)]})

                    def first_level(l):
                        for q in range(CELLS):
                            d = q // 4
                            l.wait_ge(*past(nm, "Am", q, 1))
                            l.did(G.tensor_tensor(XT[:, q, :, 0:P], Gm[:, q, :, 0:P], lm(d, 0), ALU.mult).then_inc(l.sem, 1))
                            l.did(G.tensor_tensor(XT[:, q, :, P:256], Am[:, q], lm(1 - d, 0), ALU.mult).then_inc(l.sem, 1), nm, "XT0", q)

                    def add_one(l):
                        for q in range(CELLS):
                            l.wait_ge(*past(nm, "XT0", q))
                            x4 = XT[:, q].rearrange("p h (e n) -> p (h e) n", e=2)
                            l.did(V.tensor_tensor(x4, x4, ident.unsqueeze(1).to_broadcast([P, 4, P]), ALU.add).then_inc(l.sem, 1))
                    products(nm + "gram", gs, dve_extra=add_one, pool_fn=first_level)

                    lv = nm + "lev"

                    def lev_pool(l):
                        for i in range(1, 7):
                            for q in range(CELLS):
                                if i > 1:
                                    l.wait_ge(*past(lv, "P1made", i - 1, q))
                                l.did(G.tensor_tensor(Al(q).rearrange("p (h n) -> p h n", h=2), Am[:, q],
                                                      lm(1 - q // 4, i), ALU.mult).then_inc(l.sem, 1), lv, "Al", i, q)

                    def at(r):
                        return r // CELLS + 1, r % CELLS

                    def lev_pe(l):
                        def second(i, q):
                            l.wait_ge(*past(lv, "P1", i, q))
                            r = (i - 1) * CELLS + q
                            if r >= 4:
                                l.wait_ge(*past(lv, "XT", *at(r - 4)))
                            b = banks[:, 4 + r % 4, :]
                            for h in range(2):
                                p1 = P1(q)[:, h * P:(h + 1) * P]
                                tt = XT[:, q, h, P:256]
                                ins = TE.matmul(b[:, h * 256:h * 256 + P], tt, p1, start=True, stop=True)
                                if i < 6:
                                    ins = TE.matmul(b[:, h * 256 + P:h * 256 + 256], p1, tt, start=True, stop=True)
                            l.did(ins.then_inc(l.sem, 1), lv, "XTmade", i, q)
                        for i in range(1, 7):
                            for q in range(CELLS):
                                l.wait_ge(*past(lv, "Al", i, q))
                                if i > 1:
                                    l.wait_ge(*past(lv, "XT", i - 1, q))
                                r = (i - 1) * CELLS + q
                                if r >= 4:
                                    l.wait_ge(*past(lv, "P1", *at(r - 4)))
                                b = banks[:, r % 4, :]
                                for h in range(2):
                                    ins = TE.matmul(b[:, h * P:(h + 1) * P], Al(q)[:, h * P:(h + 1) * P], XT[:, q, h, 0:P],
                                                    start=True, stop=True)
                                l.did(ins.then_inc(l.sem, 1), lv, "P1made", i, q)
                                if q >= 3:
                                    second(i, q - 3)
                            for q in range(CELLS - 3, CELLS):
                                second(i, q)

                    def lev_act(l):
                        for i in range(1, 7):
                            for q in range(CELLS):
                                l.wait_ge(*past(lv, "P1made", i, q))
                                if i > 1:
                                    l.wait_ge(*past(lv, "XTmade", i - 1, q))
                                l.did(S.activation(P1(q), banks[:, ((i - 1) * CELLS + q) % 4, 0:256], ACT.Copy).then_inc(l.sem, 1), lv, "P1", i, q)

                    def lev_dve(l):
                        for i in range(1, 7):
                            for q in range(CELLS):
                                l.wait_ge(*past(lv, "XTmade", i, q))
                                b = banks[:, 4 + ((i - 1) * CELLS + q) % 4, :].rearrange("p (h n) -> p h n", h=2)
                                w = 256 if i < 6 else P
                                l.did(V.tensor_tensor(XT[:, q, :, 0:w], b[:, :, 0:w], XT[:, q, :, 0:w], ALU.add).then_inc(l.sem, 1), lv, "XT", i, q)
                    stage(lv, pe=lev_pe, act=lev_act, dve=lev_dve, pool=lev_pool)

                    sq_ = nm + "seq"
                    hd = lambda q, h: slice((q % 4) * P + 64 * h, (q % 4) * P + 64 * h + 64)

                    def seq_pe(l):
                        for d in range(2):
                            if n:
                                l.wait_ge(*past(sq_, "state", d))
                            for q in range(4 * d, 4 * d + 4):
                                if n:
                                    TE.matmul(banks[:, d, (q % 4) * P:(q % 4 + 1) * P], RA[:, q, 0:P], state[:, d, q % 4, :],
                                              start=True, stop=False)
                                for h in range(2):
                                    ins = TE.matmul(banks[:, d, hd(q, h)], Gm[:, q, h, 256:384], vtm[:, order[d][n], hd(q, h)],
                                                    start=(n == 0), stop=(n == 0 or h == 1))
                            l.did(ins.then_inc(l.sem, 1), sq_, "Wmade", d)
                        for d in range(2):
                            l.wait_ge(*past(sq_, "W", d))
                            for q in range(4 * d, 4 * d + 4):
                                for h in range(2):
                                    ins = TE.matmul(banks[:, 2 + d, hd(q, h)], XT[:, q, h, 0:P], wu[:, 0, d, hd(q, h)],
                                                    start=True, stop=True)
                            l.did(ins.then_inc(l.sem, 1), sq_, "Umade", d)
                        for d in range(2):
                            l.wait_ge(*past(sq_, "U", d))
                            c = order[d][n]
                            if n < NTA - 1:
                                for q in range(4 * d, 4 * d + 4):
                                    js = slice((q % 4) * P, (q % 4 + 1) * P)
                                    TE.matmul(banks[:, 4 + d, js], BKt[:, q, 0, :], wu[:, 1, d, js], start=True, stop=False)
                                    ins = TE.matmul(banks[:, 4 + d, js], BKt[:, q, 1, :], vtm[:, c, js], start=False, stop=True)
                                l.did(ins.then_inc(l.sem, 1), sq_, "Smade", d)
                            if c < NT:
                                for q in range(4 * d, 4 * d + 4):
                                    TE.matmul(banks[:, 6 + d, (q % 4) * P:(q % 4 + 1) * P], RA[:, q, P:256], state[:, d, q % 4, :],
                                              start=True, stop=False)
                                    for h in range(2):
                                        TE.matmul(banks[:, 6 + d, hd(q, h)], Gm[:, q, h, 128:256], wu[:, 1, d, hd(q, h)],
                                                  start=False, stop=False)
                                        ins = TE.matmul(banks[:, 6 + d, hd(q, h)], Gm[:, q, h, 384:512], vtm[:, c, hd(q, h)],
                                                        start=False, stop=(h == 1))
                                l.did(ins.then_inc(l.sem, 1), sq_, "Ymade", d)

                    def seq_act(l):
                        for d in range(2):
                            l.wait_ge(*past(sq_, "Wmade", d))
                            l.did(S.activation(wu[:, 0, d, :], banks[:, d, :], ACT.Copy).then_inc(l.sem, 1), sq_, "W", d)
                        for d in range(2):
                            l.wait_ge(*past(sq_, "Umade", d))
                            l.did(S.activation(wu[:, 1, d, :], banks[:, 2 + d, :], ACT.Copy).then_inc(l.sem, 1), sq_, "U", d)

                    def seq_dve(l):
                        for d in range(2):
                            if n:
                                e = ends[:, d, :].rearrange("p (j e) -> p j e", e=2)
                                l.did(V.tensor_tensor(hop[:, d, :], end_old[:, d, :], e[:, :, 0], ALU.mult).then_inc(l.sem, 1))
                                l.wait_ge(*l.own())
                                l.did(V.tensor_tensor(state[:, d], state[:, d], hop[:, d, :].unsqueeze(2).to_broadcast([P, 4, P]),
                                                      ALU.mult).then_inc(l.sem, 1), sq_, "state", d)
                        for d in range(2):
                            e = ends[:, d, :].rearrange("p (j e) -> p j e", e=2)
                            l.did(V.tensor_copy(end_old[:, d, :], e[:, :, 1]).then_inc(l.sem, 1))
                        for d in range(2):
                            c = order[d][n]
                            if n < NTA - 1:
                                l.wait_ge(*past(sq_, "Smade", d))
                                own = sum_[:, d]
                                if n:
                                    l.did(V.tensor_tensor(own, four(banks[:, 4 + d, :]), ones2.unsqueeze(1).to_broadcast([P, 4, P]),
                                                          ALU.mult).then_inc(l.sem, 1))
                                    l.wait_ge(*past(sq_, "Ymade" if c < NT else "Wmade", d))
                                    l.wait_ge(*l.own())
                                    l.did(V.tensor_tensor(state[:, d], state[:, d], own, ALU.add).then_inc(l.sem, 1))
                                else:
                                    l.did(V.tensor_tensor(state[:, d], four(banks[:, 4 + d, :]), ones2.unsqueeze(1)
                                                          .to_broadcast([P, 4, P]), ALU.mult).then_inc(l.sem, 1))
                            if c < NT:
                                l.wait_ge(*past(sq_, "Ymade", d))
                                first = order[1 - d].index(c) > n
                                if first:
                                    l.did(V.tensor_copy(ytm[:, c, :], banks[:, 6 + d, :]).then_inc(l.sem, 1))
                                else:
                                    l.did(V.tensor_tensor(ytm[:, c, :], banks[:, 6 + d, :], ytm[:, c, :], ALU.add).then_inc(l.sem, 1))
                    stage(sq_, pe=seq_pe, act=seq_act, dve=seq_dve)
                sum_ = region(cells_from, 2, 4, P)
                for n in range(NTA):
                    step(n)
                views.update(ytm=ytm, vtm=vtm, bonus=bonus)

                hold_stream("rwkv5seq")
                wo = a["w_out"][0].rearrange("(k p) n -> p k n", p=P)
                wos.extend(stream(wo[:, :, hf * 512:(hf + 1) * 512], (KD, 512)) for hf in range(2))
                gn = Stack(0, SLOT)
                gate_mem = Stack(3 * SLOT, 4 * SLOT)
                gup = gate_mem.take(512)
                gtm = gate_mem.take(NT, 512)
                small("gate", [(gup, a["gate_up"][0])], after="rwkv5seq")
                products("rwkv_gate", [{"have": ("gate",), "by": halves(t), "read": copy_out(gtm[:, t, :]),
                                        "mms": acc(lambda b: b, [(sft[:, 13, t * P:(t + 1) * P], gup)])} for t in range(NT)])
                lg, lb = gn.take(512), gn.take(512)
                yc = gn.take(NT, 512)
                mu8, va8, rs8 = gn.take(32), gn.take(32), gn.take(32)
                small("lnx", [(lg, a["lnx_g"].to_broadcast([P, 512])), (lb, a["lnx_b"].to_broadcast([P, 512]))],
                      after="rwkv5seq")
                h64 = lambda ap: ap.rearrange("p t (h n) -> p (t h) n", n=HD)
                bc = lambda ap: ap.unsqueeze(2).to_broadcast([P, 32, HD])
                flat = lambda ap: ap.rearrange("p a b -> p (a b)")

                def gn_dve(l):
                    y3 = h64(ytm)
                    l.did(V.reduce_sum(mu8, y3, axis=AX.X).then_inc(l.sem, 1))
                    l.wait_ge(*l.own())
                    l.did(V.tensor_scalar(mu8, mu8, 1.0 / HD, None, ALU.mult).then_inc(l.sem, 1))
                    l.wait_ge(*l.own())
                    l.did(V.tensor_tensor(y3, y3, bc(mu8), ALU.subtract).then_inc(l.sem, 1))
                    l.wait_ge(*l.own())
                    l.did(V.tensor_tensor(yc, ytm, ytm, ALU.mult).then_inc(l.sem, 1))
                    l.wait_ge(*l.own())
                    l.did(V.reduce_sum(va8, h64(yc), axis=AX.X).then_inc(l.sem, 1))
                    l.wait_ge(*l.own())
                    l.did(V.tensor_scalar(va8, va8, 1.0 / HD, GN_EPS, ALU.mult, ALU.add).then_inc(l.sem, 1), "gn_var")
                    l.wait_ge(*past("gn_sd"))
                    l.did(V.reciprocal(va8, rs8).then_inc(l.sem, 1))
                    l.wait_ge(*l.own())
                    l.did(V.tensor_tensor(y3, y3, bc(va8), ALU.mult).then_inc(l.sem, 1))
                    l.did(V.tensor_tensor(h64(yc), h64(vtm[:, 0:NT, :]), bc(flat(bonus)), ALU.mult).then_inc(l.sem, 1))
                    l.wait_ge(*smalls["lnx"])
                    l.wait_ge(*l.own())
                    for src, op in ((lg, ALU.mult), (lb, ALU.add)):
                        l.did(V.tensor_tensor(ytm, ytm, src.unsqueeze(1).to_broadcast([P, NT, 512]), op).then_inc(l.sem, 1))
                        l.wait_ge(*l.own())
                    l.did(V.tensor_tensor(ytm, ytm, yc, ALU.add).then_inc(l.sem, 1))
                    l.wait_ge(*l.own())
                    l.did(V.tensor_tensor(ytm, ytm, gtm, ALU.mult).then_inc(l.sem, 1))

                def gn_act(l):
                    l.wait_ge(*past("gn_var"))
                    l.did(S.activation(rs8, va8, ACT.Sqrt).then_inc(l.sem, 1), "gn_sd")
                stage("rwkv_norm", dve=gn_dve, act=gn_act)
                products("rwkv_T", transpose_groups(lambda t: ytm[:, t, :], lambda k: mixT[:, 4 + k, :], NT, 0, 4))
                views.update(rwo=ytm, mixAll=mixT)

            def part_four():
                x1 = region(base.at, NT, D)
                xin_at, gt_at, y_at, hid_at = (base.at + n * D for n in (4, 12, 16, 24))
                xr = region(xin_at, NT, D)
                g1, b1 = region(hid_at, D), region(hid_at + D, D)
                tmpx = region(hid_at + 2 * D, 2, 512)
                small("ln1", [(xr, a["x"][0].rearrange("(t p) n -> p t n", p=P)),
                              (g1, a["ln1_g"].to_broadcast([P, D])), (b1, a["ln1_b"].to_broadcast([P, D]))],
                      after="rwkv5seq")

                def residual(name, ws_, gate, x_old, x_new, lhs, nk, tmpx, hv=None):
                    gs = []
                    for hf in range(2):
                        for t in range(NT):
                            i = len(gs)

                            def read(l, bank, hf=hf, t=t, i=i):
                                if hv:
                                    l.wait_ge(*smalls[hv])
                                v = slice(hf * 512, hf * 512 + 512)
                                l.wait_ge(*l.own())
                                l.did(V.tensor_tensor(tmpx[:, i % 2, :], bank, gate[:, v], ALU.mult).then_inc(l.sem, 1))
                                l.wait_ge(*l.own())
                                l.did(V.scalar_tensor_tensor(out=x_new[:, t, v], in0=x_old[:, t, v], scalar=ALPHA,
                                                             in1=tmpx[:, i % 2, :], op0=ALU.mult, op1=ALU.add).then_inc(l.sem, 1))
                            gs.append({"by": "dve", "read": read, "loads": [ws_[hf][0]] if ws_ else [],
                                       "mms": acc(lambda b: b, [lhs(k, t, hf) for k in range(nk)])})
                    products(name, gs)
                residual("w_out", wos, gt1, xr, x1,
                         lambda k, t, hf: (mixT[:, k, t * P:(t + 1) * P], wos[hf][1][:, k, :]), KD, tmpx, hv="ln1")
                norm_stage("norm_x1", lambda i: x1[:, i, :], lambda i: x1[:, i, :], NT, [], affine=(g1, b1))
                views.update(x1=x1)

                xh = region(y_at, NT, D)
                h2T = region(gt_at, KD, T)
                norm_stage("norm_h2", lambda i: x1[:, i, :], lambda i: xh[:, i, :], NT, [])
                products("h2_T", transpose_groups(lambda i: xh[:, i, :], lambda k: h2T[:, k, :], NT, 0, KD,
                                                  lambda k: (modcol[:, 32 + k, 0:1], modcol[:, 24 + k, 0:1])))
                sm = Stack(hid_at, hid_at + 5 * D)
                rw = sm.take(KD, NE)
                aff = stats[:, 120:184].rearrange("p (t e) -> p t e", e=NE)
                rank = stats[:, 184:248].rearrange("p (t e) -> p t e", e=NE)
                eqs = sm.take(NT, NE)
                late = sm.take(NT, NE)
                mx4, sm4 = sm.take(NT), sm.take(NT)
                affT = sm.take(T)
                before = sm.take(P)
                slots = sm.take(CAP)
                junk = sm.take(4, 512)
                small("router", [(rw, a["router_w"][0].rearrange("(k p) e -> p k e", p=P)),
                                 (before, a["k_before"][:, 0, 0:P]), (slots, a["k_slots"])], after="h2_T")

                def logits_read(l, bank):
                    lg = bank[:, 0:64].rearrange("p (t e) -> p t e", e=NE)
                    l.did(V.reduce_max(mx4, lg, axis=AX.X).then_inc(l.sem, 1))
                    l.wait_ge(*l.own())
                    l.did(V.tensor_tensor(aff, lg, mx4.unsqueeze(2).to_broadcast([P, NT, NE]), ALU.subtract).then_inc(l.sem, 1), "router_in")

                def router_act(l):
                    l.wait_ge(*past("router_in"))
                    l.did(S.activation(aff, aff, ACT.Exp).then_inc(l.sem, 1), "router_exp")

                def router_dve(l):
                    l.wait_ge(*past("router_exp"))
                    l.did(V.reduce_sum(sm4, aff, axis=AX.X).then_inc(l.sem, 1))
                    l.wait_ge(*l.own())
                    l.did(V.reciprocal(sm4, sm4).then_inc(l.sem, 1))
                    l.wait_ge(*l.own())
                    l.did(V.tensor_tensor(aff, aff, sm4.unsqueeze(2).to_broadcast([P, NT, NE]), ALU.mult).then_inc(l.sem, 1))
                products("router", [{"have": ("router",), "by": "dve", "read": logits_read, "mms": [
                    m_ for t in range(NT) for m_ in
                    acc(lambda b, t=t: b[:, t * NE:(t + 1) * NE],
                        [(h2T[:, k, t * P:(t + 1) * P], rw[:, k, :]) for k in range(KD)])]}],
                    act_extra=router_act, dve_extra=router_dve)
                products("aff_T", [{"by": "act", "read": copy_out(affT[0:NE, :], lambda b: b[0:NE, :]), "mms": [
                    ("t", (lambda b, t=t: b[0:NE, t * P:(t + 1) * P]), aff[:, t, :], ident) for t in range(NT)]}])

                affb = region(xin_at, NE, T)

                def bounce(l):
                    l.engine.dma_start(a["scratch"], affT[0:NE, :]).then_inc(scratch_io, 16)
                    l.engine.wait_ge(scratch_io, 16)
                    l.engine.dma_start(affb.rearrange("p e t -> p (e t)"), a["scratch"].rearrange("e t -> (e t)")
                                       .unsqueeze(0).to_broadcast([P, NE * T])).then_inc(scratch_io, 16)

                def ranks(l):
                    l.engine.wait_ge(scratch_io, 32)
                    for t in range(NT):
                        for e in range(NE):
                            s_ = aff[:, t, e:e + 1]
                            jk = junk[:, (t * NE + e) % 4, :]
                            if t:
                                l.did(V.tensor_scalar(jk[:, 0:t * P], affb[:, e, 0:t * P], s_, 0.0, ALU.is_ge, ALU.add,
                                                      accum_out=eqs[:, t, e:e + 1]).then_inc(l.sem, 1))
                            l.did(V.tensor_scalar(jk[:, t * P:T], affb[:, e, t * P:T], s_, 0.0, ALU.is_gt, ALU.add,
                                                  accum_out=rank[:, t, e:e + 1]).then_inc(l.sem, 1))
                            l.did(V.scalar_tensor_tensor(out=jk2[:, (t * NE + e) % 4, :], in0=affb[:, e, t * P:(t + 1) * P], scalar=s_,
                                                         in1=before, op0=ALU.is_equal, op1=ALU.mult,
                                                         accum_out=late[:, t, e:e + 1]).then_inc(l.sem, 1))
                            if (t * NE + e) % 4 == 3:
                                l.wait_ge(*l.own())
                    l.wait_ge(*l.own())
                    l.did(V.tensor_tensor(rank, rank, late, ALU.add).then_inc(l.sem, 1))
                    l.wait_ge(*l.own())
                    l.did(V.tensor_tensor(rank[:, 1:NT, :], rank[:, 1:NT, :], eqs[:, 1:NT, :], ALU.add).then_inc(l.sem, 1))
                jk2 = sm.take(4, P)
                stage("ranks", act=bounce, dve=ranks)

                G1 = region(y_at + 4 * D, NT, NE * CAP)
                G2 = region(hid_at, NT, NE * CAP)

                slots2 = region(gt_at, CAP)

                def save_slots(l):
                    l.did(V.tensor_copy(slots2, slots).then_inc(l.sem, 1))
                stage("slots", dve=save_slots)

                def onehot(l):
                    es = lambda ap: ap.rearrange("p (e c) -> p e c", c=CAP)
                    for t in range(NT):
                        l.did(V.tensor_tensor(es(G1[:, t, :]), slots2.unsqueeze(1).to_broadcast([P, NE, CAP]),
                                              rank[:, t, :].unsqueeze(2).to_broadcast([P, NE, CAP]), ALU.is_equal).then_inc(l.sem, 1))
                    l.wait_ge(*l.own())
                    for t in range(NT):
                        l.did(V.tensor_tensor(es(G2[:, t, :]), es(G1[:, t, :]),
                                              aff[:, t, :].unsqueeze(2).to_broadcast([P, NE, CAP]), ALU.mult).then_inc(l.sem, 1))
                stage("onehot", dve=onehot)
                xinT = region(xin_at, KD, NE * CAP)
                GgT = region(gt_at, NE // 2, T)
                gs = []
                for k in range(KD):
                    for hf in range(2):
                        v = slice(hf * 512, hf * 512 + 512)

                        def read(l, bank, k=k, v=v):
                            sc, sh = modcol[:, 32 + k, 0:1], modcol[:, 24 + k, 0:1]
                            if l is act:
                                l.did(S.activation(xinT[:, k, v], bank, ACT.Identity, bias=sh, scale=sc).then_inc(l.sem, 1))
                            else:
                                l.did(V.tensor_scalar(xinT[:, k, v], bank, sc, sh, ALU.mult, ALU.add).then_inc(l.sem, 1))
                        gs.append({"by": halves(k), "read": read, "mms": acc(lambda b: b, [
                            (xh[:, t, k * P:(k + 1) * P], G1[:, t, v]) for t in range(NT)])})
                for q in range(NE // 2):
                    gs.append({"by": halves(q), "read": copy_out(GgT[:, q, :]), "mms": [
                        ("t", (lambda b, t=t: b[:, t * P:(t + 1) * P]), G2[:, t, q * P:(q + 1) * P], ident) for t in range(NT)]})
                products("gather", gs)
                views.update(rank=rank, aff=aff, xinT=xinT)

                hold_stream("rwkv_T")
                ysb = region(y_at, NE // 2, D)
                hb = Stack(hid_at, hid_at + 5 * D)
                hid = hb.take(2, D)
                sgt = hb.take(2, 512)
                hidT = hb.take(2, KD, P)
                gs, ex_ = [], "experts"
                wsrc = {n: a["exp_w_" + n] for n in ("gate", "up", "down")}

                def pair_weights(kind, q, hf):
                    return [stream(wsrc[kind][0, 2 * q + e].rearrange("(k p) n -> p k n", p=P)[:, :, hf * 512:(hf + 1) * 512],
                                   (KD, 512)) for e in range(2)]

                def two(w, lhs):
                    return [("m", (lambda b, e=e: b[64 * e:64 * e + 64, :]), lhs(k, e), w[e][1][:, k, :], k == 0, k == KD - 1)
                            for k in range(KD) for e in range(2)]

                def gate_up(q):
                    for hf in range(2):
                        v = slice(hf * 512, hf * 512 + 512)
                        for kind in ("gate", "up"):
                            w = pair_weights(kind, q, hf)
                            lhs = lambda k, e, q=q: xinT[:, k, (2 * q + e) * CAP:(2 * q + e + 1) * CAP]
                            g = {"by": "dve", "loads": [w[0][0], w[1][0]], "mms": two(w, lhs)}
                            if kind == "gate":
                                def first(l, bank, q=q, hf=hf):
                                    if 2 * q + hf >= 2:
                                        l.wait_ge(*past(ex_, "gated", 2 * q + hf - 2))
                                    l.did(S.activation(sgt[:, hf, :], bank, ACT.Sigmoid).then_inc(l.sem, 1), ex_, "sig", q, hf)

                                def read(l, bank, q=q, hf=hf, v=v):
                                    l.wait_ge(*past(ex_, "sig", q, hf))
                                    if q >= 2:
                                        l.wait_ge(*past(ex_, "turned", q - 2))
                                    l.did(V.tensor_tensor(hid[:, q % 2, v], bank, sgt[:, hf, :], ALU.mult).then_inc(l.sem, 1), ex_, "gated", 2 * q + hf)
                                g["first"] = ("act", first)
                            else:
                                def read(l, bank, q=q, hf=hf, v=v):
                                    l.wait_ge(*l.own())
                                    l.did(V.tensor_tensor(hid[:, q % 2, v], bank, hid[:, q % 2, v], ALU.mult).then_inc(l.sem, 1), ex_, "hid", q, hf)
                            g["read"] = read
                            gs.append(g)

                def down(q):
                    for hf in range(2):
                        g = {"by": "act", "after": [(ex_, "hid", q, hf)], "mms": [
                            ("t", (lambda b, i=i: b[:, i * P:(i + 1) * P]), hid[:, q % 2, (4 * hf + i) * P:(4 * hf + i + 1) * P], ident)
                            for i in range(4)]}

                        def read(l, bank, q=q, hf=hf):
                            if q >= 2:
                                l.wait_ge(*past(ex_, "downed", q - 2))
                            l.did(S.activation(hidT[:, q % 2, 4 * hf:4 * hf + 4, :], bank.rearrange("p (a b) -> p a b", b=P),
                                               ACT.Copy).then_inc(l.sem, 1), ex_, "hidT", q, hf)
                        g["read"] = read
                        if hf == 1:
                            g["name"] = (ex_, "turned", q)
                        gs.append(g)
                    for hf in range(2):
                        v = slice(hf * 512, hf * 512 + 512)
                        w = pair_weights("down", q, hf)
                        g = {"by": halves(hf), "loads": [w[0][0], w[1][0]], "after": [(ex_, "hidT", q, 0), (ex_, "hidT", q, 1)],
                             "mms": two(w, lambda k, e, q=q: hidT[:, q % 2, k, 64 * e:64 * e + 64]),
                             "read": copy_out(ysb[:, q, v])}
                        if hf == 1:
                            g["name"] = (ex_, "downed", q)
                        gs.append(g)
                for q in range(NE // 2 + 1):
                    if q < NE // 2:
                        gate_up(q)
                    if q:
                        down(q - 1)
                products(ex_, gs)

                small("ln2", [(region(xin_at, D), a["ln2_g"].to_broadcast([P, D])),
                              (region(xin_at + D, D), a["ln2_b"].to_broadcast([P, D]))], after="experts")
                tmpx2 = region(xin_at + 2 * D, 2, 512)
                residual("scatter", None, gt2, x1, x1,
                         lambda q, t, hf: (GgT[:, q, t * P:(t + 1) * P], ysb[:, q, hf * 512:(hf + 1) * 512]), NE // 2, tmpx2, hv="ln2")
                norm_stage("norm_x2", lambda i: x1[:, i, :], lambda i: x1[:, i, :], NT, [],
                           affine=(region(xin_at, D), region(xin_at + D, D)))
                views.update(x2=x1)

            def part_five():
                x = region(base.at, NT, D)
                hT_at = base.at + 4 * D
                hT = region(hT_at, KD, T)
                rest = Stack(base.at + 8 * D)
                gcols = rest.take(98)
                grow = rest.take(D)
                ones2 = rest.take(P)
                sbk = rest.take(3, P)
                lamp = rest.take(2, 4, 32)
                lam = rest.take(8)
                st = rest.take(3, 8)
                ss = rest.take(16)
                grows = region(base.at + 4 * D, P)
                gains = a["norm_gains_2"]
                small("second", [(grows[0:96, :], gains.rearrange("l n (k p) -> (l n k) p", p=P)),
                                 (grows[96:98, 0:64], a["diff_subln_gain_2"]), (grows[96:98, 64:128], a["diff_subln_gain_2"]),
                                 (ones2, a["k_ones2"]), (sbk, a["k_sb"]),
                                 (lamp, a["diff_lambda_2"].rearrange("l a n -> (l a n)").unsqueeze(0).to_broadcast([P, 256]))],
                      after="norm_x2")
                lam_init = [0.8 - 0.6 * math.exp(-0.3 * l) for l in range(2)]

                def lam_dve(l):
                    l.wait_ge(*smalls["second"])
                    l.did(V.tensor_tensor(lamp[:, :, 0::2, :], lamp[:, :, 0::2, :], lamp[:, :, 1::2, :], ALU.mult).then_inc(l.sem, 1))
                    l.wait_ge(*l.own())
                    l.did(V.reduce_sum(lam[:, 0:4].rearrange("p (l a) -> p l a", l=2), lamp[:, :, 0::2, :], axis=AX.X).then_inc(l.sem, 1), "lam_sums")
                    l.wait_ge(*past("lam_exp"))
                    lv = lam[:, 0:4].rearrange("p (l a) -> p l a", l=2)
                    l.did(V.tensor_tensor(lam[:, 4:6], lv[:, :, 1], lv[:, :, 0], ALU.subtract).then_inc(l.sem, 1))
                    l.wait_ge(*l.own())
                    for i in range(2):
                        l.did(V.tensor_scalar(lam[:, 4 + i:5 + i], lam[:, 4 + i:5 + i], -lam_init[i], None, ALU.add).then_inc(l.sem, 1))

                def lam_act(l):
                    l.wait_ge(*past("lam_sums"))
                    l.did(S.activation(lam[:, 0:4], lam[:, 0:4], ACT.Exp).then_inc(l.sem, 1), "lam_exp")
                stage("lambda", dve=lam_dve, act=lam_act)
                products("gain_cols", [{"by": "dve", "read": copy_out(gcols, lambda b: b[:, 0:98]),
                                        "mms": [("t", lambda b: b[:, 0:98], grows[0:98, :], ident[0:98, 0:98])]}])

                def between(name, coef, row, col, key=None):
                    ybank = lambda t: banks[:, 2 * t:2 * t + 2, :].rearrange("p a b -> p (a b)")
                    scr = region(rest_end, 2, D)

                    def f_act(l):
                        if row is not None:
                            for t in range(NT):
                                l.did(S.activation(scr[:, t % 2, :], ybank(t), ACT.Square, accum_out=ss[:, t:t + 1]).then_inc(l.sem, 1), name, "yy", t)
                                l.wait_ge(*l.own())
                            for t in range(NT):
                                l.wait_ge(*past(name, "yvar", t))
                                l.did(S.activation(ss[:, 4 + t:5 + t], ss[:, 4 + t:5 + t], ACT.Sqrt).then_inc(l.sem, 1), name, "ysd", t)
                        if col is None:
                            return
                        for t in range(NT):
                            if row is not None:
                                l.wait_ge(*past(name, "x", t))
                            l.wait_ge(*l.own())
                            l.did(S.activation(scr[:, t % 2, :], x[:, t, :], ACT.Square, accum_out=ss[:, 8 + t:9 + t]).then_inc(l.sem, 1), name, "xx", t)
                        for t in range(NT):
                            l.wait_ge(*past(name, "xvar", t))
                            l.did(S.activation(ss[:, 12 + t:13 + t], ss[:, 12 + t:13 + t], ACT.Sqrt).then_inc(l.sem, 1), name, "xsd", t)
                        for t in range(NT):
                            for hf in (1,):
                                l.wait_ge(*past(name, "turned", t, hf))
                                for i in range(4):
                                    k = 4 * hf + i
                                    if True:
                                        l.did(S.activation(hT[:, k, t * P:(t + 1) * P], banks[:, 2 * t + hf, i * P:(i + 1) * P],
                                                           ACT.Copy, scale=col(k)).then_inc(l.sem, 1))

                    def f_dve(l):
                        if row is not None:
                            l.wait_ge(*smalls[key])
                            for t in range(NT):
                                l.wait_ge(*past(name, "yy", t))
                                l.did(V.tensor_scalar(ss[:, 4 + t:5 + t], ss[:, t:t + 1], 1.0 / D, NORM_EPS, ALU.mult, ALU.add).then_inc(l.sem, 1), name, "yvar", t)
                            for t in range(NT):
                                l.wait_ge(*past(name, "ysd", t))
                                l.did(V.reciprocal(ss[:, 4 + t:5 + t], ss[:, 4 + t:5 + t]).then_inc(l.sem, 1))
                            l.wait_ge(*l.own())
                            if coef != 1.0:
                                l.did(V.tensor_scalar(ss[:, 4:8], ss[:, 4:8], coef, None, ALU.mult).then_inc(l.sem, 1))
                                l.wait_ge(*l.own())
                            for t in range(NT):
                                l.did(V.scalar_tensor_tensor(out=ytmp[:, t % 2, :], in0=ybank(t), scalar=ss[:, 4 + t:5 + t], in1=grow,
                                                             op0=ALU.mult, op1=ALU.mult).then_inc(l.sem, 1))
                                l.wait_ge(*l.own())
                                l.did(V.tensor_tensor(x[:, t, :], x[:, t, :], ytmp[:, t % 2, :], ALU.add).then_inc(l.sem, 1), name, "x", t)
                        if col is None:
                            return
                        for t in range(NT):
                            l.wait_ge(*past(name, "xx", t))
                            l.did(V.tensor_scalar(ss[:, 12 + t:13 + t], ss[:, 8 + t:9 + t], 1.0 / D, NORM_EPS, ALU.mult, ALU.add).then_inc(l.sem, 1), name, "xvar", t)
                        for t in range(NT):
                            l.wait_ge(*past(name, "xsd", t))
                            l.did(V.reciprocal(ss[:, 12 + t:13 + t], ss[:, 12 + t:13 + t]).then_inc(l.sem, 1))
                            l.wait_ge(*l.own())
                            if t >= 2:
                                l.wait_ge(*past(name, "turned", t - 2, 1))
                            l.did(V.tensor_scalar(ytmp[:, t % 2, :], x[:, t, :], ss[:, 12 + t:13 + t], None, ALU.mult).then_inc(l.sem, 1), name, "xs", t)
                            if t:
                                evac(l, t - 1)
                        evac(l, NT - 1)

                    def evac(l, t):
                        for hf in (0,):
                            l.wait_ge(*past(name, "turned", t, hf))
                            for i in range(4):
                                k = 4 * hf + i
                                if True:
                                    l.did(V.tensor_scalar(hT[:, k, t * P:(t + 1) * P], banks[:, 2 * t + hf, i * P:(i + 1) * P],
                                                          col(k), None, ALU.mult).then_inc(l.sem, 1))

                    def f_pe(l):
                        if col is None:
                            return
                        for t in range(NT):
                            l.wait_ge(*past(name, "xs", t))
                            for hf in range(2):
                                for i in range(4):
                                    k = 4 * hf + i
                                    ins = TE.transpose(banks[:, 2 * t + hf, i * P:(i + 1) * P], ytmp[:, t % 2, k * P:(k + 1) * P], ident)
                                l.did(ins.then_inc(l.sem, 1), name, "turned", t, hf)
                    stage(name, act=f_act, dve=f_dve, pe=f_pe)
                rest.at += -rest.at % 8
                ytmp_at = rest.at
                ffn_r = parts_of("ffn_r", ytmp_at, ARENA - ytmp_at)
                mix_r, h_r = parts_of("mix_r", mixT_at, KD * T), parts_of("h_r", hT_at, KD * T)
                ytmp = rest.take(2, D)
                rest_end = rest.at
                rest.take(2, D)
                body = rest.at
                gcol = lambda l, n: (lambda k: gcols[:, (l * 6 + n) * KD + k:(l * 6 + n) * KD + k + 1])

                def ffn(l_, f_):
                    nm = f"ffn{l_}{f_}"
                    free = Stack(ytmp_at)
                    hid_at = free.at
                    hid = free.take(NF, T)
                    hid_lo = ffn_r(hid_at, NF, T)
                    DEPTH = 3
                    hi_at = free.at
                    free.take(DEPTH, 2048)
                    his = [ffn_r(hi_at + i * 2048, 2048) for i in range(DEPTH)]
                    hid_hi_at = free.at
                    free.take(2, 2, T)
                    hid_his = [ffn_r(hid_hi_at + i * 2 * T, 2, T) for i in range(2)]
                    hT_hi, hT_lo = mix_r(mixT_at, KD, T), h_r(hT_at, KD, T)
                    wg, wu, wd = (a["w_ffn_" + n + "_2"][l_, f_] for n in ("gate", "up", "down"))
                    src = lambda w, c: w.rearrange("(k p) n -> p k n", p=P)[:, :, c * 256:(c + 1) * 256]

                    def split_h(l):
                        for i in range(4):
                            ks = slice(2 * i, 2 * i + 2)
                            split(l, nm + "h", i, (hT[:, ks, :], hT_lo[:, ks, :], hT_hi[:, ks, :], None), 4)
                    gs, units = [], []
                    for s_ in range(NF // 2):
                        n, w = stream_many([((KD, 256), src(wg, s_)), ((KD, 256), src(wu, s_))])
                        at_ = (n[0] % RING) * SLOT
                        for c in range(2):
                            f = 2 * s_ + c
                            cut = lambda ap, c=c: ap.rearrange("p (k c n) -> p k c n", k=16, c=2)[:, :, c, :]
                            hi = his[f % DEPTH].rearrange("p (k n) -> p k n", n=P)
                            lo = cut(ring_r(at_, SLOT))
                            units.append((cut(region(at_, SLOT)), lo, hi, n))

                            def first(l, bank, f=f):
                                l.did(S.activation(hid[:, f, :], bank, ACT.Sigmoid).then_inc(l.sem, 1), nm, "sig", f)

                            def read(l, bank, f=f):
                                l.wait_ge(*past(nm, "sig", f))
                                l.did(V.tensor_tensor(hid[:, f, :], bank, hid[:, f, :], ALU.mult).then_inc(l.sem, 1))

                            def read_up(l, bank, f=f):
                                l.wait_ge(*l.own())
                                l.did(V.tensor_tensor(hid[:, f, :], bank, hid[:, f, :], ALU.mult).then_inc(l.sem, 1))
                            for j in range(2):
                                gs.append({"by": "dve", "read": read_up if j else read, "loads": [n], "unit": f,
                                           "after": [(nm + "h", "lo", 3)] if not gs else [],
                                           "mms": three(lambda b: b, [((hi[:, 8 * j + k, :], lo[:, 8 * j + k, :]),
                                                                       (hT_hi[:, k, :], hT_lo[:, k, :])) for k in range(KD)])})
                                if j == 0:
                                    gs[-1]["first"] = ("act", first)
                    products(nm, gs, units=units, depth=DEPTH, before=split_h)

                    dn, pairs = nm + "down", NF // 2
                    downs, w_units, h_units = [], [], []
                    for s_ in range((NF + 3) // 4):
                        m_ = min(4, NF - 4 * s_)
                        downs.append(stream(wd.rearrange("(f p) n -> p f n", p=P)[:, 4 * s_:4 * s_ + m_, :], (m_, D)))
                    for u in range(pairs):
                        n, _ = downs[u // 2]
                        at_ = (n[0] % RING) * SLOT + (u % 2) * 2 * D
                        w_units.append((region(at_, 2, D), ring_r(at_, 2, D),
                                        his[u % DEPTH].rearrange("p (f n) -> p f n", n=D), n))
                        fs = slice(2 * u, 2 * u + 2)
                        h_units.append((hid[:, fs, :], hid_lo[:, fs, :], hid_his[u % 2], None))
                    small(nm + "g", [(grow, gains[l_, 1 if f_ == 0 else 5, :].unsqueeze(0).to_broadcast([P, D]))], after=nm)

                    def split_down(l):
                        for u in range(pairs):
                            split(l, dn + "h", u, h_units[u], 2)
                            split(l, dn, u, w_units[u], DEPTH)

                    def down_pe(l):
                        for u in range(pairs):
                            l.wait_ge(*past(dn, "lo", u))
                            _, w_lo, w_hi, n = w_units[u]
                            for c in range(2):
                                f = 2 * u + c
                                for t in range(NT):
                                    ts = slice(t * P, (t + 1) * P)
                                    for hf in range(2):
                                        ns = slice(hf * 512, (hf + 1) * 512)
                                        h_hi, h_lo = hid_his[u % 2][:, c, ts], hid_lo[:, f, ts]
                                        bank = banks[:, 2 * t + hf, :]
                                        TE.matmul(bank, h_hi, w_hi[:, c, ns], start=(f == 0), stop=False)
                                        TE.matmul(bank, h_hi, w_lo[:, c, ns], start=False, stop=False)
                                        ins = TE.matmul(bank, h_lo, w_hi[:, c, ns], start=False, stop=(f == NF - 1))
                            l.did(ins.then_inc(l.sem, 1), dn, "used", u)
                            l.name_last(dn + "h", "used", u)
                            if u % 2 or u == pairs - 1:
                                l.name_last("freed", n[0])
                    stage(dn, pe=down_pe, act=split_down, dve=split_down)

                def mixer(l_):
                    nm = f"mix{l_}"
                    m5 = Stack(body)
                    qk = m5.take(16, T)
                    y_at_ = rest_end - 2 * D
                    odd_a = [region(y_at_ + 3 * 512, T), grow[:, 0:T], grow[:, T:2 * T]]
                    qz_a = lambda h: qk[:, h // 2, :] if h % 2 == 0 else odd_a[h // 2]
                    vt = m5.take(NT, D)
                    extra = m5.at
                    w_src = a["w_in_2"][l_].rearrange("(k p) n -> p k n", p=P)
                    ws = [stream(w_src[:, :, s_ * 512:(s_ + 1) * 512], (KD, 512)) for s_ in range(6)]
                    fm = {c * P: i for i, c in enumerate([0, 1, 2, 3, 4, 5, 9, 10, 11, 12, 15, 16, 17, 18, 19, 20])}
                    tm = {768: (256, 0), 1024: (128, 256), 1664: (256, 384), 2688: (384, 640)}
                    gs = []
                    for c0 in sorted(list(fm) + list(tm)):
                        n, w = ws[c0 // 512]
                        o = c0 % 512
                        if c0 in fm:
                            i = fm[c0]

                            def read(l, bank, i=i):
                                if 10 <= i < 13:
                                    if l is act:
                                        l.did(S.activation(qk[:, i, :], bank, ACT.Copy, scale=HD ** -0.5).then_inc(l.sem, 1))
                                    else:
                                        l.did(V.tensor_scalar(qk[:, i, :], bank, HD ** -0.5, None, ALU.mult).then_inc(l.sem, 1))
                                elif i < 3:
                                    for h in range(2):
                                        hs = slice(64 * h, 64 * h + 64)
                                        copy_out(qz_a(2 * i + h)[hs, :], lambda b, hs=hs: b[hs, :])(l, bank)
                                else:
                                    copy_out(qk[:, i, :])(l, bank)
                            gs.append({"by": halves(len(gs)), "loads": [n], "read": read,
                                       "mms": acc(lambda b: b, [(w[:, k, o:o + P], hT[:, k, :]) for k in range(KD)])})
                        else:
                            width, v0 = tm[c0]
                            for t in range(NT):
                                gs.append({"by": halves(len(gs)), "loads": [n],
                                           "read": copy_out(vt[:, t, v0:v0 + width], lambda b, width=width: b[:, 0:width]),
                                           "mms": acc(lambda b, width=width: b[:, 0:width],
                                                      [(hT[:, k, t * P:(t + 1) * P], w[:, k, o:o + width]) for k in range(KD)])})
                    def zero_a(l):
                        for h in range(6):
                            z = 64 - 64 * (h % 2)
                            l.did(G.memset(qz_a(h)[z:z + 64, :], 0.0).then_inc(l.sem, 1))
                    products(nm, gs, pool_fn=zero_a)
                    pt = region(base.at + 4 * D, 2, NT, T)
                    b_dil = region(extra, 6, T)
                    b_dif = region(rest_end, 4, T)
                    small(nm + "bias", [(b_dil, a["k_bias"][0:6, :, 0:T].rearrange("h p n -> p h n")),
                                        (b_dif, a["k_bias"][6:10, :, 0:T].rearrange("h p n -> p h n"))], after=nm)
                    width = lambda t: P * (t + 1)
                    half = lambda h: HD * (h % 2)

                    def s_dil(h, t):
                        return [[(qz_a(h)[:, t * P:(t + 1) * P], qk[:, 3 + h // 2, 0:width(t)], 0, width(t))]]
                    attention(nm + "dil", list(range(6)), width, s_dil, lambda h, j: vt[:, j, h * HD:(h + 1) * HD],
                              lambda h: mixT[half(h):half(h) + HD, h // 2, :], HD ** -0.5, ([region(y_at_ + i * 512, 512) for i in range(3)], pt, st),
                              bias=lambda h, t: b_dil[:, h, 384 - P * t:T], need=(nm + "bias",))

                    qz_b = [region(body + i * T, T) if i < 6 else region(extra + (i - 6) * T, T) for i in range(8)]

                    def pad_b_pool(l):
                        l.did(G.memset(region(body, 6 * T), 0.0).then_inc(l.sem, 1))
                        l.did(G.memset(region(extra, 2 * T), 0.0).then_inc(l.sem, 1), nm, "zero_b")

                    def pad_b_dve(l):
                        l.wait_ge(*past(nm, "zero_b"))
                        for i in range(8):
                            r0 = 32 * (i % 4)
                            l.did(V.tensor_copy(qz_b[i][r0:r0 + 32, :], qk[r0:r0 + 32, 6 + i // 4, :]).then_inc(l.sem, 1))
                    stage(nm + "padb", pool=pad_b_pool, dve=pad_b_dve)
                    small(f"mix{l_}g", [(grow, gains[l_, 3, :].unsqueeze(0).to_broadcast([P, D]))], after=nm + "dil")
                    def s_dif(h, t):
                        out_ = []
                        for e in range(2):
                            out_.append([(qz_b[2 * h + e][:, t * P:(t + 1) * P], qk[:, 8 + h // 2, 0:width(t)], 0, width(t))])
                        return out_
                    attention(nm + "dif", list(range(4)), width, s_dif, lambda h, j: vt[:, j, 384 + h * HD:384 + (h + 1) * HD],
                              lambda h: mixT[half(h):half(h) + HD, 3 + h // 2, :], 32 ** -0.5,
                              ([region(y_at_, D), region(y_at_ + D, D), region(extra + 2 * T, D)], pt, st),
                              bias=lambda h, t: b_dif[:, h, 384 - P * t:T], lam=lam[:, 4 + l_:5 + l_], need=(nm + "bias",))

                    sq2 = region(extra, 2, T)
                    rs2 = region(extra + 2 * T, 2, T)

                    def sub_sq(l):
                        l.did(V.tensor_tensor(sq2, mixT[:, 3:5, :], mixT[:, 3:5, :], ALU.mult).then_inc(l.sem, 1))
                    stage(nm + "subsq", dve=sub_sq)

                    def sub_read(l, bank, i):
                        l.did(V.tensor_scalar(sq2[:, i, :], bank, 1.0 / HD, NORM_EPS, ALU.mult, ALU.add).then_inc(l.sem, 1), nm, "subvar", i)

                    def sub_act(l):
                        for i in range(2):
                            l.wait_ge(*past(nm, "subvar", i))
                            l.did(S.activation(rs2[:, i, :], sq2[:, i, :], ACT.Sqrt).then_inc(l.sem, 1), nm, "subsd", i)

                    def sub_dve(l):
                        for i in range(2):
                            l.wait_ge(*past(nm, "subsd", i))
                            l.did(V.reciprocal(rs2[:, i, :], rs2[:, i, :]).then_inc(l.sem, 1))
                            l.wait_ge(*l.own())
                            l.did(V.scalar_tensor_tensor(out=mixT[:, 3 + i, :], in0=mixT[:, 3 + i, :], scalar=gcols[:, 96 + l_:97 + l_],
                                                         in1=rs2[:, i, :], op0=ALU.mult, op1=ALU.mult).then_inc(l.sem, 1))
                        l.wait_ge(*l.own())
                        l.did(V.tensor_scalar(mixT[:, 3:5, :], mixT[:, 3:5, :], 1.0 - lam_init[l_], None, ALU.mult).then_inc(l.sem, 1))
                    products(nm + "sub", [{"by": "dve", "read": (lambda l, b, i=i: sub_read(l, b, i)),
                                           "mms": acc(lambda b: b, [(ones2, sq2[:, i, :])])} for i in range(2)],
                             act_extra=sub_act, dve_extra=sub_dve)

                    sp = region(extra, 2, 1280)
                    wt = region(base.at + 4 * D, 2, 1280)
                    odd_c = region(base.at + 4 * D + 2560, 3, T)
                    qz_c = lambda h: qk[:, 10 + h // 2, :] if h % 2 == 0 else odd_c[:, h // 2, :]

                    def pad_c_pool(l):
                        l.did(G.memset(odd_c[0:64], 0.0).then_inc(l.sem, 1))
                        l.wait_ge(*past(nm, "odd_c"))
                        l.did(G.memset(qk[64:128, 10:13, :], 0.0).then_inc(l.sem, 1))

                    def pad_c_dve(l):
                        l.did(V.tensor_copy(odd_c[64:128], qk[64:128, 10:13, :]).then_inc(l.sem, 1), nm, "odd_c")
                    stage(nm + "padc", pool=pad_c_pool, dve=pad_c_dve)
                    nb = nm + "stick"
                    where = {0: (0, 0, 0), 1: (1, 0, 512), 3: (1, 384, 896), 2: (2, 0, 1024)}
                    full3 = lambda b0: [(banks[:, b0, :], 0), (banks[:, b0 + 1, :], 512), (banks[:, b0 + 2, 0:256], 1024)]

                    def st_pe(l):
                        def zs(i, b0, start_only):
                            for s_ in (0, 1, 3, 2):
                                b, c, _ = where[s_]
                                n = T - s_ * P
                                ins = TE.matmul(banks[:, b0 + b, c:c + n], qk[:, 13 + i // 2, s_ * P:(s_ + 1) * P],
                                                qz_c(i)[:, s_ * P:T], start=True, stop=start_only)
                                if not start_only:
                                    for j in range(s_, NT):
                                        m_ = T - j * P
                                        oj = where[j][2]
                                        ins = TE.matmul(banks[:, b0 + b, c + (j - s_) * P:c + n], sbk[:, 0 if j == s_ else 1, :],
                                                        sp[:, i % 2, oj:oj + m_], start=False, stop=(j == NT - 1))
                            return ins
                        for i in range(6 + 2):
                            if i < 6:
                                if i:
                                    l.wait_ge(*past(nb, "sp", i - 1))
                                l.did(zs(i, 0, True).then_inc(l.sem, 1), nb, "z", i)
                            if i >= 2:
                                h = i - 2
                                po = half(h)
                                l.wait_ge(*past(nb, "w", h))
                                if h >= 2:
                                    l.wait_ge(*past(nb, "o", h - 2))
                                for j in range(NT):
                                    oj = where[j][2]
                                    ins = TE.matmul(banks[po:po + HD, 6 + h % 2, j * P:T], vt[:, j, 640 + h * HD:640 + (h + 1) * HD],
                                                    wt[:, h % 2, oj:oj + T - j * P], start=(j == 0), stop=(j == NT - 1))
                                l.did(ins.then_inc(l.sem, 1), nb, "pv", h)
                            if 1 <= i <= 6:
                                h = i - 1
                                l.wait_ge(*past(nb, "sp", h))
                                if h:
                                    l.wait_ge(*past(nb, "w", h - 1))
                                l.did(zs(h, 3, False).then_inc(l.sem, 1), nb, "zc", h)

                    def st_act(l):
                        for i in range(7):
                            if i < 6:
                                l.wait_ge(*past(nb, "z", i))
                                if i >= 2:
                                    l.wait_ge(*past(nb, "zc", i - 2))
                                for b, o in full3(0):
                                    n = b.shape[1]
                                    l.did(S.activation(sp[:, i % 2, o:o + n], b, ACT.Abs).then_inc(l.sem, 1))
                                l.wait_ge(*l.own())
                                l.did(S.activation(sp[:, i % 2, :], sp[:, i % 2, :], ACT.Exp, scale=-1.0).then_inc(l.sem, 1))
                                l.wait_ge(*l.own())
                                l.did(S.activation(sp[:, i % 2, :], sp[:, i % 2, :], ACT.Ln, bias=1.0).then_inc(l.sem, 1), nb, "ln", i)
                            if i >= 1:
                                h = i - 1
                                l.wait_ge(*past(nb, "clamped", h))
                                l.did(S.activation(wt[:, h % 2, :], wt[:, h % 2, :], ACT.Exp).then_inc(l.sem, 1), nb, "exp", h)
                                if h:
                                    l.wait_ge(*past(nb, "pv", h - 1))
                                    out_copy(l, h - 1)
                        l.wait_ge(*past(nb, "pv", 5))
                        out_copy(l, 5)

                    def out_copy(l, h):
                        po = half(h)
                        l.did(S.activation(mixT[po:po + HD, 5 + h // 2, :], banks[po:po + HD, 6 + h % 2, :], ACT.Copy).then_inc(l.sem, 1), nb, "o", h)

                    def st_dve(l):
                        def mask(buf):
                            for s_ in range(NT):
                                o = where[s_][2]
                                l.did(V.tensor_tensor(buf[:, o:o + P], buf[:, o:o + P], sbk[:, 2, :], ALU.mult).then_inc(l.sem, 1))
                        for i in range(7):
                            if i >= 1:
                                h = i - 1
                                l.wait_ge(*past(nb, "zc", h))
                                if h >= 2:
                                    l.wait_ge(*past(nb, "pv", h - 2))
                                for b, o in full3(3):
                                    n = b.shape[1]
                                    l.did(V.tensor_scalar(wt[:, h % 2, o:o + n], b, 0.0, None, ALU.min).then_inc(l.sem, 1))
                                l.name_last(nb, "clamped", h)
                            if i < 6:
                                l.wait_ge(*past(nb, "ln", i))
                                for b, o in full3(0):
                                    n = b.shape[1]
                                    l.did(V.scalar_tensor_tensor(out=sp[:, i % 2, o:o + n], in0=b, scalar=0.0, in1=sp[:, i % 2, o:o + n],
                                                                 op0=ALU.max, op1=ALU.add).then_inc(l.sem, 1))
                                l.wait_ge(*l.own())
                                mask(sp[:, i % 2, :])
                                l.name_last(nb, "sp", i)
                            if i >= 1:
                                h = i - 1
                                l.wait_ge(*past(nb, "exp", h))
                                mask(wt[:, h % 2, :])
                                l.name_last(nb, "w", h)
                    stage(nb, pe=st_pe, act=st_act, dve=st_dve)

                    wo_src = a["w_out_2"][l_].rearrange("(k p) n -> p k n", p=P)
                    wos = [stream(wo_src[:, :, hf * 512:(hf + 1) * 512], (KD, 512)) for hf in range(2)]

                    def out_pe(l):
                        for hf, (n, w) in enumerate(wos):
                            l.wait_ge(ring_full[n[0] % RING], n[1])
                            for t in range(NT):
                                for k in range(KD):
                                    ins = TE.matmul(banks[:, 2 * t + hf, :], mixT[:, k, t * P:(t + 1) * P], w[:, k, :],
                                                    start=(k == 0), stop=(k == KD - 1))
                            l.did(ins.then_inc(l.sem, 1), nm, "out", hf)
                            l.name_last("freed", n[0])
                    stage(nm + "out", pe=out_pe)
                    if l_ == 0:
                        views["mix0"] = mixT

                between("open", None, None, gcol(0, 0))
                for l_ in range(2):
                    ffn(l_, 0)
                    between(f"mid{l_}a", 0.5, True, gcol(l_, 2), key=f"ffn{l_}0g")
                    mixer(l_)
                    between(f"mid{l_}b", 1.0, True, gcol(l_, 4), key=f"mix{l_}g")
                    ffn(l_, 1)
                    between(f"mid{l_}c", 0.5, True, gcol(1, 0) if l_ == 0 else None, key=f"ffn{l_}1g")
                views["final_x"] = x
                views["xfinal"] = x


            if upto >= 2:
                part_two()
            if upto >= 3:
                part_three()
            if upto >= 4:
                part_four()
            if upto >= 5:
                part_five()
            if me.name == "sp":
                for e in ("pe", "act", "dve", "pool"):
                    me.wait_ge(*past("end", stages[-1], e))
                sends = []
                if upto >= 5:
                    sends.append((out[0].rearrange("(t p) n -> p t n", p=P), views["final_x"]))
                for name in debug or ():
                    v = views[name]
                    shape = [v.shape[i] for i in range(len(v.shape))]
                    sends.append((nc.dram_tensor("dbg_" + name, shape, F32, kind="ExternalOutput").ap(), v))
                for dst, src in sends:
                    me.engine.dma_start(dst, src).then_inc(stored, 16)
                me.wait_ge(stored, 16 * len(sends))

        block = ctx.enter_context(nc.Block())

        @block.sync
        def _(eng):
            program(lanes["sp"])

        @block.tensor
        def _(eng):
            program(pe)

        @block.scalar
        def _(eng):
            program(act)

        @block.vector
        def _(eng):
            program(dve)

        @block.gpsimd
        def _(eng):
            program(pool)
    return marks.now


_INS = ['x', 'c', 'ctx', 'c_ctx', 'w_ada', 'b_ada', 'w_in', 'q_gain', 'k_gain', 'tshift_mu', 'decay_w0',
        'decay_up', 'iclr_a0', 'iclr_up', 'gate_up', 'k_k', 'k_a', 'r_k', 'lnx_g', 'lnx_b', 'w_out', 'ln1_g',
        'ln1_b', 'router_w', 'exp_w_gate', 'exp_w_up', 'exp_w_down', 'ln2_g', 'ln2_b', 'norm_gains_2',
        'w_ffn_gate_2', 'w_ffn_up_2', 'w_ffn_down_2', 'w_in_2', 'w_out_2', 'diff_lambda_2',
        'diff_subln_gain_2']


def kernel(_upto=5, _debug=None, **inputs):
    import numpy as _np
    import concourse.bacc as _bacc
    from concourse.bass_utils import run_bass_kernel_spmd as _run

    known = {}
    for final in (False, True):
        nc = _bacc.Bacc("TRN2", target_bir_lowering=False, num_devices=1)
        arrays, args = {}, {}
        for name in _INS:
            arr = _np.ascontiguousarray(inputs[name])
            arrays[f"in_{name}"] = arr
            args[name] = nc.dram_tensor(f"in_{name}", arr.shape, F32, kind="ExternalInput").ap()
        for name, arr in constants().items():
            arrays[name] = arr
            args[name] = nc.dram_tensor(name, arr.shape, F32, kind="ExternalInput").ap()
        out = nc.dram_tensor("out", (1, T, D), F32, kind="ExternalOutput").ap()
        args["scratch"] = nc.dram_tensor("scratch", (NE, T), F32, kind="Internal").ap()
        known = build(nc, args, out, known, final, _upto, _debug)
    r = _run(nc, [arrays], core_ids=[0])
    return r.results[0]["out"]
```

```python
from contextlib import ExitStack
import math

import numpy as np
import concourse.bass as bass
from concourse import mybir

F32 = mybir.dt.float32
F32R = mybir.dt.float32r
ALU = mybir.AluOpType
ACT = mybir.ActivationFunctionType
AX = mybir.AxisListType

P = 128
D = 1024
KD = D // P
T, TC = 512, 256
NT, NTC = T // P, TC // P
NTA = NT + NTC
NALL = T + TC
HD = 64
NH, NKV = 8, 2
NE, CAP = 16, 64
NRW = 14
FF = 2816
NF = FF // P
ALPHA = 2.0 ** 0.25
LN_EPS, RMS_EPS, GN_EPS, NORM_EPS, L2_EPS = 1e-5, 1e-6, 64e-5, 1e-6, 1e-12
DECAY_K = math.exp(-0.5)
SLOT = 4096
RING = 4
NEG = -1.0e30


def constants():
    t = np.arange(P)
    ident = np.eye(P, dtype=np.float32)
    cum = np.zeros((2, P, 258), np.float32)
    s = t[:, None]
    q = t[None, :]
    mid = 63
    first = (s <= mid) * 1.0
    cum[0, :, 0:128] = (s <= q) * 1.0 - first
    cum[0, :, 128:256] = (s < q) * 1.0 - first
    cum[0, :, 256] = first[:, 0]
    cum[0, :, 257] = 1.0 - first[:, 0]
    last = (s >= P - 1 - mid) * 1.0
    cum[1, :, 0:128] = (s >= q) * 1.0 - last
    cum[1, :, 128:256] = (s > q) * 1.0 - last
    cum[1, :, 256] = last[:, 0]
    cum[1, :, 257] = 1.0 - last[:, 0]
    strict = np.stack([(s < q), (s > q)]).astype(np.float32)
    incl = np.stack([(s <= q), (s >= q)]).astype(np.float32)
    gram = np.concatenate([strict, incl, strict, incl], -1)
    lev = np.zeros((2, P, 7, P), np.float32)
    for i in range(7):
        n = 1 << i
        same = (s // (2 * n)) == (q // (2 * n))
        lev[0, :, i] = same & (s // n < q // n)
        lev[1, :, i] = same & (s // n > q // n)
    ones2 = np.kron(np.eye(2), np.ones((64, 64))).astype(np.float32)
    hsel = np.kron(np.eye(2), np.ones((64, 1))).astype(np.float32)
    pos = np.arange(T)
    inv = (np.float32(10000.0) ** (-np.arange(16, dtype=np.float32) / np.float32(16))).astype(np.float32)
    ang = np.stack([pos // 64, pos % 64], -1).astype(np.float32)[:, :, None] * inv
    rope = np.stack([np.cos(ang), np.sin(ang)], 1).reshape(NT, P, 64).transpose(1, 0, 2).astype(np.float32)
    before = np.zeros((P, NT, T), np.float32)
    for i in range(NT):
        before[:, i] = (np.arange(T)[None, :] < (i * P + t)[:, None])
    slots = np.tile(np.arange(CAP, dtype=np.float32), (P, 1))
    x = np.arange(896)[None, :] - 384
    rel = t[:, None] - x
    mult = np.zeros(rel.shape)
    for w, dil in ((128, 1), (512, 4), (2048, 16)):
        mult += (rel >= 0) & (rel <= w) & (rel % dil == 0)
    lnm = np.where(mult > 0, np.log(np.maximum(mult, 1)), NEG)
    sl = lambda n: 2.0 ** (-8.0 * np.arange(1, n + 1) / n)
    dil = np.stack([np.where(mult > 0, -a * rel + lnm, NEG) for a in sl(6)]).astype(np.float32)
    dif = np.stack([np.where(rel >= 0, -a * rel, NEG) for a in sl(4)]).astype(np.float32)
    bias = np.concatenate([dil, dif])
    sufneg = -(s >= q).astype(np.float32)
    sb = np.stack([sufneg, -np.ones((P, P), np.float32), (s < q).astype(np.float32)], 1)
    rows = np.repeat(np.eye(NE, dtype=np.float32)[:, :, None], P, 2)
    return {"k_rows": rows, "k_ident": ident, "k_cum": cum, "k_gram": gram, "k_lev": lev, "k_ones2": ones2,
            "k_hsel": hsel, "k_rope": rope, "k_before": before, "k_slots": slots,
            "k_bias": np.ascontiguousarray(bias), "k_sb": np.ascontiguousarray(sb)}


class Marks:

    def __init__(self, known, final):
        self.known, self.now, self.final, self.sems = known, {}, final, {}

    def past(self, *key):
        lane, n = self.known.get(key, ("pe", 0))
        assert not self.final or key in self.known, key
        return self.sems[lane], n


class Lane:

    def __init__(self, name, engine, sem, marks):
        self.name, self.engine, self.sem, self.marks = name, engine, sem, marks
        self.wait_ge = engine.wait_ge
        self.n = 0

    def did(self, ins, *key):
        self.n += 1
        if key:
            self.marks.now[key] = (self.name, self.n)

    def name_last(self, *key):
        self.marks.now[key] = (self.name, self.n)

    def own(self):
        return self.sem, self.n


def build(nc, a, out, known, final):
    ctx = ExitStack()
    marks = Marks(known, final)
    with ctx:
        def sem(name):
            return ctx.enter_context(nc.semaphore(name))

        ARENA = 53208
        RING_WORDS = RING * SLOT
        arena_at = (nc.sbuf_base + 31) // 32 * 32
        ring = ctx.enter_context(nc.sbuf_tensor("ring", [P, RING_WORDS], F32))
        arena = ctx.enter_context(nc.sbuf_tensor("arena", [P, ARENA - RING_WORDS], F32))

        twins = {}

        def parts_of(name, off, words):
            if name not in twins:
                twins[name] = nc.alloc_sbuf_tensor_at(name, [P, words], F32R, offset=arena_at + 4 * off)
            t = twins[name]

            def view(at, *shape):
                assert off <= at and at + int(np.prod(shape)) <= off + words
                return shaped(t[:, at - off:at - off + int(np.prod(shape))], shape)
            return view
        banks = ctx.enter_context(nc.psum_tensor("banks", [P, 8, 512], F32))
        used = [0]

        def shaped(ap, shape):
            if len(shape) > 1:
                names = " ".join("abcde"[:len(shape)])
                ap = ap.rearrange(f"p ({names}) -> p {names}", **{k: v for k, v in zip("abcde", shape)})
            return ap

        def region(off, *shape):
            n = int(np.prod(shape))
            if off < RING_WORDS:
                assert off + n <= RING_WORDS, (off, shape)
                return shaped(ring[:, off:off + n], shape)
            assert off + n <= ARENA, (off, shape)
            return shaped(arena[:, off - RING_WORDS:off - RING_WORDS + n], shape)
        ring_r = parts_of("ring_r", 0, RING_WORDS)

        class Stack:
            def __init__(self, at, end=ARENA):
                self.at, self.end = at, end

            def take(self, *shape):
                r = region(self.at, *shape)
                self.at += int(np.prod(shape))
                assert self.at <= self.end, ("arena", self.at, self.end)
                return r

            def branch(self):
                return Stack(self.at, self.end)

        lanes = {}
        for name, eng in (("pe", nc.tensor), ("act", nc.scalar), ("dve", nc.vector), ("pool", nc.gpsimd),
                          ("sp", nc.sync)):
            s = sem(f"{name}_results")
            marks.sems[name] = s
            lanes[name] = Lane(name, eng, s, marks)
        pe, act, dve, pool = (lanes[n] for n in ("pe", "act", "dve", "pool"))
        ring_full = [sem(f"ring_full{i}") for i in range(RING)]
        small_in = [sem(f"small_in{i}") for i in range(40)]
        stored = sem("stored")
        past = marks.past
        V, S, TE, G = nc.vector, nc.scalar, nc.tensor, nc.gpsimd
        views = {"final_x": None}

        def program(l_):
            me = l_
            n_loads, smalls, stages = [0], {}, []
            slot_fills = [0] * RING
            keep = Stack(RING * SLOT)

            def stream_many(parts):
                n = n_loads[0]
                n_loads[0] += 1
                at, views_ = (n % RING) * SLOT, []
                if me.name == "sp" and n >= RING:
                    me.wait_ge(*past("freed", n - RING))
                for shape, src in parts:
                    views_.append(region(at, *shape))
                    at += int(np.prod(shape))
                    if me.name == "sp":
                        me.engine.dma_start(views_[-1], src).then_inc(ring_full[n % RING], 16)
                slot_fills[n % RING] += 16 * len(parts)
                return (n, slot_fills[n % RING]), views_

            def stream(src, shape):
                n, v = stream_many([(shape, src)])
                return n, v[0]

            def hold_stream(after):
                if me.name == "sp":
                    for e in ("pe", "act", "dve", "pool"):
                        me.wait_ge(*past("end", after, e))

            def small(key, pairs, after=None):
                smalls[key] = (small_in[len(smalls)], 16 * len(pairs))
                if me.name == "sp":
                    if after:
                        for e in ("pe", "act", "dve", "pool"):
                            me.wait_ge(*past("end", after, e))
                    for dst, src in pairs:
                        me.engine.dma_start(dst, src).then_inc(smalls[key][0], 16)

            def stage(name, fence=True, **fns):
                if me.name == "sp":
                    stages.append(name)
                    return
                fn = fns.get(me.name)
                if fn is not None:
                    if stages and fence:
                        for other in ("pe", "act", "dve", "pool"):
                            me.wait_ge(*past("end", stages[-1], other))
                    fn(me)
                me.name_last("end", name, me.name)
                stages.append(name)

            def split(l, name, v, unit, depth):
                x_, lo, hi, n = unit
                if l is act:
                    if n is not None:
                        l.wait_ge(ring_full[n[0] % RING], n[1])
                    if v >= depth:
                        l.wait_ge(*past(name, "used", v - depth))
                    l.did(S.activation(hi, x_, ACT.Copy).then_inc(l.sem, 1), name, "hi", v)
                else:
                    l.wait_ge(*past(name, "hi", v))
                    l.did(V.tensor_tensor(lo, x_, hi, ALU.subtract).then_inc(l.sem, 1), name, "lo", v)

            def three(view, parts, start=True, stop=True):
                ms = []
                for (xh_, xl_), (yh_, yl_) in parts:
                    ms += [(xh_, yh_), (xh_, yl_), (xl_, yh_)]
                return [("m", view, x_, y_, start and i == 0, stop and i == len(ms) - 1) for i, (x_, y_) in enumerate(ms)]

            def products(name, groups, act_extra=None, dve_extra=None, pool_fn=None, units=(), depth=2, fence=True, before=None):
                def split_ahead(l, g, done):
                    while done[0] < min(len(units), g.get("unit", -depth) + depth):
                        split(l, name, done[0], units[done[0]], depth)
                        done[0] += 1

                def f_pe(l):
                    for i, g in enumerate(groups):
                        if i >= 8:
                            l.wait_ge(*past(name, "read", i - 8))
                        for n in g.get("loads", ()):
                            l.wait_ge(ring_full[n[0] % RING], n[1])
                        for k in g.get("have", ()):
                            l.wait_ge(*smalls[k])
                        for key in g.get("after", ()):
                            l.wait_ge(*past(*key))
                        if "unit" in g:
                            l.wait_ge(*past(name, "lo", g["unit"]))
                        bank = banks[:, i % 8, :]
                        ms = g["mms"]
                        for j, m in enumerate(ms):
                            if m[0] == "t":
                                ins = TE.transpose(m[1](bank), m[2], m[3])
                            else:
                                ins = TE.matmul(m[1](bank), m[2], m[3], start=m[4], stop=m[5])
                        l.did(ins.then_inc(l.sem, 1), name, "made", i)
                        if "name" in g:
                            l.name_last(*g["name"])
                        if "unit" in g:
                            l.name_last(name, "used", g["unit"])
                        for n in g.get("loads", ()):
                            l.name_last("freed", n[0])
    
                def reader(who):
                    def f(l):
                        done = [0]
                        if before:
                            before(l)
                        for i, g in enumerate(groups):
                            split_ahead(l, g, done)
                            if g.get("first", (None,))[0] == who:
                                l.wait_ge(*past(name, "made", i))
                                g["first"][1](l, banks[:, i % 8, :])
                            if g["by"] == who:
                                l.wait_ge(*past(name, "made", i))
                                g["read"](l, banks[:, i % 8, :])
                                l.name_last(name, "read", i)
                            if who == "dve" and "then" in g:
                                g["then"](l)
                        extra = act_extra if who == "act" else dve_extra
                        if extra:
                            extra(l)
                    return f
                stage(name, fence=fence, pe=f_pe, act=reader("act"), dve=reader("dve"), pool=pool_fn)

            def copy_out(dst, view=lambda b: b):
                def read(l, bank):
                    if l is act:
                        l.did(S.activation(dst, view(bank), ACT.Copy).then_inc(l.sem, 1))
                    else:
                        l.did(V.tensor_copy(dst, view(bank)).then_inc(l.sem, 1))
                return read
    
            def acc(view, pairs):
                n = len(pairs)
                return [("m", view, x, y, i == 0, i == n - 1) for i, (x, y) in enumerate(pairs)]
    
            def halves(i):
                return "act" if i % 2 else "dve"

            ident = keep.take(P)
            ones = keep.take(P)
            mixT_at = keep.at
            mixT = keep.take(8, T)
            small("const", [(ident, a["k_ident"])])
            gt1 = keep.take(D)
            gt2 = keep.take(D)
            modcol = keep.take(48, 2)
            stats = keep.take(256)
            base = keep.branch()

            def norm_stage(name, src, dst, tiles, need, affine=None, into=None):
                st = stats[:, 0:tiles * 12].rearrange("p (a b c) -> p a b c", b=2, c=6)
                mv = stats[:, 80:80 + 2 * tiles].rearrange("p (a b) -> p a b", b=2)
                sd = stats[:, 100:100 + tiles]
                rs = stats[:, 110:110 + tiles]

                def f_dve(l):
                    for k in need:
                        l.wait_ge(*smalls[k])
                    for i in range(tiles):
                        for hf in range(2):
                            l.did(V.bn_stats(st[:, i, hf, :], src(i)[:, hf * 512:(hf + 1) * 512]).then_inc(l.sem, 1))
                    l.wait_ge(*l.own())
                    for i in range(tiles):
                        l.did(V.bn_aggr(mv[:, i, :], st[:, i, :, :]).then_inc(l.sem, 1))
                    l.wait_ge(*l.own())
                    l.did(V.tensor_scalar(sd, mv[:, :, 1], LN_EPS, None, ALU.add).then_inc(l.sem, 1), name, "var")
                    l.wait_ge(*past(name, "sd"))
                    l.did(V.reciprocal(rs, rs).then_inc(l.sem, 1))
                    l.wait_ge(*l.own())
                    for i in range(tiles):
                        l.did(V.tensor_scalar(dst(i), src(i), mv[:, i, 0:1], rs[:, i:i + 1], ALU.subtract, ALU.mult).then_inc(l.sem, 1))
                    if affine:
                        g, b = affine
                        l.wait_ge(*l.own())
                        for i in range(tiles):
                            l.did(V.tensor_tensor(dst(i), dst(i), g, ALU.mult).then_inc(l.sem, 1), name, "gained", i)

                def f_act(l):
                    l.wait_ge(*past(name, "var"))
                    l.did(S.activation(rs, sd, ACT.Sqrt).then_inc(l.sem, 1), name, "sd")

                def f_pool(l):
                    if affine:
                        for i in range(tiles):
                            l.wait_ge(*past(name, "gained", i))
                            l.did(G.tensor_tensor(dst(i), dst(i), affine[1], ALU.add).then_inc(l.sem, 1))
                stage(name, dve=f_dve, act=f_act, pool=f_pool)

            m = base.branch()
            hT = m.take(KD, NALL)
            m = base.branch()
            c16, sil, sg16 = m.take(P), m.take(16), m.take(16)
            modrow, brow = m.take(6 * D), m.take(6 * D)
            small("mod", [(c16[0:8, :], a["c"].rearrange("o (k p) -> (o k) p", p=P)),
                          (c16[8:16, :], a["c_ctx"].rearrange("(k p) -> k p", p=P)),
                          (brow[0:1, :], a["b_ada"]), (brow[1:2, :], a["b_ada"])])

            xc = m.take(NTA, D)
            xn = m.take(NTA, D)
            small("x", [(xc[:, 0:NT, :], a["x"][0].rearrange("(t p) n -> p t n", p=P)),
                        (xc[:, NT:NTA, :], a["ctx"][0].rearrange("(t p) n -> p t n", p=P))])

            def silu_c_read(l, bank):
                l.did(S.activation(sg16, bank[:, 0:16], ACT.Sigmoid).then_inc(l.sem, 1), "silu_c")

            def silu_c(l):
                l.wait_ge(*past("silu_c"))
                l.did(V.tensor_tensor(sil, banks[:, 0, 0:16], sg16, ALU.mult).then_inc(l.sem, 1))

            def fill_ones(l):
                l.did(G.memset(ones, 1.0).then_inc(l.sem, 1))
            products("c_T", [{"have": ("mod", "const"), "by": "act", "read": silu_c_read,
                              "mms": [("t", lambda b: b[:, 0:16], c16[0:16, :], ident[0:16, 0:16])]}],
                     dve_extra=silu_c, pool_fn=fill_ones)
            silv = sil.rearrange("p (v k) -> p k v", k=KD)
            w_ada = a["w_ada"][0].rearrange("(k p) n -> p k n", p=P)
            groups = []
            for n in range(12):
                ln, w = stream(w_ada[:, :, n * 512:(n + 1) * 512], (KD, 512))
                cs = slice(n * 512, (n + 1) * 512)

                def read(l, bank, cs=cs):
                    l.did(V.tensor_tensor(modrow[0:2, cs], bank[0:2, :], brow[0:2, cs], ALU.add).then_inc(l.sem, 1))
                groups.append({"loads": [ln], "by": "dve", "read": read,
                               "mms": acc(lambda b: b[0:2, :], [(silv[:, k, :], w[:, k, :]) for k in range(KD)])})
            norm_stage("norm1", lambda i: xc[:, i, :], lambda i: xn[:, i, :], NTA, ["x"])
            groups[0]["after"] = [("end", "c_T", "dve")]
            products("mod_rows", groups, fence=False)

            def modcol_read(l, bank):
                l.did(V.tensor_copy(modcol, bank[:, 0:96].rearrange("p (a b) -> p a b", b=2)).then_inc(l.sem, 1))
                l.wait_ge(*l.own())
                for j in (8, 32):
                    l.did(V.tensor_scalar(modcol[:, j:j + 8, :], modcol[:, j:j + 8, :], 1.0, None, ALU.add).then_inc(l.sem, 1))
            groups = [{"by": "dve", "read": modcol_read,
                       "mms": [("t", (lambda b, j=j: b[:, 2 * j:2 * j + 2]), modrow[0:2, j * P:(j + 1) * P],
                                ident[0:2, 0:2]) for j in range(48)]}]
            for dst, j in ((gt1, 2), (gt2, 5)):
                for hf in range(2):
                    groups.append({"by": "act", "read": copy_out(dst[:, hf * 512:(hf + 1) * 512]),
                                   "mms": acc(lambda b: b, [(ones[0:1, :], modrow[0:1, j * D + hf * 512:j * D + hf * 512 + 512])])})
            products("mod_cols", groups)

            def transpose_groups(src, dst_of, n_tiles, tile0, nk, col=None, width=P):
                gs = []
                for k in range(nk):
                    def read(l, bank, k=k):
                        v = bank[:, 0:n_tiles * P]
                        if col is None:
                            if l is act:
                                l.did(S.activation(dst_of(k), v, ACT.Copy).then_inc(l.sem, 1))
                            else:
                                l.did(V.tensor_copy(dst_of(k), v).then_inc(l.sem, 1))
                        else:
                            sc, sh = col(k)
                            if l is act:
                                l.did(S.activation(dst_of(k), v, ACT.Identity, bias=sh, scale=sc).then_inc(l.sem, 1))
                            else:
                                l.did(V.tensor_scalar(dst_of(k), v, sc, sh, ALU.mult, ALU.add).then_inc(l.sem, 1))
                    gs.append({"by": halves(k), "read": read, "mms": [
                        ("t", (lambda b, i=i: b[:, i * P:(i + 1) * P]), src(tile0 + i)[:, k * P:(k + 1) * P], ident)
                        for i in range(n_tiles)]})
                return gs

            products("h_T",
                     transpose_groups(lambda i: xn[:, i, :], lambda k: hT[:, k, 0:T], NT, 0, KD,
                                      lambda k: (modcol[:, 8 + k, 0:1], modcol[:, k, 0:1])) +
                     transpose_groups(lambda i: xn[:, i, :], lambda k: hT[:, k, T:NALL], NTC, NT, KD,
                                      lambda k: (modcol[:, 8 + k, 1:2], modcol[:, k, 1:2])))

            m = base.branch()
            w_in_hT = m.at
            hT = m.take(KD, NALL)
            cols = m.take(64)
            sft = m.take(NRW, NALL)
            qkv = m.take(NT, 768)
            kvc = m.take(NTC, 256)
            after_proj = m.branch()
            pb = m.take(2, 772)
            tmp = m.take(2, NALL)
            omu, hmu = m.take(NRW), m.take(NRW)
            rows = m.take(P)
            vec = lambda ap: ap.rearrange("(k p) -> k p", p=P)
            small("cols", [(rows[0:14, :], vec(a["tshift_mu"][0])), (rows[14:18, :], vec(a["k_k"][0])),
                           (rows[18:22, :], vec(a["k_a"][0])),
                           (rows[22:26, :], a["r_k"][0].rearrange("(k h) n -> k (h n)", h=2)),
                           (rows[26:34, :], a["iclr_a0"][0].rearrange("d (k p) -> (d k) p", p=P))], after="h_T")

            def pad_zero(l):
                for i in range(2):
                    for c in (0, 513, 514, 771):
                        l.did(G.memset(pb[:, i, c:c + 1], 0.0).then_inc(l.sem, 1))

            def cols_read(l, bank):
                l.did(V.tensor_copy(cols[:, 0:34], bank[:, 0:34]).then_inc(l.sem, 1))
                l.wait_ge(*l.own())
                l.did(V.tensor_scalar(omu, cols[:, 0:NRW], -1.0, 1.0, ALU.mult, ALU.add).then_inc(l.sem, 1))
                l.did(V.tensor_scalar(hmu, cols[:, 0:NRW], 0.5, None, ALU.mult).then_inc(l.sem, 1))
                l.wait_ge(*l.own())
            products("cols", [{"have": ("cols",), "by": "dve", "read": cols_read,
                               "mms": [("t", lambda b: b[:, 0:34], rows[0:34, :], ident[0:34, 0:34])]}],
                     pool_fn=pad_zero)
            w_in = a["w_in"][0].rearrange("(k p) n -> p k n", p=P)
            ws = [stream(w_in[:, :, s * 512:(s + 1) * 512], (KD, 512)) for s in range(5)]
            in_mix_r, in_hT_r = parts_of("mix_r", mixT_at, KD * T), parts_of("in_hT_r", w_in_hT, KD * NALL)
            m.at += -m.at % 8
            in_r = parts_of("in_r", m.at, KD * TC + 4096)
            ctx_hi = in_r(m.at, KD, TC)
            m.take(KD, TC)
            hi_at = m.at
            m.take(2, 2048)
            h_lo = in_hT_r(w_in_hT, KD, NALL)
            h_hi_of = lambda k, t0, t1: (in_mix_r(mixT_at, KD, T)[:, k, t0:t1] if t1 <= T else ctx_hi[:, k, t0 - T:t1 - T])
            h_parts = lambda k, t0, t1: (h_hi_of(k, t0, t1), h_lo[:, k, t0:t1])

            def split_h(l):
                for i in range(4):
                    ks = slice(2 * i, 2 * i + 2)
                    for j, (t0, t1, hi) in enumerate(((0, T, in_mix_r(mixT_at, KD, T)), (T, NALL, ctx_hi))):
                        split(l, "w_in_h", 2 * i + j, (hT[:, ks, t0:t1], h_lo[:, ks, t0:t1], hi[:, ks, :], None), 2 * KD)
            groups, units = [], []

            def unit(c0, width):
                n = ws[c0 // 512][0]
                o, at_, u = c0 % 512, (n[0] % RING) * SLOT, len(units)
                hi = in_r(hi_at + (u % 2) * 2048, KD, width)
                lo = ring_r(at_, KD, 512)[:, :, o:o + width]
                units.append((region(at_, KD, 512)[:, :, o:o + width], lo, hi, n))
                return u, hi, lo, n
            for c0 in (0, 256, 512):
                u, hi, lo, n = unit(c0, 256)
                for t in range(NTA if c0 == 512 else NT):
                    dst = qkv[:, t, c0:c0 + 256] if t < NT else kvc[:, t - NT, :]
                    groups.append({"loads": [n], "unit": u, "by": "act", "read": copy_out(dst, lambda b: b[:, 0:256]),
                                   "mms": three(lambda b: b[:, 0:256], [
                                       (h_parts(k, t * P, (t + 1) * P), (hi[:, k, :], lo[:, k, :])) for k in range(KD)])})
            groups[0]["after"] = [("w_in_h", "lo", 7)]
            for j in range(NRW):
                u, hi, lo, n = unit(768 + j * P, P)
                for t0, t1, o in ((0, T, 1), (T, NALL, 3)):
                    def read(l, bank, j=j, t0=t0, t1=t1, o=o):
                        if j >= 2 and t0 == 0:
                            l.wait_ge(*past("shifted", j - 2))
                        l.did(S.activation(pb[:, j % 2, t0 + o:t1 + o], bank[:, 0:t1 - t0], ACT.Copy).then_inc(l.sem, 1),
                              "projected", j, t0)
                    groups.append({"loads": [n], "unit": u, "by": "act", "read": read,
                                   "mms": three(lambda b, n=t1 - t0: b[:, 0:n], [
                                       ((hi[:, k, :], lo[:, k, :]), h_parts(k, t0, t1)) for k in range(KD)])})
                groups[-1]["then"] = lambda l, j=j: shift(l, j)

            def shift(l, j):
                l.wait_ge(*past("projected", j, T))
                p, tt = pb[:, j % 2, :], tmp[:, j % 2, :]
                for t0, t1, o in ((0, T, 1), (T, NALL, 3)):
                    l.did(V.tensor_tensor(tt[:, t0:t1], p[:, t0 + o - 1:t1 + o - 1], p[:, t0 + o + 1:t1 + o + 1], ALU.add).then_inc(l.sem, 1))
                l.wait_ge(*l.own())
                l.did(V.tensor_scalar(tt, tt, hmu[:, j:j + 1], None, ALU.mult).then_inc(l.sem, 1))
                l.wait_ge(*l.own())
                for t0, t1, o in ((0, T, 1), (T, NALL, 3)):
                    l.did(V.scalar_tensor_tensor(out=sft[:, j, t0:t1], in0=p[:, t0 + o:t1 + o], scalar=omu[:, j:j + 1],
                                                 in1=tt[:, t0:t1], op0=ALU.mult, op1=ALU.add).then_inc(l.sem, 1), "shifted", j)
            products("w_in", groups, units=units, before=split_h)

            def attention(name, heads, width, score, val, dst, scale, bufs, bias=None, lam=None, need=()):
                units = [(i, h, t) for i, h in enumerate(heads) for t in range(NT)]
                sbs, pt, st = bufs
                NB = len(sbs)
                sb = lambda u: sbs[u % NB]
                lag = 2 if NB == 3 else 3
                nset = 2 if lam is not None else 1
                full = width(0) == width(NT - 1)
                n_key = [width(t) // P for t in range(NT)]

                def sbank(u, s):
                    if nset == 1 and not full:
                        return u % 4
                    return (u % 2) * 2 + s
                tb_of, cnt = {}, 0
                for u, (i, h, t) in enumerate(units):
                    for g in range((n_key[t] + 3) // 4):
                        tb_of[u, g] = (4 + cnt % 3, cnt)
                        cnt += 1
                by_cnt = {c: ug for ug, (_, c) in tb_of.items()}

                def sc_view(u, s, w):
                    if w > 512:
                        return banks[:, sbank(u, 0):sbank(u, 0) + 2, :].rearrange("p a b -> p (a b)")[:, 0:w]
                    return banks[:, sbank(u, s), 0:w]

                def f_pe(l):
                    for k in need:
                        l.wait_ge(*smalls[k])

                    def turn(u):
                        i, h, t = units[u]
                        l.wait_ge(*past(name, "P", u))
                        for g in range((n_key[t] + 3) // 4):
                            b, c = tb_of[u, g]
                            if c >= 3:
                                l.wait_ge(*past(name, "T", *by_cnt[c - 3]))
                            for j in range(4 * g, min(4 * g + 4, n_key[t])):
                                ins = TE.transpose(banks[:, b, (j - 4 * g) * P:(j - 4 * g + 1) * P],
                                                   sb(u)[:, j * P:(j + 1) * P], ident)
                            l.did(ins.then_inc(l.sem, 1), name, "turned", u, g)

                    def values(u):
                        i, h, t = units[u]
                        if t == NT - 1:
                            if i >= 1:
                                l.wait_ge(*past(name, "out", i - 1))
                            for g in range((n_key[t] + 3) // 4):
                                l.wait_ge(*past(name, "T", u, g))
                            po = HD * (h % 2)
                            for j in range(n_key[t]):
                                q0 = 0 if full else j * P
                                ins = TE.matmul(banks[po:po + HD, 7, q0:T], val(h, j), pt[:, i % 2, j, q0:T],
                                                start=(j == 0), stop=(j == n_key[t] - 1))
                            l.did(ins.then_inc(l.sem, 1), name, "pv", i)
                    ahead = 4 if nset == 1 and not full else 2
                    for u in range(len(units) + lag + 1):
                        if u < len(units):
                            i, h, t = units[u]
                            if u >= ahead:
                                l.wait_ge(*past(name, "max" if bias is not None else "E", u - ahead))
                            for s, pieces in enumerate(score(h, t)):
                                w = width(t)
                                for q, k, c, n in pieces:
                                    ins = TE.matmul(sc_view(u, s, w)[:, c:c + n], q, k, start=True, stop=True)
                            l.did(ins.then_inc(l.sem, 1), name, "S", u)
                        if lag <= u < len(units) + lag:
                            turn(u - lag)
                        if u > lag:
                            values(u - lag - 1)

                def f_dve(l):
                    def finish(u):
                        i, h, t = units[u]
                        w = width(t)
                        l.wait_ge(*past(name, "E", u))
                        c = st[:, u % NB, :]
                        l.did(V.reciprocal(c[:, 4:4 + nset], c[:, 2:2 + nset]).then_inc(l.sem, 1))
                        l.wait_ge(*l.own())
                        p1 = sb(u)[:, 0:w]
                        if nset == 2:
                            p2 = sb(u)[:, 512:512 + w]
                            l.did(V.tensor_tensor(c[:, 5:6], c[:, 5:6], lam, ALU.mult).then_inc(l.sem, 1))
                            l.did(V.tensor_scalar(p1, p1, c[:, 4:5], None, ALU.mult).then_inc(l.sem, 1))
                            l.wait_ge(*l.own())
                            l.did(V.scalar_tensor_tensor(out=p1, in0=p2, scalar=c[:, 5:6], in1=p1,
                                                         op0=ALU.mult, op1=ALU.add).then_inc(l.sem, 1), name, "P", u)
                        else:
                            l.did(V.tensor_scalar(p1, p1, c[:, 4:5], None, ALU.mult).then_inc(l.sem, 1), name, "P", u)
                    for u in range(len(units) + 1):
                        if u < len(units):
                            i, h, t = units[u]
                            w = width(t)
                            l.wait_ge(*past(name, "S", u))
                            c = st[:, u % NB, :]
                            if u >= NB:
                                l.wait_ge(*past(name, "turned", u - NB, (n_key[units[u - NB][2]] + 3) // 4 - 1))
                            for s in range(nset):
                                v = sc_view(u, s, w)
                                if bias is not None:
                                    x = sb(u)[:, 512 * s:512 * s + w]
                                    l.did(V.scalar_tensor_tensor(out=x, in0=v, scalar=scale, in1=bias(h, t),
                                                                 op0=ALU.mult, op1=ALU.add).then_inc(l.sem, 1))
                                    l.wait_ge(*l.own())
                                    v = x
                                l.did(V.reduce_max(c[:, s:s + 1], v, axis=AX.X).then_inc(l.sem, 1))
                            l.wait_ge(*l.own())
                            l.did(V.tensor_scalar(c[:, 0:nset], c[:, 0:nset], -1.0 if bias is not None else -scale,
                                                  None, ALU.mult).then_inc(l.sem, 1), name, "max", u)
                        if u >= 1:
                            finish(u - 1)

                def f_act(l):
                    def evac(u):
                        i, h, t = units[u]
                        for g in range((n_key[t] + 3) // 4):
                            l.wait_ge(*past(name, "turned", u, g))
                            if i >= 2:
                                l.wait_ge(*past(name, "pv", i - 2))
                            m_ = min(4, n_key[t] - 4 * g)
                            l.did(S.activation(pt[:, i % 2, 4 * g:4 * g + m_, t * P:(t + 1) * P],
                                               banks[:, tb_of[u, g][0], 0:m_ * P].rearrange("p (a b) -> p a b", b=P),
                                               ACT.Copy).then_inc(l.sem, 1), name, "T", u, g)

                    def out_(u):
                        i, h, t = units[u]
                        if t == NT - 1:
                            l.wait_ge(*past(name, "pv", i))
                            po = HD * (h % 2)
                            l.did(S.activation(dst(h), banks[po:po + HD, 7, :], ACT.Copy).then_inc(l.sem, 1), name, "out", i)
                    for u in range(len(units) + lag + 1):
                        if u < len(units):
                            i, h, t = units[u]
                            w = width(t)
                            l.wait_ge(*past(name, "max", u))
                            c = st[:, u % NB, :]
                            for s in range(nset):
                                src = sb(u)[:, 512 * s:512 * s + w] if bias is not None else sc_view(u, s, w)
                                l.did(S.activation(sb(u)[:, 512 * s:512 * s + w], src, ACT.Exp,
                                                   bias=c[:, s:s + 1], scale=1.0 if bias is not None else scale,
                                                   accum_out=c[:, 2 + s:3 + s]).then_inc(l.sem, 1))
                            l.name_last(name, "E", u)
                        if lag <= u < len(units) + lag:
                            evac(u - lag)
                        if u > lag:
                            out_(u - lag - 1)
                stage(name, pe=f_pe, act=f_act, dve=f_dve)

            def part_two():
                hole = Stack(base.at, base.at + KD * NALL)
                m2 = after_proj.branch()
                sb_at = m2.at
                gain = m2.take(640)
                rope = m2.take(NT, 64)
                kdup = m2.take(NTA, 2, 128)
                rms = m2.take(3, 44)
                qz = m2.take(NH, T)
                kT = m2.take(2, NALL)
                sbs = [region(sb_at + i * NALL, NALL) for i in range(3)]
                st = m2.take(3, 8)
                ptb = hole.branch().take(2, NTA, T)
                hh = hole.branch()
                sq = hh.take(NT, 640)
                sqc = hh.take(NTC, 128)
                r1, r2, r3, r4 = (hh.take(10, 2, 16) for _ in range(4))
                gs = [(gain[:, h * HD:(h + 1) * HD], a["q_gain"].to_broadcast([P, HD])) for h in range(NH)]
                gs += [(gain[:, h * HD:(h + 1) * HD], a["k_gain"].to_broadcast([P, HD])) for h in range(NH, NH + NKV)]
                small("qk", gs + [(rope, a["k_rope"])], after="w_in")
                heads10 = lambda ap: ap.rearrange("p (h n) -> p h n", n=HD)

                def qk_dve(l):
                    l.wait_ge(*smalls["qk"])
                    for t in range(NT):
                        l.did(V.tensor_tensor(sq[:, t, :], qkv[:, t, 0:640], qkv[:, t, 0:640], ALU.mult).then_inc(l.sem, 1))
                    for t in range(NTC):
                        l.did(V.tensor_tensor(sqc[:, t, :], kvc[:, t, 0:128], kvc[:, t, 0:128], ALU.mult).then_inc(l.sem, 1))
                    l.wait_ge(*l.own())
                    for t in range(NT):
                        l.did(V.reduce_sum(rms[:, 0, 10 * t:10 * t + 10], heads10(sq[:, t, :]), axis=AX.X).then_inc(l.sem, 1))
                    l.did(V.reduce_sum(rms[:, 0, 40:44], heads10(sqc.rearrange("p a b -> p (a b)")), axis=AX.X).then_inc(l.sem, 1))
                    l.wait_ge(*l.own())
                    l.did(V.tensor_scalar(rms[:, 1, :], rms[:, 0, :], 1.0 / HD, RMS_EPS, ALU.mult, ALU.add).then_inc(l.sem, 1), "qk_var")
                    l.wait_ge(*past("qk_sd"))
                    l.did(V.reciprocal(rms[:, 0, :], rms[:, 2, :]).then_inc(l.sem, 1))
                    l.wait_ge(*l.own())
                    for t in range(NT):
                        v = heads10(qkv[:, t, 0:640])
                        l.did(V.tensor_tensor(v, v, rms[:, 0, 10 * t:10 * t + 10].unsqueeze(2).to_broadcast([P, 10, HD]), ALU.mult).then_inc(l.sem, 1))
                    for t in range(NTC):
                        v = heads10(kvc[:, t, 0:128])
                        l.did(V.tensor_tensor(v, v, rms[:, 0, 40 + 2 * t:42 + 2 * t].unsqueeze(2).to_broadcast([P, 2, HD]), ALU.mult).then_inc(l.sem, 1))
                    l.wait_ge(*l.own())
                    for t in range(NT):
                        l.did(V.tensor_tensor(qkv[:, t, 0:640], qkv[:, t, 0:640], gain, ALU.mult).then_inc(l.sem, 1))
                    for t in range(NTC):
                        l.did(V.tensor_tensor(kvc[:, t, 0:128], kvc[:, t, 0:128], gain[:, 512:640], ALU.mult).then_inc(l.sem, 1))
                    l.wait_ge(*l.own())
                    for t in range(NT):
                        v = qkv[:, t, 0:640].rearrange("p (h x y e) -> p h x y e", h=10, x=2, y=2)
                        t1, t2 = v[:, :, :, 0, :], v[:, :, :, 1, :]
                        tab = rope[:, t, :].rearrange("p (y x e) -> p y x e", y=2, x=2)
                        cs = tab[:, 0].unsqueeze(1).to_broadcast([P, 10, 2, 16])
                        sn = tab[:, 1].unsqueeze(1).to_broadcast([P, 10, 2, 16])
                        l.did(V.tensor_tensor(r1, t1, cs, ALU.mult).then_inc(l.sem, 1))
                        l.did(V.tensor_tensor(r2, t2, sn, ALU.mult).then_inc(l.sem, 1))
                        l.did(V.tensor_tensor(r3, t2, cs, ALU.mult).then_inc(l.sem, 1))
                        l.did(V.tensor_tensor(r4, t1, sn, ALU.mult).then_inc(l.sem, 1))
                        l.wait_ge(*l.own())
                        l.did(V.tensor_tensor(t1, r1, r2, ALU.subtract).then_inc(l.sem, 1))
                        l.did(V.tensor_tensor(t2, r3, r4, ALU.add).then_inc(l.sem, 1))
                        l.wait_ge(*l.own())
                    for t in range(NTA):
                        src = qkv[:, t, 512:640] if t < NT else kvc[:, t - NT, 0:128]
                        for e in range(2):
                            l.did(V.tensor_copy(kdup[:, t, :, e * HD:(e + 1) * HD], heads10(src)).then_inc(l.sem, 1))

                def qk_act(l):
                    l.wait_ge(*past("qk_var"))
                    l.did(S.activation(rms[:, 2, :], rms[:, 1, :], ACT.Sqrt).then_inc(l.sem, 1), "qk_sd")
                stage("qk_norm", dve=qk_dve, act=qk_act)
                gs = []
                for k in range(4):
                    def read(l, bank, k=k):
                        for h in range(2):
                            hs = slice(64 * h, 64 * h + 64)
                            copy_out(qz[hs, 2 * k + h, :], lambda b, hs=hs: b[hs, :])(l, bank)
                    gs.append({"by": halves(k), "read": read, "mms": [
                        ("t", (lambda b, t=t: b[:, t * P:(t + 1) * P]), qkv[:, t, k * P:(k + 1) * P], ident)
                        for t in range(NT)]})

                def zero_q(l):
                    for h in range(NH):
                        z = 64 - 64 * (h % 2)
                        l.did(G.memset(qz[z:z + 64, h, :], 0.0).then_inc(l.sem, 1))
                gs += transpose_groups(lambda t: kdup[:, t].rearrange("p a b -> p (a b)"), lambda k: kT[:, k, 0:T], NT, 0, 2)
                gs += transpose_groups(lambda t: kdup[:, t].rearrange("p a b -> p (a b)"), lambda k: kT[:, k, T:NALL], NTC, NT, 2)
                products("qk_T", gs, pool_fn=zero_q)

                def score(h, t):
                    q = qz[:, h, t * P:(t + 1) * P]
                    g = h // (NH // NKV)
                    return [[(q, kT[:, g, 0:512], 0, 512), (q, kT[:, g, 512:768], 512, 256)]]

                def val(h, j):
                    g = h // (NH // NKV)
                    src = qkv[:, j, 640:768] if j < NT else kvc[:, j - NT, 128:256]
                    return src[:, g * HD:(g + 1) * HD]
                attention("attend", list(range(NH)), lambda t: NALL, score, val,
                          lambda h: mixT[HD * (h % 2):HD * (h % 2) + HD, h // 2, :], HD ** -0.5, (sbs, ptb, st))

            wos = []

            def part_three():
                low = Stack(0, RING * SLOT)
                hole = Stack(base.at, base.at + KD * NALL)
                sft_at = base.at + KD * NALL + 64
                high = after_proj.branch()
                high.at -= NT * 768 + NTC * 256
                R, K_, V_ = 0, 4, 8
                CELLS = 8
                masks = low.take(2, 512)
                levm = low.take(2, 7, P)
                cum = low.take(2, 258)
                ones2 = low.take(P)
                hsel = low.take(2)
                w0 = low.take(2, 512)
                upd, upi = low.take(2, 512), low.take(2, 512)
                low_cells = [low.take(512) for _ in range(3)]
                big = low.branch()
                vtm = hole.take(NTA, 4, 192)
                window = lambda v, q, h: v[:, q % 4, 64 * h:64 * h + 128]
                both = lambda v: v.rearrange("p q (x c) -> p q x c", x=3)[:, :, 0::2, :]
                ytm = high.take(NT, 512)
                bonus = high.take(NT, 8)
                kkn = high.take(4, NALL)
                RA = high.take(CELLS, 256)
                XT = high.take(CELLS, 2, 256)
                ends = high.take(2, 8)
                end_old = high.take(2, 4)
                hop = high.take(2, 4)
                vdead = Stack(sft_at + V_ * NALL, sft_at + 12 * NALL)
                BKt = vdead.take(CELLS, 2, P)
                state = vdead.take(2, 4, P)
                Am = region(RING * SLOT + 2 * P + 4 * T, CELLS, 2, P)
                U_ = region(RING * SLOT + 2 * P + 4 * T, 2, 4, 192)
                cells_from = hole.at
                W_ = region(cells_from, 2, 4, 192)
                sum_at = high.at
                cell_at = [hole.take(512) for _ in range(3)] + [high.take(512) for _ in range(2)] + low_cells
                BKz = lambda q, h: cell_at[q][:, h * 256:(h + 1) * 256]
                P1 = lambda q: cell_at[q][:, 0:256]
                Al = lambda q: cell_at[q][:, 256:512]
                Gm = big.take(CELLS, 2, 512)
                pre = Stack(big.at - CELLS * 2 * 512)
                sw, aa = pre.take(2, 512), pre.take(2, 4, P)
                kd, bb = pre.take(2, 4, P), pre.take(2, 4, P)
                E1, Em, E0 = pre.take(2, 4, P), pre.take(2, 4, P), pre.take(2, 4, P)
                order = [[4, 5, 0, 1, 2, 3], [5, 4, 3, 2, 1, 0]]
                small("rwkv", [(masks, a["k_gram"].rearrange("d p n -> p d n")),
                               (levm, a["k_lev"].rearrange("d p l n -> p d l n")),
                               (cum, a["k_cum"].rearrange("d p n -> p d n")),
                               (ones2, a["k_ones2"]), (hsel, a["k_hsel"]),
                               (w0[:, 0, :], a["decay_w0"][0, 0:1, :].to_broadcast([P, 512])),
                               (w0[:, 1, :], a["decay_w0"][0, 1:2, :].to_broadcast([P, 512])),
                               (upd[0:64], a["decay_up"][0].rearrange("d p n -> p d n")),
                               (upi[64:128], a["iclr_up"][0].rearrange("d p n -> p d n"))], after="attend")
                rkx = region(big.at - CELLS * 2 * 512 + 4 * NALL, 4, T)
                sq = region(big.at - CELLS * 2 * 512, 4, NALL)

                def gates(l):
                    l.did(S.activation(sft[0:64, 12, :], sft[0:64, 12, :], ACT.Tanh).then_inc(l.sem, 1))
                    l.did(S.activation(sft[:, 13, 0:T], sft[:, 13, 0:T], ACT.Sigmoid).then_inc(l.sem, 1))

                def gates_dve(l):
                    for j in range(4):
                        l.did(V.scalar_tensor_tensor(out=rkx[:, j, :], in0=sft[:, R + j, 0:T], scalar=cols[:, 22 + j:23 + j],
                                                     in1=sft[:, K_ + j, 0:T], op0=ALU.mult, op1=ALU.mult).then_inc(l.sem, 1))
                        l.did(V.tensor_scalar(kkn[:, j, :], sft[:, K_ + j, :], cols[:, 14 + j:15 + j], None, ALU.mult)
                              .then_inc(l.sem, 1))
                    l.wait_ge(*l.own())
                    l.did(V.tensor_tensor(sq, kkn, kkn, ALU.mult).then_inc(l.sem, 1))

                def gates_pool(l):
                    l.did(G.memset(upd[64:128], 0.0).then_inc(l.sem, 1))
                    l.did(G.memset(upi[0:64], 0.0).then_inc(l.sem, 1))
                stage("rwkv_gates", act=gates, dve=gates_dve, pool=gates_pool)
                gs = []
                for j in range(4):
                    for t0, t1 in ((0, T), (T, NALL)):
                        def read(l, bank, j=j, t0=t0, t1=t1):
                            l.did(V.tensor_scalar(sq[:, j, t0:t1], bank[:, 0:t1 - t0], L2_EPS ** 2, None, ALU.max).then_inc(l.sem, 1),
                                  "kk_squares")
                        gs.append({"by": "dve", "read": read, "have": ("rwkv",),
                                   "mms": acc(lambda b, n=t1 - t0: b[:, 0:n], [(ones2, sq[:, j, t0:t1])])})
                for t in range(NTA):
                    gs.append({"by": "dve", "read": copy_out(both(vtm[:, t]), lambda b: b.rearrange("p (q x c) -> p q x c", q=4, x=2)),
                               "mms": [("t", (lambda b, j=j: b[:, j * P:(j + 1) * P]),
                                        sft[:, V_ + j, t * P:(t + 1) * P], ident) for j in range(4)]})
                for t in range(NT):
                    gs.append({"by": "dve", "read": copy_out(bonus[:, t, :], lambda b: b[:, 0:8]),
                               "mms": [("m", (lambda b, j=j: b[:, 2 * j:2 * j + 2]), rkx[:, j, t * P:(t + 1) * P],
                                        hsel, True, True) for j in range(4)]})

                def over_norm(l):
                    l.wait_ge(*past("kk_squares"))
                    l.did(S.activation(sq, sq, ACT.Ln).then_inc(l.sem, 1))
                    l.wait_ge(*l.own())
                    l.did(S.activation(sq, sq, ACT.Exp, scale=-0.5).then_inc(l.sem, 1), "kk_over")

                def unit_kk(l):
                    l.wait_ge(*past("kk_over"))
                    l.did(V.tensor_tensor(kkn, kkn, sq, ALU.mult).then_inc(l.sem, 1))

                def zero_v(l):
                    for t in range(NTA):
                        l.did(G.memset(vtm[:, t, :, 64:128], 0.0).then_inc(l.sem, 1))
                products("rwkv_tm", gs, act_extra=over_norm, dve_extra=unit_kk, pool_fn=zero_v)

                lm = lambda dd, i: levm[:, dd, i, :].unsqueeze(1).to_broadcast([P, 2, P])
                idb = ident.unsqueeze(1).to_broadcast([P, 2, P])
                col4 = lambda c: cols[:, c:c + 4].unsqueeze(2).to_broadcast([P, 4, P])
                four = lambda ap: ap.rearrange("p (j n) -> p j n", j=4)

                def step(n):
                    nm = f"rwkv{n}"
                    tok = [slice(order[d][n] * P, order[d][n] * P + P) for d in range(2)]

                    gs = []
                    for d in range(2):
                        def read(l, bank, d=d):
                            l.did(V.tensor_tensor(sw[:, d, :], bank, w0[:, d, :], ALU.add).then_inc(l.sem, 1), nm, "w", d)

                        def read_a(l, bank, d=d):
                            l.did(V.tensor_tensor(aa[:, d], four(bank), col4(26 + 4 * d), ALU.add).then_inc(l.sem, 1), nm, "a_in", d)
                        gs.append({"by": "dve", "read": read, "mms": acc(lambda b: b, [(sft[:, 12, tok[d]], upd[:, d, :])])})
                        gs.append({"by": "dve", "read": read_a, "mms": [
                            ("m", (lambda b, j=j: b[:, j * P:(j + 1) * P]), upi[:, d, j * P:(j + 1) * P], sft[:, 12, tok[d]],
                             True, True) for j in range(4)]})

                    def act_x(l):
                        for d in range(2):
                            l.wait_ge(*past(nm, "w", d))
                            l.did(S.activation(sw[:, d, :], sw[:, d, :], ACT.Sigmoid).then_inc(l.sem, 1), nm, "sw", d)
                            l.wait_ge(*past(nm, "a_in", d))
                            l.did(S.activation(aa[:, d], aa[:, d], ACT.Sigmoid).then_inc(l.sem, 1), nm, "a", d)

                    def zero_pool(l):
                        for q in range(CELLS):
                            for h in range(2):
                                l.did(G.memset(BKz(q, h)[64 - 64 * h:128 - 64 * h, :], 0.0).then_inc(l.sem, 1), nm, "zeros")

                    def dve_x(l):
                        for d in range(2):
                            l.wait_ge(*past(nm, "a", d))
                            l.did(V.scalar_tensor_tensor(out=kd[:, d], in0=aa[:, d], scalar=-1.0, in1=col4(18), op0=ALU.add,
                                                         op1=ALU.mult).then_inc(l.sem, 1))
                            l.did(V.tensor_tensor(bb[:, d], kkn[:, :, tok[d]], aa[:, d], ALU.mult).then_inc(l.sem, 1))
                            l.wait_ge(*l.own())
                            l.did(V.scalar_tensor_tensor(out=kd[:, d], in0=kd[:, d], scalar=1.0, in1=sft[:, K_:K_ + 4, tok[d]],
                                                         op0=ALU.add, op1=ALU.mult).then_inc(l.sem, 1))
                    products(nm + "in", gs, act_extra=act_x, dve_extra=dve_x, pool_fn=zero_pool)

                    gs = []
                    for d in range(2):
                        def read1(l, bank, d=d):
                            l.did(S.activation(E1[:, d], four(bank), ACT.Exp, scale=-DECAY_K).then_inc(l.sem, 1))
                            l.did(S.activation(Em[:, d], four(bank), ACT.Exp, scale=DECAY_K).then_inc(l.sem, 1))

                        def read0(l, bank, d=d):
                            l.did(S.activation(E0[:, d], four(bank), ACT.Exp, scale=-DECAY_K).then_inc(l.sem, 1), nm, "exps", d)

                        def read_e(l, bank, d=d):
                            l.did(S.activation(ends[:, d, :], bank[:, 0:8], ACT.Exp, scale=-DECAY_K).then_inc(l.sem, 1))
                        for c0, w, read in ((0, P, read1), (P, P, read0), (256, 2, read_e)):
                            gs.append({"by": "act", "read": read,
                                       "after": [(nm, "sw", d)] + ([(nm + "in", "read", len(gs))] if len(gs) < 4 else []),
                                       "mms": [("m", (lambda b, j=j, w=w: b[:, j * w:(j + 1) * w]),
                                                sw[:, d, j * P:(j + 1) * P], cum[:, d, c0:c0 + w], True, True)
                                               for j in range(4)]})

                    def dve_y(l):
                        l.wait_ge(*l.own())
                        for d in range(2):
                            l.wait_ge(*past(nm, "exps", d))
                            qs = slice(4 * d, 4 * d + 4)
                            l.did(V.scalar_tensor_tensor(out=RA[:, qs, 0:P], in0=E0[:, d], scalar=-1.0, in1=kkn[:, :, tok[d]],
                                                         op0=ALU.mult, op1=ALU.mult).then_inc(l.sem, 1))
                            l.did(V.tensor_tensor(RA[:, qs, P:256], E1[:, d], sft[:, R:R + 4, tok[d]], ALU.mult).then_inc(l.sem, 1))
                            for j in range(4):
                                for h in range(2):
                                    hs = slice(64 * h, 64 * h + 64)
                                    z = BKz(4 * d + j, h)
                                    l.did(V.tensor_tensor(z[hs, 0:P], Em[hs, d, j], bb[hs, d, j], ALU.mult).then_inc(l.sem, 1))
                                    l.did(V.tensor_tensor(z[hs, P:256], Em[hs, d, j], kd[hs, d, j], ALU.mult).then_inc(l.sem, 1),
                                          nm, "scaled", d)
                        l.wait_ge(*past(nm + "cum", "read", 5))
                        l.wait_ge(*l.own())
                    products(nm + "cum", gs, dve_extra=dve_y, fence=False)

                    gs = []
                    for q in range(CELLS):
                        d = q // 4
                        for h in range(2):
                            hs = slice(64 * h, 64 * h + 64)
                            z = BKz(q, h)

                            def read(l, bank, q=q, h=h, d=d):
                                l.did(V.tensor_tensor(Gm[:, q, h, :], bank, masks[:, d, :], ALU.mult).then_inc(l.sem, 1), nm, "Gm", q, h)

                            def turned(l, bank, q=q, h=h):
                                l.did(S.activation(BKt[:, q, :, 64 * h:64 * h + 64], bank[:, 256:384].rearrange("p (e n) -> p e n", e=2),
                                                   ACT.Copy).then_inc(l.sem, 1), nm, "BKt", q, h)

                            def read_A(l, bank, q=q, h=h, d=d):
                                l.wait_ge(*past(nm, "BKt", q, h))
                                l.did(V.tensor_tensor(Am[:, q, h], bank[:, 0:P], masks[:, 1 - d, 0:P], ALU.mult).then_inc(l.sem, 1), nm, "Am", q, h)
                            gs.append({"by": "dve", "read": read,
                                       "after": [(nm, "scaled", d), (nm, "zeros"), (nm + "cum", "read", 5)] if q % 4 == 0 else [],
                                       "mms": [
                                ("m", lambda b: b[:, 0:256], z[:, 0:P], RA[:, q, :], True, True),
                                ("m", lambda b: b[:, 256:512], z[:, P:256], RA[:, q, :], True, True)]})
                            gs.append({"by": "dve", "first": ("act", turned), "read": read_A, "mms": [
                                ("m", lambda b: b[:, 0:P], RA[:, q, 0:P], z[:, 0:P], True, True)] + [
                                ("t", (lambda b, e=e: b[:, 256 + 64 * e:320 + 64 * e]), z[hs, e * P:(e + 1) * P], ident[hs, hs])
                                for e in range(2)]})

                    def first_level(l):
                        for q in range(CELLS):
                            d = q // 4
                            l.wait_ge(*past(nm, "Am", q, 1))
                            l.did(G.tensor_tensor(XT[:, q, :, 0:P], Gm[:, q, :, 0:P], lm(d, 0), ALU.mult).then_inc(l.sem, 1))
                            l.did(G.tensor_tensor(XT[:, q, :, P:256], Am[:, q], lm(1 - d, 0), ALU.mult).then_inc(l.sem, 1), nm, "XT0", q)

                    def add_one(l):
                        for q in range(CELLS):
                            l.wait_ge(*past(nm, "XT0", q))
                            x4 = XT[:, q].rearrange("p h (e n) -> p (h e) n", e=2)
                            l.did(V.tensor_tensor(x4, x4, ident.unsqueeze(1).to_broadcast([P, 4, P]), ALU.add).then_inc(l.sem, 1),
                                  nm, "X1", q)
                    products(nm + "gram", gs, dve_extra=add_one, pool_fn=first_level, fence=False)

                    lv = nm + "lev"

                    def lev_pool(l):
                        for i in range(1, 7):
                            for q in range(CELLS):
                                if i > 1:
                                    l.wait_ge(*past(lv, "P1made", i - 1, q))
                                l.did(G.tensor_tensor(Al(q).rearrange("p (h n) -> p h n", h=2), Am[:, q],
                                                      lm(1 - q // 4, i), ALU.mult).then_inc(l.sem, 1), lv, "Al", i, q)

                    def at(r):
                        return r // CELLS + 1, r % CELLS

                    def lev_pe(l):
                        def second(i, q):
                            l.wait_ge(*past(lv, "P1", i, q))
                            r = (i - 1) * CELLS + q
                            if r >= 4:
                                l.wait_ge(*past(lv, "XT", *at(r - 4)))
                            b = banks[:, 4 + r % 4, :]
                            for h in range(2):
                                p1 = P1(q)[:, h * P:(h + 1) * P]
                                tt = XT[:, q, h, P:256]
                                ins = TE.matmul(b[:, h * 256:h * 256 + P], tt, p1, start=True, stop=True)
                                if i < 6:
                                    ins = TE.matmul(b[:, h * 256 + P:h * 256 + 256], p1, tt, start=True, stop=True)
                            l.did(ins.then_inc(l.sem, 1), lv, "XTmade", i, q)
                        for i in range(1, 7):
                            for q in range(CELLS):
                                l.wait_ge(*past(lv, "Al", i, q))
                                if i > 1:
                                    l.wait_ge(*past(lv, "XT", i - 1, q))
                                else:
                                    l.wait_ge(*past(nm, "X1", q))
                                r = (i - 1) * CELLS + q
                                if r >= 4:
                                    l.wait_ge(*past(lv, "P1", *at(r - 4)))
                                b = banks[:, r % 4, :]
                                for h in range(2):
                                    ins = TE.matmul(b[:, h * P:(h + 1) * P], Al(q)[:, h * P:(h + 1) * P], XT[:, q, h, 0:P],
                                                    start=True, stop=True)
                                l.did(ins.then_inc(l.sem, 1), lv, "P1made", i, q)
                                if q >= 3:
                                    second(i, q - 3)
                            for q in range(CELLS - 3, CELLS):
                                second(i, q)

                    def lev_act(l):
                        for i in range(1, 7):
                            for q in range(CELLS):
                                l.wait_ge(*past(lv, "P1made", i, q))
                                if i > 1:
                                    l.wait_ge(*past(lv, "XTmade", i - 1, q))
                                l.did(S.activation(P1(q), banks[:, ((i - 1) * CELLS + q) % 4, 0:256], ACT.Copy).then_inc(l.sem, 1), lv, "P1", i, q)

                    def lev_dve(l):
                        for i in range(1, 7):
                            for q in range(CELLS):
                                l.wait_ge(*past(lv, "XTmade", i, q))
                                b = banks[:, 4 + ((i - 1) * CELLS + q) % 4, :].rearrange("p (h n) -> p h n", h=2)
                                w = 256 if i < 6 else P
                                l.did(V.tensor_tensor(XT[:, q, :, 0:w], b[:, :, 0:w], XT[:, q, :, 0:w], ALU.add).then_inc(l.sem, 1), lv, "XT", i, q)
                    stage(lv, fence=False, pe=lev_pe, act=lev_act, dve=lev_dve, pool=lev_pool)

                    sq_ = nm + "seq"
                    js = lambda q: slice((q % 4) * P, (q % 4 + 1) * P)
                    of_bank = lambda b: b.rearrange("p (q x c) -> p q x c", q=4, x=2)

                    def seq_pool(l):
                        l.wait_ge(*past(lv, "XTmade", 6, CELLS - 1))
                        for d in range(2):
                            for v in (W_, U_):
                                l.did(G.memset(v[:, d, :, 64:128], 0.0).then_inc(l.sem, 1), sq_, "zeros", d)

                    def seq_pe(l):
                        for d in range(2):
                            v = vtm[:, order[d][n]]
                            if n:
                                l.wait_ge(*past(sq_, "state", d))
                            for q in range(4 * d, 4 * d + 4):
                                if n:
                                    TE.matmul(banks[:, d, js(q)], RA[:, q, 0:P], state[:, d, q % 4, :], start=True, stop=False)
                                for h in range(2):
                                    ins = TE.matmul(banks[:, d, js(q)], Gm[:, q, h, 256:384], window(v, q, h),
                                                    start=(n == 0 and h == 0), stop=(h == 1))
                            l.did(ins.then_inc(l.sem, 1), sq_, "Wmade", d)
                        l.wait_ge(*past(lv, "XT", 6, CELLS - 1))
                        for d in range(2):
                            l.wait_ge(*past(sq_, "zeros", d))
                            l.wait_ge(*past(sq_, "W", d))
                            for q in range(4 * d, 4 * d + 4):
                                for h in range(2):
                                    ins = TE.matmul(banks[:, 2 + d, js(q)], XT[:, q, h, 0:P], window(W_[:, d], q, h),
                                                    start=(h == 0), stop=(h == 1))
                            l.did(ins.then_inc(l.sem, 1), sq_, "Umade", d)
                        for d in range(2):
                            l.wait_ge(*past(sq_, "U", d))
                            c = order[d][n]
                            if n < NTA - 1:
                                for q in range(4 * d, 4 * d + 4):
                                    TE.matmul(banks[:, 4 + d, js(q)], BKt[:, q, 0, :], both(U_[:, d])[:, q % 4], start=True, stop=False)
                                    ins = TE.matmul(banks[:, 4 + d, js(q)], BKt[:, q, 1, :], both(vtm[:, c])[:, q % 4],
                                                    start=False, stop=True)
                                l.did(ins.then_inc(l.sem, 1), sq_, "Smade", d)
                            if c < NT:
                                for q in range(4 * d, 4 * d + 4):
                                    TE.matmul(banks[:, 6 + d, js(q)], RA[:, q, P:256], state[:, d, q % 4, :], start=True, stop=False)
                                    for h in range(2):
                                        TE.matmul(banks[:, 6 + d, js(q)], Gm[:, q, h, 128:256], window(U_[:, d], q, h),
                                                  start=False, stop=False)
                                        ins = TE.matmul(banks[:, 6 + d, js(q)], Gm[:, q, h, 384:512], window(vtm[:, c], q, h),
                                                        start=False, stop=(h == 1))
                                l.did(ins.then_inc(l.sem, 1), sq_, "Ymade", d)

                    def seq_act(l):
                        for d in range(2):
                            l.wait_ge(*past(sq_, "Wmade", d))
                            l.did(S.activation(both(W_[:, d]), of_bank(banks[:, d, :]), ACT.Copy).then_inc(l.sem, 1), sq_, "W", d)
                        for d in range(2):
                            l.wait_ge(*past(sq_, "Umade", d))
                            l.did(S.activation(both(U_[:, d]), of_bank(banks[:, 2 + d, :]), ACT.Copy).then_inc(l.sem, 1), sq_, "U", d)

                    def seq_dve(l):
                        for d in range(2):
                            if n:
                                e = ends[:, d, :].rearrange("p (j e) -> p j e", e=2)
                                l.did(V.tensor_tensor(hop[:, d, :], end_old[:, d, :], e[:, :, 0], ALU.mult).then_inc(l.sem, 1))
                                l.wait_ge(*l.own())
                                l.did(V.tensor_tensor(state[:, d], state[:, d], hop[:, d, :].unsqueeze(2).to_broadcast([P, 4, P]),
                                                      ALU.mult).then_inc(l.sem, 1), sq_, "state", d)
                        for d in range(2):
                            e = ends[:, d, :].rearrange("p (j e) -> p j e", e=2)
                            l.did(V.tensor_copy(end_old[:, d, :], e[:, :, 1]).then_inc(l.sem, 1))
                        for d in range(2):
                            c = order[d][n]
                            if n < NTA - 1:
                                l.wait_ge(*past(sq_, "Smade", d))
                                own = sum_[:, d]
                                if n:
                                    l.did(V.tensor_tensor(own, four(banks[:, 4 + d, :]), ones2.unsqueeze(1).to_broadcast([P, 4, P]),
                                                          ALU.mult).then_inc(l.sem, 1))
                                    l.wait_ge(*past(sq_, "Ymade" if c < NT else "Wmade", d))
                                    l.wait_ge(*l.own())
                                    l.did(V.tensor_tensor(state[:, d], state[:, d], own, ALU.add).then_inc(l.sem, 1))
                                else:
                                    l.did(V.tensor_tensor(state[:, d], four(banks[:, 4 + d, :]), ones2.unsqueeze(1)
                                                          .to_broadcast([P, 4, P]), ALU.mult).then_inc(l.sem, 1))
                            if c < NT:
                                l.wait_ge(*past(sq_, "Ymade", d))
                                first = order[1 - d].index(c) > n
                                if first:
                                    l.did(V.tensor_copy(ytm[:, c, :], banks[:, 6 + d, :]).then_inc(l.sem, 1))
                                else:
                                    l.did(V.tensor_tensor(ytm[:, c, :], banks[:, 6 + d, :], ytm[:, c, :], ALU.add).then_inc(l.sem, 1))
                    stage(sq_, fence=False, pe=seq_pe, act=seq_act, dve=seq_dve, pool=seq_pool)
                sum_ = region(sum_at, 2, 4, P)
                for n in range(NTA):
                    step(n)

                hold_stream("rwkv5seq")
                wo = a["w_out"][0].rearrange("(k p) n -> p k n", p=P)
                wos.extend(stream(wo[:, :, hf * 512:(hf + 1) * 512], (KD, 512)) for hf in range(2))
                gn = Stack(0, SLOT)
                gate_mem = Stack(3 * SLOT, 4 * SLOT)
                gup = gate_mem.take(512)
                gtm = gate_mem.take(NT, 512)
                small("gate", [(gup, a["gate_up"][0])], after="rwkv5seq")
                products("rwkv_gate", [{"have": ("gate",), "by": halves(t), "read": copy_out(gtm[:, t, :]),
                                        "mms": acc(lambda b: b, [(sft[:, 13, t * P:(t + 1) * P], gup)])} for t in range(NT)])
                lg, lb = gn.take(512), gn.take(512)
                yc = gn.take(NT, 512)
                mu8, va8, rs8 = gn.take(32), gn.take(32), gn.take(32)
                small("lnx", [(lg, a["lnx_g"].to_broadcast([P, 512])), (lb, a["lnx_b"].to_broadcast([P, 512]))],
                      after="rwkv5seq")
                h64 = lambda ap: ap.rearrange("p t (h n) -> p (t h) n", n=HD)
                bc = lambda ap: ap.unsqueeze(2).to_broadcast([P, 32, HD])
                flat = lambda ap: ap.rearrange("p a b -> p (a b)")

                def gn_dve(l):
                    y3 = h64(ytm)
                    l.did(V.reduce_sum(mu8, y3, axis=AX.X).then_inc(l.sem, 1))
                    l.wait_ge(*l.own())
                    l.did(V.tensor_scalar(mu8, mu8, 1.0 / HD, None, ALU.mult).then_inc(l.sem, 1))
                    l.wait_ge(*l.own())
                    l.did(V.tensor_tensor(y3, y3, bc(mu8), ALU.subtract).then_inc(l.sem, 1))
                    l.wait_ge(*l.own())
                    l.did(V.tensor_tensor(yc, ytm, ytm, ALU.mult).then_inc(l.sem, 1))
                    l.wait_ge(*l.own())
                    l.did(V.reduce_sum(va8, h64(yc), axis=AX.X).then_inc(l.sem, 1))
                    l.wait_ge(*l.own())
                    l.did(V.tensor_scalar(va8, va8, 1.0 / HD, GN_EPS, ALU.mult, ALU.add).then_inc(l.sem, 1), "gn_var")
                    l.wait_ge(*past("gn_sd"))
                    l.did(V.reciprocal(va8, rs8).then_inc(l.sem, 1))
                    l.wait_ge(*l.own())
                    l.did(V.tensor_tensor(y3, y3, bc(va8), ALU.mult).then_inc(l.sem, 1))
                    pairs = lambda ap: ap.rearrange("p (tq x) c -> p tq x c", x=2)
                    l.did(V.tensor_tensor(pairs(h64(yc)), both(vtm[:, 0:NT].rearrange("p t q c -> p (t q) c")),
                                          flat(bonus).rearrange("p (tq x) -> p tq x", x=2).unsqueeze(3)
                                          .to_broadcast([P, 16, 2, HD]), ALU.mult).then_inc(l.sem, 1))
                    l.wait_ge(*smalls["lnx"])
                    l.wait_ge(*l.own())
                    for src, op in ((lg, ALU.mult), (lb, ALU.add)):
                        l.did(V.tensor_tensor(ytm, ytm, src.unsqueeze(1).to_broadcast([P, NT, 512]), op).then_inc(l.sem, 1))
                        l.wait_ge(*l.own())
                    l.did(V.tensor_tensor(ytm, ytm, yc, ALU.add).then_inc(l.sem, 1))
                    l.wait_ge(*l.own())
                    l.did(V.tensor_tensor(ytm, ytm, gtm, ALU.mult).then_inc(l.sem, 1))

                def gn_act(l):
                    l.wait_ge(*past("gn_var"))
                    l.did(S.activation(rs8, va8, ACT.Sqrt).then_inc(l.sem, 1), "gn_sd")
                stage("rwkv_norm", dve=gn_dve, act=gn_act)
                products("rwkv_T", transpose_groups(lambda t: ytm[:, t, :], lambda k: mixT[:, 4 + k, :], NT, 0, 4))

            def part_four():
                x1 = region(base.at, NT, D)
                xin_at, gt_at, y_at, hid_at = (base.at + n * D for n in (4, 12, 16, 24))
                xr = region(xin_at, NT, D)
                g1, b1 = region(hid_at, D), region(hid_at + D, D)
                tmpx = region(hid_at + 2 * D, 2, 512)
                small("ln1", [(xr, a["x"][0].rearrange("(t p) n -> p t n", p=P)),
                              (g1, a["ln1_g"].to_broadcast([P, D])), (b1, a["ln1_b"].to_broadcast([P, D]))],
                      after="rwkv5seq")

                def residual(name, ws_, gate, x_old, x_new, lhs, nk, tmpx, hv=None):
                    gs = []
                    for hf in range(2):
                        for t in range(NT):
                            i = len(gs)

                            def read(l, bank, hf=hf, t=t, i=i):
                                if hv:
                                    l.wait_ge(*smalls[hv])
                                v = slice(hf * 512, hf * 512 + 512)
                                l.wait_ge(*l.own())
                                l.did(V.tensor_tensor(tmpx[:, i % 2, :], bank, gate[:, v], ALU.mult).then_inc(l.sem, 1))
                                l.wait_ge(*l.own())
                                l.did(V.scalar_tensor_tensor(out=x_new[:, t, v], in0=x_old[:, t, v], scalar=ALPHA,
                                                             in1=tmpx[:, i % 2, :], op0=ALU.mult, op1=ALU.add).then_inc(l.sem, 1))
                            gs.append({"by": "dve", "read": read, "loads": [ws_[hf][0]] if ws_ else [],
                                       "mms": acc(lambda b: b, [lhs(k, t, hf) for k in range(nk)])})
                    products(name, gs)
                residual("w_out", wos, gt1, xr, x1,
                         lambda k, t, hf: (mixT[:, k, t * P:(t + 1) * P], wos[hf][1][:, k, :]), KD, tmpx, hv="ln1")
                norm_stage("norm_x1", lambda i: x1[:, i, :], lambda i: x1[:, i, :], NT, [], affine=(g1, b1))

                xh = region(y_at, NT, D)
                h2T = region(gt_at, KD, T)
                norm_stage("norm_h2", lambda i: x1[:, i, :], lambda i: xh[:, i, :], NT, [])
                products("h2_T", transpose_groups(lambda i: xh[:, i, :], lambda k: h2T[:, k, :], NT, 0, KD,
                                                  lambda k: (modcol[:, 32 + k, 0:1], modcol[:, 24 + k, 0:1])))
                sm = Stack(hid_at, hid_at + 5 * D)
                rw = sm.take(KD, NE)
                aff = stats[:, 120:184].rearrange("p (t e) -> p t e", e=NE)
                rank = stats[:, 184:248].rearrange("p (t e) -> p t e", e=NE)
                eqs = sm.take(NT, NE)
                late = sm.take(NT, NE)
                mx4, sm4 = sm.take(NT), sm.take(NT)
                affT = sm.take(T)
                before = sm.take(P)
                slots = sm.take(CAP)
                junk = sm.take(4, 512)
                small("router", [(rw, a["router_w"][0].rearrange("(k p) e -> p k e", p=P)),
                                 (before, a["k_before"][:, 0, 0:P]), (slots, a["k_slots"])], after="norm_x1")

                def logits_read(l, bank):
                    lg = bank[:, 0:64].rearrange("p (t e) -> p t e", e=NE)
                    l.did(V.reduce_max(mx4, lg, axis=AX.X).then_inc(l.sem, 1))
                    l.wait_ge(*l.own())
                    l.did(V.tensor_tensor(aff, lg, mx4.unsqueeze(2).to_broadcast([P, NT, NE]), ALU.subtract).then_inc(l.sem, 1), "router_in")

                def router_act(l):
                    l.wait_ge(*past("router_in"))
                    l.did(S.activation(aff, aff, ACT.Exp).then_inc(l.sem, 1), "router_exp")

                def router_dve(l):
                    l.wait_ge(*past("router_exp"))
                    l.did(V.reduce_sum(sm4, aff, axis=AX.X).then_inc(l.sem, 1))
                    l.wait_ge(*l.own())
                    l.did(V.reciprocal(sm4, sm4).then_inc(l.sem, 1))
                    l.wait_ge(*l.own())
                    l.did(V.tensor_tensor(aff, aff, sm4.unsqueeze(2).to_broadcast([P, NT, NE]), ALU.mult).then_inc(l.sem, 1))
                products("router", [{"have": ("router",), "by": "dve", "read": logits_read, "mms": [
                    m_ for t in range(NT) for m_ in
                    acc(lambda b, t=t: b[:, t * NE:(t + 1) * NE],
                        [(h2T[:, k, t * P:(t + 1) * P], rw[:, k, :]) for k in range(KD)])]}],
                    act_extra=router_act, dve_extra=router_dve)
                products("aff_T", [{"by": "act", "read": copy_out(affT[0:NE, :], lambda b: b[0:NE, :]), "mms": [
                    ("t", (lambda b, t=t: b[0:NE, t * P:(t + 1) * P]), aff[:, t, :], ident) for t in range(NT)]}])

                affb = region(xin_at, NE, T)

                def spread(l):
                    l.wait_ge(*smalls["rows"])
                    for e in range(NE):
                        if e >= 8:
                            l.wait_ge(*past("affb", e - 8))
                        l.did(TE.matmul(banks[:, e % 8, :], rows16[:, e, :], affT[0:NE, :], start=True, stop=True)
                              .then_inc(l.sem, 1), "spread", e)

                y_r, mix_r = parts_of("y_r", y_at, 8 * D), parts_of("mix_r", mixT_at, KD * T)
                xh_hi, xh_lo = mix_r(mixT_at, NT, D), y_r(y_at, NT, D)

                def rest_xh(l):
                    for t in range(NT):
                        l.wait_ge(*past("xh_hi", t))
                        l.did(G.tensor_tensor(xh_lo[:, t, :], xh[:, t, :], xh_hi[:, t, :], ALU.subtract).then_inc(l.sem, 1))

                def keep_rows(l):
                    for e in range(NE):
                        l.wait_ge(*past("spread", e))
                        l.did(S.activation(affb[:, e, :], banks[:, e % 8, :], ACT.Copy).then_inc(l.sem, 1), "affb", e)
                    for t in range(NT):
                        l.did(S.activation(xh_hi[:, t, :], xh[:, t, :], ACT.Copy).then_inc(l.sem, 1), "xh_hi", t)

                def ranks(l):
                    for e in range(NE):
                        l.wait_ge(*past("affb", e))
                        for t in range(NT):
                            s_ = aff[:, t, e:e + 1]
                            jk = junk[:, t, :]
                            if t:
                                l.did(V.tensor_scalar(jk[:, 0:t * P], affb[:, e, 0:t * P], s_, 0.0, ALU.is_ge, ALU.add,
                                                      accum_out=eqs[:, t, e:e + 1]).then_inc(l.sem, 1))
                            l.did(V.tensor_scalar(jk[:, t * P:T], affb[:, e, t * P:T], s_, 0.0, ALU.is_gt, ALU.add,
                                                  accum_out=rank[:, t, e:e + 1]).then_inc(l.sem, 1))
                            l.did(V.scalar_tensor_tensor(out=jk2[:, t, :], in0=affb[:, e, t * P:(t + 1) * P], scalar=s_,
                                                         in1=before, op0=ALU.is_equal, op1=ALU.mult,
                                                         accum_out=late[:, t, e:e + 1]).then_inc(l.sem, 1))
                        l.wait_ge(*l.own())
                    l.wait_ge(*l.own())
                    l.did(V.tensor_tensor(rank, rank, late, ALU.add).then_inc(l.sem, 1))
                    l.wait_ge(*l.own())
                    l.did(V.tensor_tensor(rank[:, 1:NT, :], rank[:, 1:NT, :], eqs[:, 1:NT, :], ALU.add).then_inc(l.sem, 1))
                jk2 = sm.take(4, P)
                rows16 = region(y_at + 4 * D, NE, P)[0:NE]
                small("rows", [(rows16, a["k_rows"])], after="norm_x1")
                stage("ranks", pe=spread, act=keep_rows, dve=ranks, pool=rest_xh)

                G1 = y_r(y_at + 4 * D, NT, NE * CAP)
                G2 = region(hid_at, NT, NE * CAP)

                slots2 = region(gt_at, CAP)

                def save_slots(l):
                    l.did(V.tensor_copy(slots2, slots).then_inc(l.sem, 1))
                stage("slots", dve=save_slots)

                def onehot(l):
                    l.wait_ge(*l.own())
                    es = lambda ap: ap.rearrange("p (e c) -> p e c", c=CAP)
                    for t in range(NT):
                        l.did(V.tensor_tensor(es(G1[:, t, :]), slots2.unsqueeze(1).to_broadcast([P, NE, CAP]),
                                              rank[:, t, :].unsqueeze(2).to_broadcast([P, NE, CAP]), ALU.is_equal).then_inc(l.sem, 1))
                    l.wait_ge(*l.own())
                    for t in range(NT):
                        l.did(V.tensor_tensor(es(G2[:, t, :]), es(G1[:, t, :]),
                                              aff[:, t, :].unsqueeze(2).to_broadcast([P, NE, CAP]), ALU.mult).then_inc(l.sem, 1))
                stage("onehot", fence=False, dve=onehot)
                xinT = region(xin_at, KD, NE * CAP)
                GgT = region(gt_at, NE // 2, T)
                gs = []
                for k in range(KD):
                    for hf in range(2):
                        v = slice(hf * 512, hf * 512 + 512)

                        def read(l, bank, k=k, v=v):
                            sc, sh = modcol[:, 32 + k, 0:1], modcol[:, 24 + k, 0:1]
                            if l is act:
                                l.did(S.activation(xinT[:, k, v], bank, ACT.Identity, bias=sh, scale=sc).then_inc(l.sem, 1))
                            else:
                                l.did(V.tensor_scalar(xinT[:, k, v], bank, sc, sh, ALU.mult, ALU.add).then_inc(l.sem, 1))
                        gs.append({"by": halves(k), "read": read, "mms": acc(lambda b: b, [
                            (part[:, t, k * P:(k + 1) * P], G1[:, t, v]) for t in range(NT) for part in (xh_hi, xh_lo)])})
                for q in range(NE // 2):
                    gs.append({"by": halves(q), "read": copy_out(GgT[:, q, :]), "mms": [
                        ("t", (lambda b, t=t: b[:, t * P:(t + 1) * P]), G2[:, t, q * P:(q + 1) * P], ident) for t in range(NT)]})
                products("gather", gs)

                hold_stream("rwkv_T")
                ysb = region(y_at, NE // 2, D)
                hb = Stack(hid_at, hid_at + 5 * D)
                hid = hb.take(2, D)
                sgt = hb.take(2, 512)
                hidT = hb.take(2, KD, P)
                gs, ex_ = [], "experts"
                wsrc = {n: a["exp_w_" + n] for n in ("gate", "up", "down")}

                def pair_weights(kind, q, hf):
                    return [stream(wsrc[kind][0, 2 * q + e].rearrange("(k p) n -> p k n", p=P)[:, :, hf * 512:(hf + 1) * 512],
                                   (KD, 512)) for e in range(2)]

                def two(w, lhs):
                    return [("m", (lambda b, e=e: b[64 * e:64 * e + 64, :]), lhs(k, e), w[e][1][:, k, :], k == 0, k == KD - 1)
                            for k in range(KD) for e in range(2)]

                def gate_up(q):
                    for hf in range(2):
                        v = slice(hf * 512, hf * 512 + 512)
                        for kind in ("gate", "up"):
                            w = pair_weights(kind, q, hf)
                            lhs = lambda k, e, q=q: xinT[:, k, (2 * q + e) * CAP:(2 * q + e + 1) * CAP]
                            g = {"by": "dve", "loads": [w[0][0], w[1][0]], "mms": two(w, lhs)}
                            if kind == "gate":
                                def first(l, bank, q=q, hf=hf):
                                    if 2 * q + hf >= 2:
                                        l.wait_ge(*past(ex_, "gated", 2 * q + hf - 2))
                                    l.did(S.activation(sgt[:, hf, :], bank, ACT.Sigmoid).then_inc(l.sem, 1), ex_, "sig", q, hf)

                                def read(l, bank, q=q, hf=hf, v=v):
                                    l.wait_ge(*past(ex_, "sig", q, hf))
                                    if q >= 2:
                                        l.wait_ge(*past(ex_, "turned", q - 2))
                                    l.did(V.tensor_tensor(hid[:, q % 2, v], bank, sgt[:, hf, :], ALU.mult).then_inc(l.sem, 1), ex_, "gated", 2 * q + hf)
                                g["first"] = ("act", first)
                            else:
                                def read(l, bank, q=q, hf=hf, v=v):
                                    l.wait_ge(*l.own())
                                    l.did(V.tensor_tensor(hid[:, q % 2, v], bank, hid[:, q % 2, v], ALU.mult).then_inc(l.sem, 1), ex_, "hid", q, hf)
                            g["read"] = read
                            gs.append(g)

                def down(q):
                    for hf in range(2):
                        g = {"by": "act", "after": [(ex_, "hid", q, hf)], "mms": [
                            ("t", (lambda b, i=i: b[:, i * P:(i + 1) * P]), hid[:, q % 2, (4 * hf + i) * P:(4 * hf + i + 1) * P], ident)
                            for i in range(4)]}

                        def read(l, bank, q=q, hf=hf):
                            if q >= 2:
                                l.wait_ge(*past(ex_, "downed", q - 2))
                            l.did(S.activation(hidT[:, q % 2, 4 * hf:4 * hf + 4, :], bank.rearrange("p (a b) -> p a b", b=P),
                                               ACT.Copy).then_inc(l.sem, 1), ex_, "hidT", q, hf)
                        g["read"] = read
                        if hf == 1:
                            g["name"] = (ex_, "turned", q)
                        gs.append(g)
                    for hf in range(2):
                        v = slice(hf * 512, hf * 512 + 512)
                        w = pair_weights("down", q, hf)
                        g = {"by": halves(hf), "loads": [w[0][0], w[1][0]], "after": [(ex_, "hidT", q, 0), (ex_, "hidT", q, 1)],
                             "mms": two(w, lambda k, e, q=q: hidT[:, q % 2, k, 64 * e:64 * e + 64]),
                             "read": copy_out(ysb[:, q, v])}
                        if hf == 1:
                            g["name"] = (ex_, "downed", q)
                        gs.append(g)
                for q in range(NE // 2 + 1):
                    if q < NE // 2:
                        gate_up(q)
                    if q:
                        down(q - 1)
                products(ex_, gs)

                small("ln2", [(region(xin_at, D), a["ln2_g"].to_broadcast([P, D])),
                              (region(xin_at + D, D), a["ln2_b"].to_broadcast([P, D]))], after="experts")
                tmpx2 = region(xin_at + 2 * D, 2, 512)
                residual("scatter", None, gt2, x1, x1,
                         lambda q, t, hf: (GgT[:, q, t * P:(t + 1) * P], ysb[:, q, hf * 512:(hf + 1) * 512]), NE // 2, tmpx2, hv="ln2")
                norm_stage("norm_x2", lambda i: x1[:, i, :], lambda i: x1[:, i, :], NT, [],
                           affine=(region(xin_at, D), region(xin_at + D, D)))

            def part_five():
                x = region(base.at, NT, D)
                hT_at = base.at + 4 * D
                hT = region(hT_at, KD, T)
                rest = Stack(base.at + 8 * D)
                gcols = rest.take(98)
                grow = rest.take(D)
                ones2 = rest.take(P)
                sbk = rest.take(3, P)
                lamp = rest.take(2, 4, 32)
                lam = rest.take(8)
                st = rest.take(5, 8)
                ss = rest.take(8)
                eps = rest.take(2)
                grows = region(base.at + 4 * D, P)
                gains = a["norm_gains_2"]
                small("second", [(grows[0:96, :], gains.rearrange("l n (k p) -> (l n k) p", p=P)),
                                 (grows[96:98, 0:64], a["diff_subln_gain_2"]), (grows[96:98, 64:128], a["diff_subln_gain_2"]),
                                 (ones2, a["k_ones2"]), (sbk, a["k_sb"]),
                                 (lamp, a["diff_lambda_2"].rearrange("l a n -> (l a n)").unsqueeze(0).to_broadcast([P, 256]))],
                      after="norm_x2")
                lam_init = [0.8 - 0.6 * math.exp(-0.3 * l) for l in range(2)]

                def lam_dve(l):
                    l.wait_ge(*smalls["second"])
                    l.did(V.tensor_tensor(lamp[:, :, 0::2, :], lamp[:, :, 0::2, :], lamp[:, :, 1::2, :], ALU.mult).then_inc(l.sem, 1))
                    l.wait_ge(*l.own())
                    l.did(V.reduce_sum(lam[:, 0:4].rearrange("p (l a) -> p l a", l=2), lamp[:, :, 0::2, :], axis=AX.X).then_inc(l.sem, 1), "lam_sums")
                    l.wait_ge(*past("lam_exp"))
                    lv = lam[:, 0:4].rearrange("p (l a) -> p l a", l=2)
                    l.did(V.tensor_tensor(lam[:, 4:6], lv[:, :, 1], lv[:, :, 0], ALU.subtract).then_inc(l.sem, 1))
                    l.wait_ge(*l.own())
                    for i in range(2):
                        l.did(V.tensor_scalar(lam[:, 4 + i:5 + i], lam[:, 4 + i:5 + i], -lam_init[i], None, ALU.add).then_inc(l.sem, 1))

                def lam_act(l):
                    l.wait_ge(*past("lam_sums"))
                    l.did(S.activation(lam[:, 0:4], lam[:, 0:4], ACT.Exp).then_inc(l.sem, 1), "lam_exp")

                def fill_eps(l):
                    for i, coef in enumerate((1.0, 0.5)):
                        l.did(G.memset(eps[:, i:i + 1], NORM_EPS / coef ** 2).then_inc(l.sem, 1))
                stage("lambda", dve=lam_dve, act=lam_act, pool=fill_eps)

                def gain_read(l, bank):
                    l.did(V.tensor_copy(gcols[:, 0:96], bank[:, 0:96]).then_inc(l.sem, 1))
                    for i in range(2):
                        l.did(V.tensor_scalar(gcols[:, 96 + i:97 + i], bank[:, 96 + i:97 + i], 1.0 - lam_init[i], None, ALU.mult)
                              .then_inc(l.sem, 1))
                products("gain_cols", [{"by": "dve", "read": gain_read,
                                        "mms": [("t", lambda b: b[:, 0:98], grows[0:98, :], ident[0:98, 0:98])]}])

                rest.at += -rest.at % 8
                ytmp_at = rest.at
                ffn_r = parts_of("ffn_r", ytmp_at, ARENA - ytmp_at)
                mix_r, h_r = parts_of("mix_r", mixT_at, KD * T), parts_of("h_r", hT_at, KD * T)
                ytmp = rest.take(2, D)
                rest_end = rest.at
                scr = rest.take(2, D)[:, 0, :]
                body = rest.at
                xs = region(body, NT, D)
                gnext = region(ARENA - D, D)
                four = lambda ap: ap.rearrange("p (j n) -> p j n", j=4)
                hT_hi, hT_lo = mix_r(mixT_at, KD, T), h_r(hT_at, KD, T)

                def gain_rows(key, mine, following, after):
                    row_of = lambda at_: gains[at_[0], at_[1], :].unsqueeze(0).to_broadcast([P, D])
                    small(key, [(dst, row_of(at_)) for dst, at_ in ((grow, mine), (gnext, following)) if at_], after=after)

                def between(name, coef, key, last=False):
                    ybank = lambda t: banks[:, 2 * t:2 * t + 2, :].rearrange("p a b -> p (a b)")
                    root = 1.0 / math.sqrt(D)

                    def f_act(l):
                        def sums(src, t, at_, scale, eps_, what):
                            l.did(S.activation(scr, src, ACT.Square, scale=scale, accum_out=ss[:, at_ + t:at_ + t + 1]).then_inc(l.sem, 1))
                            l.wait_ge(*l.own())
                            l.did(S.activation(ss[:, at_ + t:at_ + t + 1], ss[:, at_ + t:at_ + t + 1], ACT.Sqrt, bias=eps_)
                                  .then_inc(l.sem, 1), name, what, t)

                        def of_x(t):
                            if coef is not None:
                                l.wait_ge(*past(name, "x", t))
                            sums(x[:, t, :], t, 4, root, eps[:, 0:1], "xsd")

                        def evac(t):
                            for hf in range(2):
                                l.wait_ge(*past(name, "turned", t, hf))
                                l.did(S.activation(hT_hi[:, 4 * hf:4 * hf + 4, t * P:(t + 1) * P], four(banks[:, 2 * t + hf, :]),
                                                   ACT.Copy).then_inc(l.sem, 1), name, "hi", t, hf)
                        for t in range(NT + 1):
                            if coef is not None and t < NT:
                                sums(ybank(t), t, 0, root / coef, eps[:, 0:1] if coef == 1.0 else eps[:, 1:2], "ysd")
                            if not last and t:
                                of_x(t - 1)
                            if not last and t > 2:
                                evac(t - 3)
                        if not last:
                            for t in range(NT - 2, NT):
                                evac(t)

                    def f_dve(l):
                        def add(t):
                            l.wait_ge(*past(name, "ysd", t))
                            l.did(V.reciprocal(ss[:, t:t + 1], ss[:, t:t + 1]).then_inc(l.sem, 1))
                            l.wait_ge(*l.own())
                            l.did(V.scalar_tensor_tensor(out=ytmp[:, t % 2, :], in0=ybank(t), scalar=ss[:, t:t + 1], in1=grow,
                                                         op0=ALU.mult, op1=ALU.mult).then_inc(l.sem, 1))
                            l.wait_ge(*l.own())
                            l.did(V.tensor_tensor(x[:, t, :], x[:, t, :], ytmp[:, t % 2, :], ALU.add).then_inc(l.sem, 1), name, "x", t)

                        def scale(t):
                            l.wait_ge(*past(name, "xsd", t))
                            l.did(V.reciprocal(ss[:, 4 + t:5 + t], ss[:, 4 + t:5 + t]).then_inc(l.sem, 1))
                            l.wait_ge(*l.own())
                            l.did(V.scalar_tensor_tensor(out=xs[:, t, :], in0=x[:, t, :], scalar=ss[:, 4 + t:5 + t], in1=gnext,
                                                         op0=ALU.mult, op1=ALU.mult).then_inc(l.sem, 1), name, "xs", t)

                        def evac(t):
                            for hf in range(2):
                                l.wait_ge(*past(name, "hi", t, hf))
                                ks, ts = slice(4 * hf, 4 * hf + 4), slice(t * P, (t + 1) * P)
                                l.did(V.tensor_tensor(hT_lo[:, ks, ts], four(banks[:, 2 * t + hf, :]), hT_hi[:, ks, ts],
                                                      ALU.subtract).then_inc(l.sem, 1))
                        l.wait_ge(*smalls[key])
                        for t in range(NT + 1):
                            if coef is not None and t < NT:
                                add(t)
                            if not last and t:
                                scale(t - 1)
                            if not last and t > 2:
                                evac(t - 3)
                        if not last:
                            for t in range(NT - 2, NT):
                                evac(t)

                    def f_pe(l):
                        if last:
                            return
                        for t in range(NT):
                            l.wait_ge(*past(name, "xs", t))
                            for hf in range(2):
                                for i in range(4):
                                    k = 4 * hf + i
                                    ins = TE.transpose(banks[:, 2 * t + hf, i * P:(i + 1) * P], xs[:, t, k * P:(k + 1) * P], ident)
                                l.did(ins.then_inc(l.sem, 1), name, "turned", t, hf)
                    stage(name, act=f_act, dve=f_dve, pe=f_pe)

                def ffn(l_, f_):
                    nm = f"ffn{l_}{f_}"
                    free = Stack(ytmp_at)
                    hid_at = free.at
                    hid = free.take(NF, T)
                    hid_lo = ffn_r(hid_at, NF, T)
                    DEPTH = 2
                    hi_at = free.at
                    free.take(DEPTH, 2048)
                    his = [ffn_r(hi_at + i * 2048, 2048) for i in range(DEPTH)]
                    hid_hi_at = free.at
                    free.take(2, 2, T)
                    hid_his = [ffn_r(hid_hi_at + i * 2 * T, 2, T) for i in range(2)]
                    wg, wu, wd = (a["w_ffn_" + n + "_2"][l_, f_] for n in ("gate", "up", "down"))
                    src = lambda w, c: w.rearrange("(k p) n -> p k n", p=P)[:, :, c * 256:(c + 1) * 256]
                    gs, units = [], []
                    for s_ in range(NF // 2):
                        n, w = stream_many([((KD, 256), src(wg, s_)), ((KD, 256), src(wu, s_))])
                        at_ = (n[0] % RING) * SLOT
                        for c in range(2):
                            f = 2 * s_ + c
                            cut = lambda ap, c=c: ap.rearrange("p (k c n) -> p k c n", k=16, c=2)[:, :, c, :]
                            hi = his[f % DEPTH].rearrange("p (k n) -> p k n", n=P)
                            lo = cut(ring_r(at_, SLOT))
                            units.append((cut(region(at_, SLOT)), lo, hi, n))

                            def first(l, bank, f=f):
                                l.did(S.activation(hid[:, f, :], bank, ACT.Sigmoid).then_inc(l.sem, 1), nm, "sig", f)

                            def read(l, bank, f=f):
                                l.wait_ge(*past(nm, "sig", f))
                                l.did(V.tensor_tensor(hid[:, f, :], bank, hid[:, f, :], ALU.mult).then_inc(l.sem, 1))

                            def read_up(l, bank, f=f):
                                l.wait_ge(*l.own())
                                l.did(V.tensor_tensor(hid[:, f, :], bank, hid[:, f, :], ALU.mult).then_inc(l.sem, 1))
                            for j in range(2):
                                gs.append({"by": "dve", "read": read_up if j else read, "loads": [n], "unit": f,
                                           "mms": three(lambda b: b, [((hi[:, 8 * j + k, :], lo[:, 8 * j + k, :]),
                                                                       (hT_hi[:, k, :], hT_lo[:, k, :])) for k in range(KD)])})
                                if j == 0:
                                    gs[-1]["first"] = ("act", first)
                    products(nm, gs, units=units, depth=DEPTH)

                    dn, pairs = nm + "down", NF // 2
                    downs, w_units, h_units = [], [], []
                    for s_ in range((NF + 3) // 4):
                        m_ = min(4, NF - 4 * s_)
                        downs.append(stream(wd.rearrange("(f p) n -> p f n", p=P)[:, 4 * s_:4 * s_ + m_, :], (m_, D)))
                    for u in range(pairs):
                        n, _ = downs[u // 2]
                        at_ = (n[0] % RING) * SLOT + (u % 2) * 2 * D
                        w_units.append((region(at_, 2, D), ring_r(at_, 2, D),
                                        his[u % DEPTH].rearrange("p (f n) -> p f n", n=D), n))
                        fs = slice(2 * u, 2 * u + 2)
                        h_units.append((hid[:, fs, :], hid_lo[:, fs, :], hid_his[u % 2], None))
                    following = (l_, 2) if f_ == 0 else ((1, 0) if l_ == 0 else None)
                    gain_rows(nm + "g", (l_, 4 * f_ + 1), following, nm)

                    def split_down(l):
                        for u in range(pairs):
                            split(l, dn + "h", u, h_units[u], 2)
                            split(l, dn, u, w_units[u], DEPTH)

                    def down_pe(l):
                        for u in range(pairs):
                            l.wait_ge(*past(dn, "lo", u))
                            _, w_lo, w_hi, n = w_units[u]
                            for c in range(2):
                                f = 2 * u + c
                                for t in range(NT):
                                    ts = slice(t * P, (t + 1) * P)
                                    for hf in range(2):
                                        ns = slice(hf * 512, (hf + 1) * 512)
                                        h_hi, h_lo = hid_his[u % 2][:, c, ts], hid_lo[:, f, ts]
                                        bank = banks[:, 2 * t + hf, :]
                                        TE.matmul(bank, h_hi, w_hi[:, c, ns], start=(f == 0), stop=False)
                                        TE.matmul(bank, h_hi, w_lo[:, c, ns], start=False, stop=False)
                                        ins = TE.matmul(bank, h_lo, w_hi[:, c, ns], start=False, stop=(f == NF - 1))
                            l.did(ins.then_inc(l.sem, 1), dn, "used", u)
                            l.name_last(dn + "h", "used", u)
                            if u % 2 or u == pairs - 1:
                                l.name_last("freed", n[0])
                    stage(dn, pe=down_pe, act=split_down, dve=split_down)

                def mixer(l_):
                    nm = f"mix{l_}"
                    m5 = Stack(body)
                    qk = m5.take(16, T)
                    y_at_ = rest_end - 2 * D
                    odd_a = [region(y_at_ + 3 * 512, T), grow[:, 0:T], grow[:, T:2 * T]]
                    qz_a = lambda h: qk[:, h // 2, :] if h % 2 == 0 else odd_a[h // 2]
                    vt = m5.take(NT, D)
                    extra = m5.at
                    w_src = a["w_in_2"][l_].rearrange("(k p) n -> p k n", p=P)
                    ws = [stream(w_src[:, :, s_ * 512:(s_ + 1) * 512], (KD, 512)) for s_ in range(6)]
                    fm = {c * P: i for i, c in enumerate([0, 1, 2, 3, 4, 5, 9, 10, 11, 12, 15, 16, 17, 18, 19, 20])}
                    tm = {768: (256, 0), 1024: (128, 256), 1664: (256, 384), 2688: (384, 640)}
                    unit_cols = []
                    for c0 in sorted(list(fm) + list(tm)):
                        if c0 == 1024:
                            unit_cols.append((c0, 256))
                        elif c0 != 1152:
                            unit_cols.append((c0, P if c0 in fm else tm[c0][0]))
                    units, unit_of = [], {}
                    for u, (c0, width) in enumerate(unit_cols):
                        n = ws[c0 // 512][0]
                        o, at_ = c0 % 512, (n[0] % RING) * SLOT
                        cut = lambda ap, o=o, width=width: ap[:, :, o:o + width]
                        hi = ffn_r(rest_end if u % 2 else extra, KD, width)
                        lo = cut(ring_r(at_, KD, 512))
                        units.append((cut(region(at_, KD, 512)), lo, hi, n))
                        unit_of[c0] = (u, lo, hi)
                        if c0 == 1024:
                            unit_of[1152] = (u, lo[:, :, P:2 * P], hi[:, :, P:2 * P])
                    assert len(units) % 2 == 1, "the last unit, the widest, needs the larger buffer"
                    gs = []
                    for c0 in sorted(list(fm) + list(tm)):
                        n, w = ws[c0 // 512]
                        u, lo, hi = unit_of[c0]
                        if c0 in fm:
                            i = fm[c0]

                            def read(l, bank, i=i):
                                if 10 <= i < 13:
                                    if l is act:
                                        l.did(S.activation(qk[:, i, :], bank, ACT.Copy, scale=HD ** -0.5).then_inc(l.sem, 1))
                                    else:
                                        l.did(V.tensor_scalar(qk[:, i, :], bank, HD ** -0.5, None, ALU.mult).then_inc(l.sem, 1))
                                elif i < 3:
                                    for h in range(2):
                                        hs = slice(64 * h, 64 * h + 64)
                                        copy_out(qz_a(2 * i + h)[hs, :], lambda b, hs=hs: b[hs, :])(l, bank)
                                else:
                                    copy_out(qk[:, i, :])(l, bank)
                            gs.append({"by": halves(len(gs)), "loads": [n], "read": read, "unit": u,
                                       "mms": three(lambda b: b, [((hi[:, k, :], lo[:, k, :]), (hT_hi[:, k, :], hT_lo[:, k, :]))
                                                                  for k in range(KD)])})
                        else:
                            width, v0 = tm[c0]
                            wide = max(width, 256)
                            for t in range(NT):
                                ts = slice(t * P, (t + 1) * P)
                                gs.append({"by": halves(len(gs)), "loads": [n], "unit": u,
                                           "read": copy_out(vt[:, t, v0:v0 + width], lambda b, width=width: b[:, 0:width]),
                                           "mms": three(lambda b, wide=wide: b[:, 0:wide],
                                                        [((hT_hi[:, k, ts], hT_lo[:, k, ts]), (hi[:, k, :], lo[:, k, :]))
                                                         for k in range(KD)])})

                    def zero_a(l):
                        for h in range(6):
                            z = 64 - 64 * (h % 2)
                            l.did(G.memset(qz_a(h)[z:z + 64, :], 0.0).then_inc(l.sem, 1))
                    products(nm, gs, pool_fn=zero_a, units=units)
                    pt = region(base.at + 4 * D, 2, NT, T)
                    b_dil = region(extra, 6, T)
                    b_dif = region(rest_end, 4, T)
                    small(nm + "bias", [(b_dil, a["k_bias"][0:6, :, 0:T].rearrange("h p n -> p h n")),
                                        (b_dif, a["k_bias"][6:10, :, 0:T].rearrange("h p n -> p h n"))], after=nm)
                    width = lambda t: P * (t + 1)
                    half = lambda h: HD * (h % 2)

                    def s_dil(h, t):
                        return [[(qz_a(h)[:, t * P:(t + 1) * P], qk[:, 3 + h // 2, 0:width(t)], 0, width(t))]]
                    attention(nm + "dil", list(range(6)), width, s_dil, lambda h, j: vt[:, j, h * HD:(h + 1) * HD],
                              lambda h: mixT[half(h):half(h) + HD, h // 2, :], HD ** -0.5, ([region(y_at_ + i * 512, 512) for i in range(3)] + [gt1[:, 0:512], gt1[:, 512:D]], pt, st),
                              bias=lambda h, t: b_dil[:, h, 384 - P * t:T], need=(nm + "bias",))

                    qz_b = [region(body + i * T, T) if i < 6 else region(extra + (i - 6) * T, T) for i in range(8)]

                    def pad_b_pool(l):
                        l.did(G.memset(region(body, 6 * T), 0.0).then_inc(l.sem, 1))
                        l.did(G.memset(region(extra, 2 * T), 0.0).then_inc(l.sem, 1), nm, "zero_b")

                    def pad_b_dve(l):
                        l.wait_ge(*past(nm, "zero_b"))
                        for i in range(8):
                            r0 = 32 * (i % 4)
                            l.did(V.tensor_copy(qz_b[i][r0:r0 + 32, :], qk[r0:r0 + 32, 6 + i // 4, :]).then_inc(l.sem, 1))
                    stage(nm + "padb", pool=pad_b_pool, dve=pad_b_dve)
                    def s_dif(h, t):
                        out_ = []
                        for e in range(2):
                            out_.append([(qz_b[2 * h + e][:, t * P:(t + 1) * P], qk[:, 8 + h // 2, 0:width(t)], 0, width(t))])
                        return out_
                    attention(nm + "dif", list(range(4)), width, s_dif, lambda h, j: vt[:, j, 384 + h * HD:384 + (h + 1) * HD],
                              lambda h: mixT[half(h):half(h) + HD, 3 + h // 2, :], 32 ** -0.5,
                              ([region(y_at_, D), region(y_at_ + D, D), region(extra + 2 * T, D), gt1, gt2], pt, st),
                              bias=lambda h, t: b_dif[:, h, 384 - P * t:T], lam=lam[:, 4 + l_:5 + l_], need=(nm + "bias",))

                    sq2 = region(extra, 2, T)
                    rs2 = region(extra + 2 * T, 2, T)

                    def sub_sq(l):
                        l.did(V.tensor_tensor(sq2, mixT[:, 3:5, :], mixT[:, 3:5, :], ALU.mult).then_inc(l.sem, 1))
                    stage(nm + "subsq", dve=sub_sq)

                    def sub_read(l, bank, i):
                        l.did(V.tensor_scalar(sq2[:, i, :], bank, 1.0 / HD, NORM_EPS, ALU.mult, ALU.add).then_inc(l.sem, 1), nm, "subvar", i)

                    def sub_act(l):
                        for i in range(2):
                            l.wait_ge(*past(nm, "subvar", i))
                            l.did(S.activation(rs2[:, i, :], sq2[:, i, :], ACT.Ln).then_inc(l.sem, 1))
                        l.wait_ge(*l.own())
                        for i in range(2):
                            l.did(S.activation(rs2[:, i, :], rs2[:, i, :], ACT.Exp, scale=-0.5).then_inc(l.sem, 1), nm, "subsd", i)

                    def sub_dve(l):
                        for i in range(2):
                            l.wait_ge(*past(nm, "subsd", i))
                            l.did(V.scalar_tensor_tensor(out=mixT[:, 3 + i, :], in0=mixT[:, 3 + i, :], scalar=gcols[:, 96 + l_:97 + l_],
                                                         in1=rs2[:, i, :], op0=ALU.mult, op1=ALU.mult).then_inc(l.sem, 1))
                    products(nm + "sub", [{"by": "dve", "read": (lambda l, b, i=i: sub_read(l, b, i)),
                                           "mms": acc(lambda b: b, [(ones2, sq2[:, i, :])])} for i in range(2)],
                             act_extra=sub_act, dve_extra=sub_dve)

                    sp = region(extra, 2, 1280)
                    wt = region(base.at + 4 * D, 2, 1280)
                    odd_c = region(base.at + 4 * D + 2560, 3, T)
                    qz_c = lambda h: qk[:, 10 + h // 2, :] if h % 2 == 0 else odd_c[:, h // 2, :]

                    def pad_c_pool(l):
                        l.did(G.memset(odd_c[0:64], 0.0).then_inc(l.sem, 1))
                        l.wait_ge(*past(nm, "odd_c"))
                        l.did(G.memset(qk[64:128, 10:13, :], 0.0).then_inc(l.sem, 1))

                    def pad_c_dve(l):
                        l.did(V.tensor_copy(odd_c[64:128], qk[64:128, 10:13, :]).then_inc(l.sem, 1), nm, "odd_c")
                    stage(nm + "padc", pool=pad_c_pool, dve=pad_c_dve)
                    nb = nm + "stick"
                    where = {0: (0, 0, 0), 1: (1, 0, 512), 3: (1, 384, 896), 2: (2, 0, 1024)}
                    full3 = lambda b0: [(banks[:, b0, :], 0), (banks[:, b0 + 1, :], 512), (banks[:, b0 + 2, 0:256], 1024)]

                    def st_pe(l):
                        def zs(i, b0, start_only):
                            for s_ in (0, 1, 3, 2):
                                b, c, _ = where[s_]
                                n = T - s_ * P
                                ins = TE.matmul(banks[:, b0 + b, c:c + n], qk[:, 13 + i // 2, s_ * P:(s_ + 1) * P],
                                                qz_c(i)[:, s_ * P:T], start=True, stop=start_only)
                                if not start_only:
                                    for j in range(s_, NT):
                                        m_ = T - j * P
                                        oj = where[j][2]
                                        ins = TE.matmul(banks[:, b0 + b, c + (j - s_) * P:c + n], sbk[:, 0 if j == s_ else 1, :],
                                                        sp[:, i % 2, oj:oj + m_], start=False, stop=(j == NT - 1))
                            return ins
                        for i in range(6 + 2):
                            if i < 6:
                                if i:
                                    l.wait_ge(*past(nb, "sp", i - 1))
                                l.did(zs(i, 0, True).then_inc(l.sem, 1), nb, "z", i)
                            if 1 <= i <= 6:
                                h = i - 1
                                l.wait_ge(*past(nb, "sp", h))
                                if h:
                                    l.wait_ge(*past(nb, "clamped", h - 1))
                                l.did(zs(h, 3, False).then_inc(l.sem, 1), nb, "zc", h)
                            if i >= 2:
                                h = i - 2
                                po = half(h)
                                l.wait_ge(*past(nb, "w", h))
                                if h >= 2:
                                    l.wait_ge(*past(nb, "o", h - 2))
                                for j in range(NT):
                                    oj = where[j][2]
                                    ins = TE.matmul(banks[po:po + HD, 6 + h % 2, j * P:T], vt[:, j, 640 + h * HD:640 + (h + 1) * HD],
                                                    wt[:, h % 2, oj:oj + T - j * P], start=(j == 0), stop=(j == NT - 1))
                                l.did(ins.then_inc(l.sem, 1), nb, "pv", h)

                    def st_act(l):
                        for i in range(7):
                            if i < 6:
                                l.wait_ge(*past(nb, "z", i))
                                if i >= 2:
                                    l.wait_ge(*past(nb, "zc", i - 2))
                                for b, o in full3(0):
                                    n = b.shape[1]
                                    l.did(S.activation(sp[:, i % 2, o:o + n], b, ACT.Abs).then_inc(l.sem, 1))
                                l.wait_ge(*l.own())
                                l.did(S.activation(sp[:, i % 2, :], sp[:, i % 2, :], ACT.Exp, scale=-1.0).then_inc(l.sem, 1))
                                l.wait_ge(*l.own())
                                l.did(S.activation(sp[:, i % 2, :], sp[:, i % 2, :], ACT.Ln, bias=1.0).then_inc(l.sem, 1), nb, "ln", i)
                            if i >= 1:
                                h = i - 1
                                l.wait_ge(*past(nb, "clamped", h))
                                l.did(S.activation(wt[:, h % 2, :], wt[:, h % 2, :], ACT.Exp).then_inc(l.sem, 1), nb, "exp", h)
                                if h:
                                    l.wait_ge(*past(nb, "pv", h - 1))
                                    out_copy(l, h - 1)
                        l.wait_ge(*past(nb, "pv", 5))
                        out_copy(l, 5)

                    def out_copy(l, h):
                        po = half(h)
                        l.did(S.activation(mixT[po:po + HD, 5 + h // 2, :], banks[po:po + HD, 6 + h % 2, :], ACT.Copy).then_inc(l.sem, 1), nb, "o", h)

                    def st_dve(l):
                        def mask(buf):
                            for s_ in range(NT):
                                o = where[s_][2]
                                l.did(V.tensor_tensor(buf[:, o:o + P], buf[:, o:o + P], sbk[:, 2, :], ALU.mult).then_inc(l.sem, 1))
                        for i in range(7):
                            if i < 6:
                                l.wait_ge(*past(nb, "ln", i))
                                for b, o in full3(0):
                                    n = b.shape[1]
                                    l.did(V.scalar_tensor_tensor(out=sp[:, i % 2, o:o + n], in0=b, scalar=0.0, in1=sp[:, i % 2, o:o + n],
                                                                 op0=ALU.max, op1=ALU.add).then_inc(l.sem, 1))
                                l.wait_ge(*l.own())
                                mask(sp[:, i % 2, :])
                                l.name_last(nb, "sp", i)
                            if i >= 1:
                                h = i - 1
                                l.wait_ge(*past(nb, "zc", h))
                                if h >= 2:
                                    l.wait_ge(*past(nb, "pv", h - 2))
                                for b, o in full3(3):
                                    n = b.shape[1]
                                    l.did(V.tensor_scalar(wt[:, h % 2, o:o + n], b, 0.0, None, ALU.min).then_inc(l.sem, 1))
                                l.name_last(nb, "clamped", h)
                                l.wait_ge(*past(nb, "exp", h))
                                mask(wt[:, h % 2, :])
                                l.name_last(nb, "w", h)
                    stage(nb, pe=st_pe, act=st_act, dve=st_dve)

                    wo_src = a["w_out_2"][l_].rearrange("(k p) n -> p k n", p=P)
                    wos = [stream(wo_src[:, 4 * s_:4 * s_ + 4, :], (4, D)) for s_ in range(2)]
                    gain_rows(nm + "g", (l_, 3), (l_, 4), nm + "stick")
                    mix_hi, mix_lo = h_r(hT_at, KD, T), mix_r(mixT_at, KD, T)
                    on = nm + "out"
                    w_units, m_units = [], []
                    for u in range(KD // 2):
                        n = wos[u // 2][0]
                        at_ = (n[0] % RING) * SLOT + (u % 2) * 2 * D
                        w_units.append((region(at_, 2, D), ring_r(at_, 2, D), ffn_r(ytmp_at + u * 2 * D, 2, D), n))
                        ks = slice(2 * u, 2 * u + 2)
                        m_units.append((mixT[:, ks, :], mix_lo[:, ks, :], mix_hi[:, ks, :], None))

                    def split_out(l):
                        for u in range(KD // 2):
                            split(l, on + "m", u, m_units[u], KD)
                            split(l, on, u, w_units[u], KD)

                    def out_pe(l):
                        for u, (_, w_lo, w_hi, n) in enumerate(w_units):
                            l.wait_ge(*past(on, "lo", u))
                            for k in (2 * u, 2 * u + 1):
                                for t in range(NT):
                                    ts = slice(t * P, (t + 1) * P)
                                    for hf in range(2):
                                        ns = slice(hf * 512, (hf + 1) * 512)
                                        bank = banks[:, 2 * t + hf, :]
                                        TE.matmul(bank, mix_hi[:, k, ts], w_hi[:, k % 2, ns], start=(k == 0), stop=False)
                                        TE.matmul(bank, mix_hi[:, k, ts], w_lo[:, k % 2, ns], start=False, stop=False)
                                        ins = TE.matmul(bank, mix_lo[:, k, ts], w_hi[:, k % 2, ns], start=False, stop=(k == KD - 1))
                            l.did(ins.then_inc(l.sem, 1), on, "used", u)
                            if u % 2:
                                l.name_last("freed", n[0])
                    stage(on, pe=out_pe, act=split_out, dve=split_out)

                gain_rows("open", None, (0, 0), "scatter")
                between("open", None, "open")
                for l_ in range(2):
                    ffn(l_, 0)
                    between(f"mid{l_}a", 0.5, f"ffn{l_}0g")
                    mixer(l_)
                    between(f"mid{l_}b", 1.0, f"mix{l_}g")
                    ffn(l_, 1)
                    between(f"mid{l_}c", 0.5, f"ffn{l_}1g", last=(l_ == 1))
                views["final_x"] = x


            part_two()
            part_three()
            part_four()
            part_five()
            if me.name == "sp":
                for e in ("pe", "act", "dve", "pool"):
                    me.wait_ge(*past("end", stages[-1], e))
                me.engine.dma_start(out[0].rearrange("(t p) n -> p t n", p=P), views["final_x"]).then_inc(stored, 16)
                me.wait_ge(stored, 16)

        block = ctx.enter_context(nc.Block())

        @block.sync
        def _(eng):
            program(lanes["sp"])

        @block.tensor
        def _(eng):
            program(pe)

        @block.scalar
        def _(eng):
            program(act)

        @block.vector
        def _(eng):
            program(dve)

        @block.gpsimd
        def _(eng):
            program(pool)
    return marks.now


_INS = ['x', 'c', 'ctx', 'c_ctx', 'w_ada', 'b_ada', 'w_in', 'q_gain', 'k_gain', 'tshift_mu', 'decay_w0',
        'decay_up', 'iclr_a0', 'iclr_up', 'gate_up', 'k_k', 'k_a', 'r_k', 'lnx_g', 'lnx_b', 'w_out', 'ln1_g',
        'ln1_b', 'router_w', 'exp_w_gate', 'exp_w_up', 'exp_w_down', 'ln2_g', 'ln2_b', 'norm_gains_2',
        'w_ffn_gate_2', 'w_ffn_up_2', 'w_ffn_down_2', 'w_in_2', 'w_out_2', 'diff_lambda_2',
        'diff_subln_gain_2']


def kernel(**inputs):
    import numpy as _np
    import concourse.bacc as _bacc
    from concourse.bass_utils import run_bass_kernel_spmd as _run

    known = {}
    for final in (False, True):
        nc = _bacc.Bacc("TRN2", target_bir_lowering=False, num_devices=1)
        arrays, args = {}, {}
        for name in _INS:
            arr = _np.ascontiguousarray(inputs[name])
            arrays[f"in_{name}"] = arr
            args[name] = nc.dram_tensor(f"in_{name}", arr.shape, F32, kind="ExternalInput").ap()
        for name, arr in constants().items():
            arrays[name] = arr
            args[name] = nc.dram_tensor(name, arr.shape, F32, kind="ExternalInput").ap()
        out = nc.dram_tensor("out", (1, T, D), F32, kind="ExternalOutput").ap()
        known = build(nc, args, out, known, final)
    r = _run(nc, [arrays], core_ids=[0])
    return r.results[0]["out"]
```
